# Optimizing a Trainium2 kernel written in Bass

```python
import jax, jax.numpy as jnp
from jax import lax
import numpy as np

D_MODEL = 1024
BATCH = 1
SEQ = 512
DEPTH = 1
DEC_BATCH = 8
DEC_SEQ = 1
PAST_LEN = 4096
PAGE_SIZE = 128

D_A = D_MODEL
D_B = D_MODEL
D_C = D_MODEL
K_A = 3
K_B = 31
CHUNK = 128
C_GROUPS = 8
C_HEAD = D_C // C_GROUPS
N_BRANCH = 3
SPLIT_WIDTHS = (D_A, D_A, D_A, D_B, D_B, D_C, D_C, N_BRANCH * D_MODEL)
D_IN_TOTAL = 3 * D_A + 2 * D_B + 2 * D_C + N_BRANCH * D_MODEL
N_EXPERTS = 16
N_EXPERT_GROUPS = 4
EXPERTS_PER_GROUP = N_EXPERTS // N_EXPERT_GROUPS
TOP_K = 2
D_EXPERT = D_MODEL // 2
ALPHA = (2 * DEPTH) ** 0.25
BETA = (8 * DEPTH) ** -0.25
LN_EPS = 1e-5

kernel_name = 'parallel_conv_chunkmlp_moe_decode_step'

def layer_norm(x, g, b):
    xf = x.astype(jnp.float32)
    mu = jnp.mean(xf, axis=-1, keepdims=True)
    xc = xf - mu
    var = jnp.mean(xc * xc, axis=-1, keepdims=True)
    return (xc * lax.rsqrt(var + LN_EPS) * g.astype(jnp.float32) + b.astype(jnp.float32)).astype(x.dtype)

def causal_dwconv(x_full, w):
    c = x_full.shape[-1]
    return lax.conv_general_dilated(x_full, w[:, None, :].astype(x_full.dtype), window_strides=(1,), padding='VALID',
                                    dimension_numbers=('NWC', 'WIO', 'NWC'), feature_group_count=c)

def chunk_spatial_gate(v, w_s, b_s):
    n, L, _ = v.shape
    ch = min(L, CHUNK)
    nc = -(-L // ch)
    lp = nc * ch
    if lp != L:
        v = jnp.pad(v, ((0, 0), (0, lp - L), (0, 0)))
    causal = jnp.tril(jnp.ones((ch, ch), dtype=bool))
    w = jnp.where(causal[None], w_s[:, :ch, :ch], 0).astype(v.dtype)
    vc = v.reshape(n, nc, ch, C_GROUPS, C_HEAD)
    s = jnp.einsum('gts,bcsgd->bctgd', w, vc) + jnp.swapaxes(b_s[:, :ch], 0, 1)[None, None, :, :, None].astype(v.dtype)
    return s.reshape(n, lp, D_C)[:, :L]

def token_mixer(x, ctx_a, ctx_b, w_in, conv_a_w, w_a_out, conv_b_w, conv_b_bias, norm_b_g, norm_b_b, w_b_out,
                v_norm_g, v_norm_b, w_spatial, b_spatial, w_c_out, w_o):
    z = jnp.einsum('bld,de->ble', x, w_in)
    a_bg, a_cg, a_h, b_val, b_gate, c_u, c_v, gate_pre = jnp.split(z, list(np.cumsum(SPLIT_WIDTHS)[:-1]), axis=-1)
    a_full = jnp.concatenate([ctx_a, a_cg * a_h], axis=1)
    y_a = jnp.einsum('blc,cd->bld', a_bg * causal_dwconv(a_full, conv_a_w), w_a_out)
    b_full = jnp.concatenate([ctx_b, b_val * jax.nn.sigmoid(b_gate)], axis=1)
    b_conv = causal_dwconv(b_full, conv_b_w) + conv_b_bias
    y_b = jnp.einsum('blc,cd->bld', jax.nn.silu(layer_norm(b_conv, norm_b_g, norm_b_b)), w_b_out)
    v = layer_norm(c_v, v_norm_g, v_norm_b)
    y_c = jnp.einsum('blc,cd->bld', c_u * chunk_spatial_gate(v, w_spatial, b_spatial), w_c_out)
    g_a, g_b, g_c = jnp.split(jax.nn.sigmoid(gate_pre), N_BRANCH, axis=-1)
    merged = g_a * y_a + g_b * y_b + g_c * y_c
    out = jnp.einsum('bld,de->ble', merged, w_o)
    return out, a_full[:, -(K_A - 1):], b_full[:, -(K_B - 1):], v

def moe_ffn(h, router_w, router_b, w_gate, w_up, w_down):
    n, L, d = h.shape
    t = h.reshape(n * L, d)
    logits = jnp.dot(t.astype(jnp.float32), router_w.astype(jnp.float32)) + router_b.astype(jnp.float32)
    probs = jax.nn.softmax(logits, axis=-1)
    grouped = probs.reshape(-1, N_EXPERT_GROUPS, EXPERTS_PER_GROUP)
    top_v, top_i = lax.top_k(grouped, TOP_K)
    best = jnp.argmax(jnp.sum(top_v, axis=-1), axis=-1)
    sel_v = jnp.take_along_axis(top_v, best[:, None, None], axis=1)[:, 0]
    sel_i = jnp.take_along_axis(top_i, best[:, None, None], axis=1)[:, 0] + best[:, None] * EXPERTS_PER_GROUP
    weights = sel_v / jnp.sum(sel_v, axis=-1, keepdims=True)
    gates = jnp.sum(jax.nn.one_hot(sel_i, N_EXPERTS, dtype=jnp.float32) * weights[..., None], axis=1).astype(h.dtype)
    out = jnp.zeros_like(t)
    for e in range(N_EXPERTS):
        u = jax.nn.silu(t @ w_gate[e]) * (t @ w_up[e])
        out = out + gates[:, e:e + 1] * (u @ w_down[e])
    return out.reshape(n, L, d)

def decoder_layer(x, ctx_a, ctx_b, w_in, conv_a_w, w_a_out, conv_b_w, conv_b_bias, norm_b_g, norm_b_b, w_b_out,
                  v_norm_g, v_norm_b, w_spatial, b_spatial, w_c_out, w_o, ln1_g, ln1_b, router_w, router_b,
                  expert_w_gate, expert_w_up, expert_w_down, ln2_g, ln2_b):
    m, new_a, new_b, v = token_mixer(x, ctx_a, ctx_b, w_in, conv_a_w, w_a_out, conv_b_w, conv_b_bias, norm_b_g,
                                     norm_b_b, w_b_out, v_norm_g, v_norm_b, w_spatial, b_spatial, w_c_out, w_o)
    h = layer_norm(ALPHA * x + m, ln1_g, ln1_b)
    f = moe_ffn(h, router_w, router_b, expert_w_gate, expert_w_up, expert_w_down)
    y = layer_norm(ALPHA * h + f, ln2_g, ln2_b)
    return y, new_a, new_b, v

def setup_inputs(seed: int = 0) -> dict:
    key = jax.random.key(seed)
    ks = iter(jax.random.split(key, 40))
    f32 = jnp.float32

    def nrm(shape, scale):
        return jax.random.normal(next(ks), shape, f32) * scale

    return {
        'x_prompt': nrm((BATCH, SEQ, D_MODEL), 1.0),
        'x_sample': nrm((DEC_BATCH, DEC_SEQ, D_MODEL), 1.0),
        'state_conv_a': nrm((DEPTH, DEC_BATCH, K_A - 1, D_A), 1.0),
        'state_conv_b': nrm((DEPTH, DEC_BATCH, K_B - 1, D_B), 1.0),
        'w_in': nrm((DEPTH, D_MODEL, D_IN_TOTAL), D_MODEL ** -0.5),
        'conv_a_w': nrm((DEPTH, K_A, D_A), K_A ** -0.5),
        'w_a_out': nrm((DEPTH, D_A, D_MODEL), BETA * D_A ** -0.5),
        'conv_b_w': nrm((DEPTH, K_B, D_B), K_B ** -0.5),
        'conv_b_bias': nrm((DEPTH, D_B), 0.02),
        'norm_b_g': 1.0 + nrm((DEPTH, D_B), 0.1),
        'norm_b_b': nrm((DEPTH, D_B), 0.02),
        'w_b_out': nrm((DEPTH, D_B, D_MODEL), BETA * D_B ** -0.5),
        'v_norm_g': 1.0 + nrm((DEPTH, D_C), 0.1),
        'v_norm_b': nrm((DEPTH, D_C), 0.02),
        'w_spatial': nrm((DEPTH, C_GROUPS, CHUNK, CHUNK), CHUNK ** -0.5),
        'b_spatial': 1.0 + nrm((DEPTH, C_GROUPS, CHUNK), 0.1),
        'w_c_out': nrm((DEPTH, D_C, D_MODEL), BETA * D_C ** -0.5),
        'w_o': nrm((DEPTH, D_MODEL, D_MODEL), BETA * D_MODEL ** -0.5),
        'ln1_g': 1.0 + nrm((DEPTH, D_MODEL), 0.1),
        'ln1_b': nrm((DEPTH, D_MODEL), 0.02),
        'router_w': nrm((D_MODEL, N_EXPERTS), D_MODEL ** -0.5),
        'router_b': nrm((N_EXPERTS,), 0.01),
        'expert_w_gate': nrm((DEPTH, N_EXPERTS, D_MODEL, D_EXPERT), D_MODEL ** -0.5),
        'expert_w_up': nrm((DEPTH, N_EXPERTS, D_MODEL, D_EXPERT), D_MODEL ** -0.5),
        'expert_w_down': nrm((DEPTH, N_EXPERTS, D_EXPERT, D_MODEL), BETA * D_EXPERT ** -0.5),
        'ln2_g': 1.0 + nrm((DEPTH, D_MODEL), 0.1),
        'ln2_b': nrm((DEPTH, D_MODEL), 0.02),
    }

def reference(x_prompt, x_sample, state_conv_a, state_conv_b, w_in, conv_a_w, w_a_out, conv_b_w, conv_b_bias,
              norm_b_g, norm_b_b, w_b_out, v_norm_g, v_norm_b, w_spatial, b_spatial, w_c_out, w_o, ln1_g, ln1_b,
              router_w, router_b, expert_w_gate, expert_w_up, expert_w_down, ln2_g, ln2_b):
    xp, xs = x_prompt, x_sample
    pa, pb, sa, sb, sv = [], [], [], [], []
    zero_a = jnp.zeros((xp.shape[0], K_A - 1, D_A), xp.dtype)
    zero_b = jnp.zeros((xp.shape[0], K_B - 1, D_B), xp.dtype)
    for l in range(DEPTH):
        lp = dict(w_in=w_in[l], conv_a_w=conv_a_w[l], w_a_out=w_a_out[l], conv_b_w=conv_b_w[l],
                  conv_b_bias=conv_b_bias[l], norm_b_g=norm_b_g[l], norm_b_b=norm_b_b[l], w_b_out=w_b_out[l],
                  v_norm_g=v_norm_g[l], v_norm_b=v_norm_b[l], w_spatial=w_spatial[l], b_spatial=b_spatial[l],
                  w_c_out=w_c_out[l], w_o=w_o[l], ln1_g=ln1_g[l], ln1_b=ln1_b[l], router_w=router_w,
                  router_b=router_b, expert_w_gate=expert_w_gate[l], expert_w_up=expert_w_up[l],
                  expert_w_down=expert_w_down[l], ln2_g=ln2_g[l], ln2_b=ln2_b[l])
        xp, na, nb, _ = decoder_layer(xp, zero_a, zero_b, **lp)
        pa.append(na)
        pb.append(nb)
        xs, na, nb, v = decoder_layer(xs, state_conv_a[l], state_conv_b[l], **lp)
        sa.append(na)
        sb.append(nb)
        sv.append(v)
    return (xp, xs, jnp.stack(pa), jnp.stack(pb), jnp.stack(sa), jnp.stack(sb), jnp.stack(sv))


_drawn_inputs = setup_inputs


def setup_inputs(seed=0):
    import zlib

    import numpy as np

    out = dict(_drawn_inputs(seed))
    spreads = {}
    factors = {'norm_b_b': 8.0, 'v_norm_b': 2.778, 'ln2_b': 2.816, 'conv_b_bias': 3.829}
    for name, (base, spread) in spreads.items():
        noise = np.random.default_rng([zlib.crc32(name.encode()), seed]).standard_normal(out[name].shape)
        drawn = base * np.exp(spread * noise) if base else spread * noise
        out[name] = __import__('jax').numpy.asarray(drawn.astype(out[name].dtype))
    for name, factor in factors.items():
        out[name] = (out[name] * factor).astype(out[name].dtype)
    return out
```

```python
from contextlib import ExitStack

import concourse.bass as bass
from concourse import mybir

F32 = mybir.dt.float32
F32R = mybir.dt.float32r
BF16 = mybir.dt.bfloat16
I32 = mybir.dt.int32
ALU = mybir.AluOpType
ACT = mybir.ActivationFunctionType
AX = mybir.AxisListType

P = 128
D = 1024
KB = D // P
TP, TS = 512, 8
T = TP + TS
HALF = T // 2
NTB = 5
KA, KC = 3, 31
E, EF = 16, 512
FB = EF // P
GROUPS, PER_GROUP = 4, 4
PASSES = 5
ALPHA = 2.0 ** 0.25
EPS = 1e-5

A_BG, A_CG, A_H, B_VAL, B_GATE, C_U, C_V, G_A, G_B, G_C = (D * i for i in range(10))

R_CONVB, R_CONVA, R_BIAS, R_NBG, R_NBB, R_VG, R_VB, R_L1G, R_L1B, R_STA = 0, 31, 34, 35, 36, 37, 38, 39, 40, 41
NROWS = R_STA + 2 * TS

N_S1 = 0
N_GA = N_S1 + 6 * KB
N_U = N_GA + 2 * KB
N_GC = N_U + KB
N_GB = N_GC + 2 * KB
N_WO = N_GB + 2 * KB
N_END = N_WO + KB

ROUNDS = [("rows", 1), ("xs", 0), ("sb0", 1), ("sb1", 0), ("ws0", 1), ("ws1", 0),
          ("meanV", 0), ("varV", 0), ("meanB", 1), ("varB", 0),
          ("vt0", 1), ("vt1", 0), ("vt2", 1), ("vt3", 0), ("tailB", 1), ("tailA", 0), ("tailV", 1),
          ("sp0", 0), ("sp1", 1), ("sp2", 0), ("sp3", 1),
          ("meanH", 0), ("varH", 0), ("logits", 1), ("ht0", 0), ("ht1", 1), ("ht2", 0), ("ht3", 1), ("ht4", 0),
          ("pos", 1)]
DONE = {name: i + 1 for i, (name, _) in enumerate(ROUNDS)}
TILE = dict(ROUNDS)
BEFORE = {name: next((n for n, t in reversed(ROUNDS[:i]) if t == tile), None) for i, (name, tile) in enumerate(ROUNDS)}


class Tally:

    def __init__(self, eng, sem, start=0):
        self.eng, self.sem, self.base, self.n, self.var = eng, sem, start, 0, None

    def inc(self, ins):
        ins.then_inc(self.sem, 1)
        self.n += 1

    def value(self, lag=0):
        now = self.base + self.n - lag
        return now if self.var is None else self.var + now

    def wait(self, lag=0):
        self.eng.wait_ge(self.sem, self.value(lag))

    def enter(self, i, per):
        self.outer, self.per, self.var, self.n0 = self.n, per, i * per, self.n

    def leave(self, count):
        assert self.n - self.n0 == self.per, (self.n - self.n0, self.per)
        self.var, self.n = None, self.n0 + self.per * count


def rep(ap, axis, n):
    v = ap.unsqueeze(axis)
    shape = list(v.shape)
    shape[axis] = n
    return v.to_broadcast(shape)


def build(nc, x_prompt, x_sample, state_conv_a, state_conv_b, w_in, conv_a_w, w_a_out, conv_b_w, conv_b_bias,
          norm_b_g, norm_b_b, w_b_out, v_norm_g, v_norm_b, w_spatial, b_spatial, w_c_out, w_o, ln1_g, ln1_b,
          router_w, router_b, expert_w_gate, expert_w_up, expert_w_down, ln2_g, ln2_b,
          y_prompt, y_sample, new_a_prompt, new_b_prompt, new_a_sample, new_b_sample, new_v_sample):
    h_rows = nc.dram_tensor("h_rows", (T, D), F32, kind="Internal").ap()
    y_rows = nc.dram_tensor("y_rows", (PASSES * E * P, D), F32, kind="Internal").ap()

    in_v = w_in[0].rearrange("(k p) n -> p k n", p=P)
    a_out_v = w_a_out[0].rearrange("(k p) n -> p k n", p=P)
    b_out_v = w_b_out[0].rearrange("(k p) n -> p k n", p=P)
    c_out_v = w_c_out[0].rearrange("(k p) n -> p k n", p=P)
    o_v = w_o[0].rearrange("(k p) n -> p k n", p=P)
    gate_v = expert_w_gate[0].rearrange("e (k p) f -> p (e k) f", p=P)
    up_v = expert_w_up[0].rearrange("e (k p) f -> p (e k) f", p=P)
    down_v = expert_w_down[0].rearrange("e (k p) n -> p (e k) n", p=P)

    with ExitStack() as ctx:
        U = KB * T * 4
        base = (nc.sbuf_base + 31) // 32 * 32
        at = {}
        cursor = [base]

        def region(name, size):
            at[name] = cursor[0]
            cursor[0] += (size + 31) // 32 * 32

        for name in ("P_HI", "P_LO", "CB", "Q_HI", "Q_LO", "X_HI", "X_LO", "V", "M"):
            region(name, U)
        region("RING", 6 * D * 4)

        def place(name, where, shape, dt=F32, plus=0):
            return nc.alloc_sbuf_tensor_at(name, shape, dt, offset=at[where] + plus)

        def sb(name, shape, dt=F32):
            size = 1
            for n in shape[1:]:
                size *= n
            region(name, size * (2 if dt == BF16 else 4))
            return place(name, name, shape, dt)

        def sem(name):
            return ctx.enter_context(nc.semaphore(name))

        p_hi, p_lo = place("p_hi", "P_HI", [P, KB, T], F32R), place("p_lo", "P_LO", [P, KB, T], F32R)
        q_hi, q_lo = place("q_hi", "Q_HI", [P, KB, T], F32R), place("q_lo", "Q_LO", [P, KB, T], F32R)
        x_hi, x_lo = place("x_hi", "X_HI", [P, KB, T], F32R), place("x_lo", "X_LO", [P, KB, T], F32R)
        cb = place("cb", "CB", [P, KB, T])
        v = place("v", "V", [P, KB, T])
        m = place("m", "M", [P, KB, T])
        sig_b = place("sig_b", "V", [P, KB, T])
        vt = place("vt", "Q_HI", [P, 4, D])
        sq = place("sq", "Q_LO", [P, KB, T])
        sq_h = place("sq_h", "V", [P, KB, T])
        tails = place("tails", "Q_LO", [38, 3, D])
        raw = place("raw", "RING", [P, 2, KB, P])
        w_hi = place("w_hi", "RING", [P, 2, KB, P], F32R, plus=2 * D * 4)
        w_lo = place("w_lo", "RING", [P, 2, KB, P], F32R, plus=4 * D * 4)
        x_tok = place("x_tok", "V", [P, 4, D])
        rows = place("rows", "M", [NROWS, D])
        xs_tok = place("xs_tok", "M", [TS, D], plus=D * 4)
        sb_tok = place("sb_tok", "M", [120, 2, D], plus=2 * D * 4)
        ws_nat = place("ws_nat", "CB", [P, KB, P])
        sb_t = place("sb_t", "Q_LO", [P, KB, TS, KC - 1])
        w_gate = [place("w_gate0", "P_HI", [P, KB, EF]), place("w_gate1", "Q_HI", [P, KB, EF])]
        w_up = [place("w_up0", "P_HI", [P, KB, EF], plus=16384), place("w_up1", "Q_HI", [P, KB, EF], plus=16384)]
        w_down = [place("w_down0", "P_HI", [P, FB, D], plus=32768), place("w_down1", "Q_HI", [P, FB, D], plus=32768)]
        h_tok = place("h_tok", "X_LO", [P, NTB, D])
        hs = place("hs", "X_LO", [P, 2, D], plus=NTB * D * 4)
        hs_t = place("hs_t", "M", [P, 2, KB, P])
        silu = place("silu", "M", [P, 2, FB, P], plus=2 * D * 4)
        u_t = place("u_t", "M", [P, 2, FB, P], plus=3 * D * 4)
        y_out = place("y_out", "RING", [P, 2, D])
        ln2_rows = place("ln2_rows", "RING", [P, 2, D], plus=2 * D * 4)
        onehot = place("onehot", "RING", [P, 2, NTB, P], BF16, plus=4 * D * 4)
        y_a = place("y_a", "P_HI", [P, 2, D])
        y_b = place("y_b", "P_HI", [P, 2, D], plus=2 * D * 4)
        fin = place("fin", "P_HI", [P, 2, D], plus=4 * D * 4)

        ev = [sb(f"ev{i}", [P, T]) for i in range(5)]
        b_pad = sb("b_pad", [P, KC - 1 + T])
        a_pad = sb("a_pad", [P, KA - 1 + T])
        acc_b = sb("acc_b", [P, TP])
        acc_a = sb("acc_a", [P, T])
        par = sb("par", [P, KB * NROWS])
        bs = sb("bs", [P, KB, P])
        w00 = sb("w00", [P, KB])
        ws_t = sb("ws_t", [P, KB, P])
        ident = sb("ident", [P, P])
        mean_w = sb("mean_w", [P, P])
        tail_b = sb("tail_b", [P, KB, 38])
        tail_a = sb("tail_a", [P, KB, 10])
        samp_b = sb("samp_b", [P, KB, TS])
        samp_a = sb("samp_a", [P, KB, TS])
        samp_t = sb("samp_t", [P, KB, TS])
        std = sb("std", [P, T])
        eps_t = sb("eps_t", [P, 1])
        rw = sb("rw", [P, KB, E])
        rb = sb("rb", [P, E])
        tri = sb("tri", [P, P], BF16)
        ones_b = sb("ones_b", [P, P], BF16)
        id_cols = sb("id_cols", [P, NTB, 2], BF16)
        probs, oh1, oh2, t1, t2, posm = (place(f"router{i}", "b_pad", [P, NTB, E], plus=i * NTB * E * 4) for i in range(6))
        e_off, c4 = sb("e_off", [P, NTB, E]), sb("c4", [P, NTB, E])
        mb = sb("mb", [P, NTB, E], BF16)
        g_m1, g_m2, g_t, g_best = (sb(f"g{i}", [P, NTB, GROUPS]) for i in range(4))
        s_max, s_sum, s_w1, s_w2, s_ps, s_t, s_slot = (sb(f"s{i}", [P, NTB]) for i in range(7))
        slot_a, slot_b = sb("slot_a", [P, NTB], I32), sb("slot_b", [P, NTB], I32)
        ids = sb("ids", [P, E], I32)
        count_i = sb("count_i", [P, 1], I32)
        iota = ev[0][:, 0:P]
        stats = sb("stats", [P, 2, 2, 6])
        agg = sb("agg", [P, 2, 4])
        assert cursor[0] <= nc.sbuf_usable_end - 64, (cursor[0], nc.sbuf_usable_end)

        pr = [ctx.enter_context(nc.psum_tensor(f"pr{i}", [P, 2, 512], F32)) for i in range(2)]
        work = [ctx.enter_context(nc.psum_tensor(f"work{i}", [P, 2, 512], F32)) for i in range(2)]

        x_in, rows_in, states_in, spatial_in, late_in = (sem(n) for n in ("x_in", "rows_in", "states_in", "spatial_in", "late_in"))
        const_ready, spatial_masked, pool_chain = sem("const_ready"), sem("spatial_masked"), sem("pool_chain")
        x_turned, x_rounded, x_split = sem("x_turned"), sem("x_rounded"), sem("x_split")
        raw_in = [sem("raw_in0"), sem("raw_in1")]
        w_rounded = sem("w_rounded")
        w_split = sem("w_split")
        proj_done = sem("proj_done")
        evacuated = sem("evacuated")
        gated = sem("gated")
        round_done = sem("round_done")
        dve_chain = sem("dve_chain")
        setup_done = sem("setup_done")
        sq_ready = sem("sq_ready")
        centred = sem("centred")
        std_ready = sem("std_ready")
        std_used = sem("std_used")
        v_ready = sem("v_ready")
        tails_ready = sem("tails_ready")
        tails_out = sem("tails_out")
        vt_ready = sem("vt_ready")
        tail_cols = sem("tail_cols")
        a_split, b_split, c_split, merged_split = sem("a_split"), sem("b_split"), sem("c_split"), sem("merged_split")
        conv_done = sem("conv_done")
        b_normed, b_sig = sem("b_normed"), sem("b_sig")
        spatial_read = sem("spatial_read")
        pos_read = sem("pos_read")
        h_pre = sem("h_pre")
        h_ready = sem("h_ready")
        h_tok_ready = sem("h_tok_ready")
        h_stored = sem("h_stored")
        logits_ready, exp_ready = sem("logits_ready"), sem("exp_ready")
        mb_ready = sem("mb_ready")
        count_ready = sem("count_ready")
        states_out = sem("states_out")
        slots_ready = sem("slots_ready")
        loads_begun, gathers_begun = sem("loads_begun"), sem("gathers_begun")
        more_posm = sem("more_posm")
        y_in = [sem("y_in0"), sem("y_in1")]
        y_read = sem("y_read")
        var_ready, std2_ready, scale_ready, normed, fin_ready, fin_g = (sem(n) for n in ("var_ready", "std2_ready", "scale_ready", "normed", "fin_ready", "fin_g"))
        fin_out = [sem("fin_out0"), sem("fin_out1")]

        class Pass:

            def __init__(self, tag):
                self.onehot_ready, self.ids_mm, self.ids_ready = sem(tag + "onehot"), sem(tag + "ids_mm"), sem(tag + "ids_ready")
                self.gathered = [sem(tag + "gathered0"), sem(tag + "gathered1")]
                self.turned, self.hs_t_ready = sem(tag + "turned"), sem(tag + "hs_t")
                self.gate_in = [sem(tag + "gate_in0"), sem(tag + "gate_in1")]
                self.up_in = [sem(tag + "up_in0"), sem(tag + "up_in1")]
                self.down_in = [sem(tag + "down_in0"), sem(tag + "down_in1")]
                self.gate_done, self.up_done, self.down_done = sem(tag + "gate_done"), sem(tag + "up_done"), sem(tag + "down_done")
                self.silu_ready, self.u_ready, self.y_ready = sem(tag + "silu"), sem(tag + "u"), sem(tag + "y_ready")
                self.stored = [sem(tag + "stored0"), sem(tag + "stored1")]

        first, further = Pass("first_"), Pass("more_")

        block = ctx.enter_context(nc.Block())

        READ = {"rows": (setup_done, 1), "xs": (x_split, KB + 1), "sb0": (setup_done, 2), "sb1": (setup_done, 3),
                "ws0": (setup_done, 4), "ws1": (setup_done, 5), "meanV": (centred, 1), "varV": (std_ready, 1),
                "meanB": (centred, 2), "varB": (std_ready, 2), "meanH": (centred, 3), "varH": (std_ready, 3),
                "tailB": (tails_ready, 1), "tailA": (tails_ready, 2), "tailV": (tails_ready, 3), "logits": (logits_ready, 1)}
        READ.update({f"vt{c}": (vt_ready, c + 1) for c in range(4)})
        READ.update({f"sp{q}": (spatial_read, q + 1) for q in range(4)})
        READ.update({f"ht{b}": (h_tok_ready, b + 1) for b in range(NTB)})

        def work_wait(eng, name):
            if BEFORE[name]:
                eng.wait_ge(*READ[BEFORE[name]])

        def further_passes(eng):
            eng.wait_ge(count_ready, 1)
            return eng.value_load(count_i[0:1, 0:1], min_val=0, max_val=T)

        @block.sync
        def _(sp):
            sp.dma_start(x_tok[:], x_prompt[0].rearrange("(b p) n -> p b n", p=P)).then_inc(x_in, 16)
            sp.dma_start(xs_tok[:], x_sample[:, 0, :]).then_inc(x_in, 16)

            def load(slot, n, view, col):
                sp.wait_ge(w_split, n + 1)
                sp.sem_inc(loads_begun, 1)
                sp.dma_start(raw[:, slot], view[:, :, bass.ds(col, P)]).then_inc(raw_in[slot], 16)

            with sp.Fori(0, KB) as j:
                for r, role in enumerate((B_GATE, B_VAL, C_V, A_CG, A_H, A_BG)):
                    load(r % 2, j * 6 + (N_S1 + r), in_v, j * P + role)

            def pairs(n0, gate, out_v):
                with sp.Fori(0, KB) as o:
                    load(0, o * 2 + n0, in_v, o * P + gate)
                    load(1, o * 2 + (n0 + 1), out_v, o * P)

            def singles(n0, view, col0):
                with sp.Fori(0, KB // 2) as i:
                    for s in range(2):
                        load(s, i * 2 + (n0 + s), view, i * 2 * P + (col0 + s * P))

            pairs(N_GA, G_A, a_out_v)
            singles(N_U, in_v, C_U)
            sp.dma_start(new_a_sample[0, :, 0:KA - 2, :], state_conv_a[0, :, 1:KA - 1, :]).then_inc(states_out, 16)
            sp.dma_start(new_b_sample[0, :, 0:KC - 2, :], state_conv_b[0, :, 1:KC - 1, :]).then_inc(states_out, 16)
            pairs(N_GC, G_C, c_out_v)
            pairs(N_GB, G_B, b_out_v)
            singles(N_WO, o_v, 0)

            def expert_load(ps, s, e, which):
                dst, src, k, sems = {"gate": (w_gate, gate_v, KB, ps.gate_in), "up": (w_up, up_v, KB, ps.up_in),
                                     "down": (w_down, down_v, FB, ps.down_in)}[which]
                sp.dma_start(dst[s][:], src[:, bass.ds(e * k, k), :]).then_inc(sems[s], 16)

            def expert_pass(ps, row0, n0, ready):
                for s in range(2):
                    if s < len(ready):
                        ready[s]()
                    for which in ("gate", "up", "down"):
                        expert_load(ps, s, s, which)
                if ready:
                    ready[2]()

                def store(s, e, t):
                    sp.wait_ge(ps.y_ready, t + 2)
                    sp.dma_start(y_rows[bass.ds(e * P + row0, P), :], y_out[:, s]).then_inc(ps.stored[s], 16)

                with sp.Fori(0, E // 2 - 1) as i:
                    for s in range(2):
                        e = i * 2 + s
                        t = e + n0
                        for which, done in (("gate", ps.gate_done), ("up", ps.up_done), ("down", ps.down_done)):
                            sp.wait_ge(done, t + 1)
                            expert_load(ps, s, e + 2, which)
                        store(s, e, t)
                for s in range(2):
                    store(s, E - 2 + s, n0 + E - 2 + s)

            def slot0_free():
                sp.wait_ge(proj_done, 2 + N_WO + 1)

            def slot1_free():
                sp.wait_ge(h_pre, KB)
                sp.wait_ge(proj_done, 2 + N_END)

            def h_out():
                for b in range(NTB):
                    n = P if b < 4 else TS
                    sp.wait_ge(h_tok_ready, b + 1)
                    sp.dma_start(h_rows[b * P:b * P + n, :], h_tok[0:n, b, :]).then_inc(h_stored, 16)

            sp.sem_inc(first.stored[0], 16)
            sp.sem_inc(first.stored[1], 16)
            expert_pass(first, 0, 0, [slot0_free, slot1_free, h_out])
            for s in range(2):
                sp.wait_ge(first.stored[s], 16 * (E // 2 + 1))
            n_max = further_passes(sp)
            with sp.If(n_max > P):
                sp.sem_inc(further.stored[0], 16)
                sp.sem_inc(further.stored[1], 16)
                with sp.Fori(0, PASSES - 1) as q:
                    expert_pass(further, q * (E * P) + E * P, q * E, [])
                for s in range(2):
                    sp.wait_ge(further.stored[s], 16 * (E // 2 * (PASSES - 1) + 1))
                sp.nop()
            with sp.Else():
                sp.nop()
            sp.sem_inc(y_read, 1)
            for b in range(NTB):
                n = P if b < 4 else TS
                sp.wait_ge(fin_ready, b + 1)
                dst = y_prompt[0, b * P:(b + 1) * P, :] if b < 4 else y_sample[:, 0, :]
                sp.dma_start(dst, fin[0:n, b % 2, :]).then_inc(fin_out[b % 2], 16)
            sp.wait_ge(fin_out[0], 48)
            sp.wait_ge(fin_out[1], 32)
            sp.wait_ge(tails_out, 80)
            sp.wait_ge(states_out, 32)

        @block.gpsimd
        def _(pool):
            chain = Tally(pool, pool_chain)
            pool.sem_inc(w_split, 2)
            chain.inc(pool.memset(ident[:], 0.0))
            chain.wait()
            pool.affine_select(out=ident[:], in_=ident[:], compare_op=ALU.not_equal, fill=1.0, base=0,
                               pattern=[[-1, P]], channel_multiplier=1).then_inc(const_ready, 1)
            pool.memset(mean_w[:], 1.0 / D)
            pool.memset(eps_t[:], EPS).then_inc(const_ready, 1)
            pool.wait_ge(spatial_in, 48)
            pool.affine_select(out=ws_nat[:], in_=ws_nat[:], compare_op=ALU.is_ge, fill=0.0, base=0,
                               pattern=[[0, KB], [-1, P]], channel_multiplier=1).then_inc(spatial_masked, 1)

            def lower(slot, n):
                pool.wait_ge(w_rounded, n + 1)
                pool.tensor_tensor(w_lo[:, slot], raw[:, slot], w_hi[:, slot].bitcast(F32), ALU.subtract).then_inc(w_split, 1)

            with pool.Fori(0, N_GA // 6) as j:
                for r in range(6):
                    lower(r % 2, j * 6 + r)
            chain.inc(pool.memset(tri[:], 1.0))
            pool.memset(ones_b[:], 1.0)
            chain.wait()
            pool.affine_select(out=tri[:], in_=tri[:], compare_op=ALU.is_ge, fill=0.0, base=-1,
                               pattern=[[1, P]], channel_multiplier=-1)
            pool.iota(id_cols[:, :, 0], pattern=[[P, NTB]], base=0, channel_multiplier=0, allow_small_or_imprecise_dtypes=True)
            pool.iota(id_cols[:, :, 1], pattern=[[0, NTB]], base=0, channel_multiplier=1, allow_small_or_imprecise_dtypes=True)
            pool.iota(e_off[:], pattern=[[0, NTB], [P, E]], base=0, channel_multiplier=0, allow_small_or_imprecise_dtypes=True)
            pool.iota(c4[:].rearrange("p b (g i) -> p (b g) i", i=PER_GROUP), pattern=[[0, NTB * GROUPS], [-1, PER_GROUP]],
                      base=PER_GROUP, channel_multiplier=0, allow_small_or_imprecise_dtypes=True).then_inc(const_ready, 1)
            with pool.Fori(0, (N_END - N_GA) // 2) as j:
                for s in range(2):
                    lower(s, j * 2 + (N_GA + s))
            pool.wait_ge(h_pre, KB)
            pool.iota(iota, pattern=[[1, P]], base=0, channel_multiplier=0,
                      allow_small_or_imprecise_dtypes=True).then_inc(const_ready, 1)

            def gathers(ps, n0):
                for e in range(E):
                    t = e + n0
                    pool.wait_ge(ps.ids_ready, t + 3)
                    pool.wait_ge(ps.turned, t + 1)
                    pool.sem_inc(gathers_begun, 1)
                    pool.indirect_dma_start(out=hs[:, e % 2, :], out_offset=None, in_=h_rows,
                                            in_offset=bass.IndirectOffsetOnAxis(ap=ids[:, e:e + 1], axis=0)).then_inc(ps.gathered[e % 2], 16)

            pool.wait_ge(h_stored, 16 * NTB)
            gathers(first, 0)

            def finish(table):
                pool.wait_ge(y_read, 1)
                pool.wait_ge(slots_ready, 2)

                def fetch(b):
                    n = P if b < 4 else TS
                    for dst, slot in ((y_a, slot_a), (y_b, slot_b)):
                        pool.indirect_dma_start(out=dst[0:n, b % 2, :], out_offset=None, in_=table,
                                                in_offset=bass.IndirectOffsetOnAxis(ap=slot[0:n, b:b + 1], axis=0)).then_inc(y_in[b % 2], 16)

                fetch(0)
                fetch(1)
                for b in range(NTB):
                    n = P if b < 4 else TS
                    pool.wait_ge(normed, b + 1)
                    pool.tensor_tensor(fin[0:n, b % 2, :], fin[0:n, b % 2, :], ln2_rows[0:n, 0, :], ALU.mult).then_inc(fin_g, 1)
                    if b + 2 < NTB:
                        fetch(b + 2)

            n_max = further_passes(pool)
            with pool.If(n_max > P):
                pool.wait_ge(first.turned, 2 + E)
                with pool.Fori(0, PASSES - 1) as q:
                    gathers(further, q * E)
                finish(y_rows)
            with pool.Else():
                finish(y_rows[0:E * P, :])

        @block.scalar
        def _(act):
            act.sem_inc(evacuated, 2)
            for view, r, k in ((conv_b_w[0], R_CONVB, KC), (conv_a_w[0], R_CONVA, KA), (conv_b_bias, R_BIAS, 1), (norm_b_g, R_NBG, 1),
                               (norm_b_b, R_NBB, 1), (v_norm_g, R_VG, 1), (v_norm_b, R_VB, 1), (ln1_g, R_L1G, 1), (ln1_b, R_L1B, 1),
                               (state_conv_a[0].rearrange("s k n -> (s k) n"), R_STA, 2 * TS)):
                act.dma_start(rows[r:r + k, :], view).then_inc(rows_in, 16)
            act.dma_start(sb_tok[:], state_conv_b[0].rearrange("(b s) k n -> (s k) b n", b=2)).then_inc(states_in, 16)
            act.dma_start(ws_nat[:], w_spatial[0].rearrange("g t s -> t g s")).then_inc(spatial_in, 16)
            act.dma_start(bs[:], b_spatial[0].partition_broadcast(P)).then_inc(spatial_in, 16)
            with nc.allow_non_contiguous_dma(reason="one weight per group"):
                act.dma_start(w00[:].unsqueeze(2), w_spatial[0, :, 0, 0:1].partition_broadcast(P)).then_inc(spatial_in, 16)
            act.dma_start(rw[:], router_w.rearrange("(k p) e -> p k e", p=P)).then_inc(late_in, 16)
            act.dma_start(rb[:], router_b.partition_broadcast(P)).then_inc(late_in, 16)

            def round_w(slot, use, n):
                act.wait_ge(raw_in[slot], use * 16 + 16)
                act.wait_ge(proj_done, n + 1)
                act.activation(w_hi[:, slot], raw[:, slot], ACT.Copy).then_inc(w_rounded, 1)

            def evacuate(n, src, out, func=ACT.Copy):
                act.wait_ge(proj_done, n + 3)
                act.activation(out, src[:, :, 0:HALF], func).then_inc(evacuated, 1)

            def halves(ap):
                return ap.rearrange("p (h t) -> p h t", h=2)

            for j in range(KB):
                act.wait_ge(x_turned, j + 1)
                act.activation(x_hi[:, j, 0:TP], pr[j // 2 % 2][:, j % 2, :], ACT.Copy).then_inc(x_rounded, 1)
            act.wait_ge(round_done, DONE["xs"])
            act.activation(x_hi[:, :, TP:T], work[TILE["xs"]][:, 0, 0:KB * TS].rearrange("p (k s) -> p k s", s=TS),
                           ACT.Copy).then_inc(x_rounded, 1)
            round_w(0, 0, 0)

            def next_w(s, use, n):
                round_w(1 - s, use if s == 0 else use + 1, n + 1)

            with act.Fori(0, KB) as j:
                for r, (out, func, g) in enumerate(((halves(ev[0][:]), ACT.Sigmoid, 1), (halves(ev[1][:]), ACT.Copy, 1),
                                                    (None, ACT.Copy, 0), (halves(ev[2][:]), ACT.Copy, 2),
                                                    (halves(ev[3][:]), ACT.Copy, 2), (halves(ev[4][:]), ACT.Copy, 3))):
                    n = j * 6 + r
                    next_w(r % 2, j * 3 + r // 2, n)
                    if out is None:
                        out = v[:, bass.ds(j, 1), :].rearrange("p o (h t) -> p (o h) t", h=2)
                    else:
                        act.wait_ge(gated, j * 3 + g)
                    evacuate(n, pr[r % 2], out, func)

            def gate_pairs(n0, m0, count, with_b=False):
                with act.Fori(0, count // 2) as i:
                    for b in range(2):
                        mm = i * 2 + (m0 + b)
                        for s in range(2):
                            n = i * 4 + (n0 + 2 * b + s)
                            next_w(s, i * 2 + (n0 // 2 + b), n)
                            if s == 0:
                                act.wait_ge(gated, mm + 26)
                            evacuate(n, pr[s], halves(ev[2 * b + s][:]), ACT.Copy if s else ACT.Sigmoid)
                        if with_b:
                            act.wait_ge(b_normed, i * 2 + (b + 1))
                            act.activation(sig_b[:, bass.ds(i * 2 + b, 1), :], cb[:, bass.ds(i * 2 + b, 1), :], ACT.Sigmoid).then_inc(b_sig, 1)

            def singles(n0, m0, count, last=False):
                with act.Fori(0, count // 2 - (1 if last else 0)) as i:
                    for s in range(2):
                        n = i * 2 + (n0 + s)
                        next_w(s, i + n0 // 2, n)
                        act.wait_ge(gated, i * 2 + (m0 + s + 26))
                        evacuate(n, pr[s], halves(ev[2 * s][:]))
                if last:
                    for s in range(2):
                        n = n0 + count - 2 + s
                        if s == 0:
                            next_w(s, n // 2, n)
                        act.wait_ge(gated, m0 + count - 2 + s + 26)
                        evacuate(n, pr[s], halves(ev[2 * s][:]))

            def root(name, k):
                act.wait_ge(round_done, DONE[name])
                if k:
                    act.wait_ge(std_used, k)
                act.activation(halves(std[:]), work[TILE[name]][:, :, 0:HALF], ACT.Sqrt, bias=eps_t[:]).then_inc(std_ready, 1)

            gate_pairs(N_GA, 0, 4)
            root("varV", 0)
            gate_pairs(N_GA + 8, 4, 4)
            root("varB", 1)
            for c in range(4):
                act.wait_ge(round_done, DONE[f"vt{c}"])
                act.activation(vt[:, c, :].rearrange("p (h t) -> p h t", h=2), work[TILE[f"vt{c}"]][:], ACT.Copy).then_inc(vt_ready, 1)
            for i, (name, k) in enumerate((("tailB", 38), ("tailA", 10), ("tailV", 8))):
                act.wait_ge(round_done, DONE[name])
                act.activation(tails[0:k, i, :].rearrange("p (h t) -> p h t", h=2), work[TILE[name]][0:k], ACT.Copy).then_inc(tails_ready, 1)
            act.wait_ge(tails_ready, 3)
            act.dma_start(new_b_prompt[0, 0], tails[0:30, 0, :]).then_inc(tails_out, 16)
            act.dma_start(new_b_sample[0, :, KC - 2, :], tails[30:38, 0, :]).then_inc(tails_out, 16)
            act.dma_start(new_a_prompt[0, 0], tails[0:2, 1, :]).then_inc(tails_out, 16)
            act.dma_start(new_a_sample[0, :, KA - 2, :], tails[2:10, 1, :]).then_inc(tails_out, 16)
            act.dma_start(new_v_sample[0, :, 0, :], tails[0:8, 2, :]).then_inc(tails_out, 16)
            singles(N_U, 8, 8)
            gate_pairs(N_GC, 16, 8, with_b=True)
            gate_pairs(N_GB, 24, 8)
            singles(N_WO, 32, 8, last=True)
            root("varH", 2)
            act.wait_ge(logits_ready, 1)
            act.activation(probs[:], probs[:], ACT.Exp).then_inc(exp_ready, 1)
            for b in range(NTB):
                n = P if b < 4 else TS
                act.wait_ge(round_done, DONE[f"ht{b}"])
                act.activation(h_tok[0:n, b, :].rearrange("p (h t) -> p h t", h=2), work[TILE[f"ht{b}"]][0:n], ACT.Copy).then_inc(h_tok_ready, 1)
            act.wait_ge(proj_done, 2 + N_END)
            act.dma_start(ln2_rows[:, 0, :], ln2_g[0].partition_broadcast(P)).then_inc(late_in, 16)
            act.dma_start(ln2_rows[:, 1, :], ln2_b[0].partition_broadcast(P)).then_inc(late_in, 16)

            def turn_in(ps, s, t):
                act.wait_ge(ps.turned, t + 3)
                act.activation(hs_t[:, s].rearrange("p (h k) t -> p h (k t)", h=2), work[0][:], ACT.Copy).then_inc(ps.hs_t_ready, 1)

            def expert(ps, s, t, i, ahead):
                act.wait_ge(ps.gate_done, t + 1)
                act.activation(silu[:, s], pr[s][:, 0, :].rearrange("p (f t) -> p f t", f=FB), ACT.Silu).then_inc(ps.silu_ready, 1)
                if ahead:
                    turn_in(ps, 1 - s, t + 1)
                act.wait_ge(ps.down_done, t + 1)
                act.wait_ge(ps.stored[s], i * 16 + 16)
                act.activation(y_out[:, s].rearrange("p (h n) -> p h n", h=2), work[1][:], ACT.Copy).then_inc(ps.y_ready, 1)

            def expert_pass(ps, n0, i0):
                turn_in(ps, 0, n0)
                with act.Fori(0, E // 2 - 1) as i:
                    for s in range(2):
                        expert(ps, s, i * 2 + s + n0, i + i0, True)
                for s in range(2):
                    expert(ps, s, n0 + (E - 2 + s), i0 + (E // 2 - 1), s == 0)

            act.sem_inc(first.hs_t_ready, 1)
            act.sem_inc(first.y_ready, 1)
            act.wait_ge(mb_ready, 1)
            expert_pass(first, 0, 0)
            n_max = further_passes(act)
            with act.If(n_max > P):
                act.sem_inc(further.hs_t_ready, 1)
                act.sem_inc(further.y_ready, 1)
                with act.Fori(0, PASSES - 1) as q:
                    expert_pass(further, q * E, q * (E // 2))
                act.nop()
            with act.Else():
                act.nop()
            for b in range(NTB):
                n = P if b < 4 else TS
                s = b % 2
                act.wait_ge(var_ready, b + 1)
                act.activation(agg[0:n, s, 2:3], agg[0:n, s, 1:2], ACT.Sqrt, bias=eps_t[0:n]).then_inc(std2_ready, 1)
                act.wait_ge(scale_ready, b + 1)
                if b >= 2:
                    act.wait_ge(fin_out[s], 16 * (b // 2))
                act.activation(fin[0:n, s, :], y_a[0:n, s, :], ACT.Identity, scale=agg[0:n, s, 2:3],
                               bias=agg[0:n, s, 3:4]).then_inc(normed, 1)

        @block.tensor
        def _(pe):
            pe.sem_inc(proj_done, 2)
            pe.wait_ge(const_ready, 1)
            pe.wait_ge(x_in, 32)
            for j in range(KB):
                if j >= 4:
                    pe.wait_ge(x_split, j - 3)
                for b in range(4):
                    mm = pe.transpose(pr[j // 2 % 2][:, j % 2, b * P:(b + 1) * P], x_tok[:, b, j * P:(j + 1) * P], ident[:])
                mm.then_inc(x_turned, 1)
            pe.wait_ge(rows_in, 160)
            for k in range(KB):
                mm = pe.transpose(work[1][:, 0, k * NROWS:(k + 1) * NROWS], rows[:, k * P:(k + 1) * P], ident[0:NROWS, 0:NROWS])
            mm.then_inc(round_done, 1)
            for k in range(KB):
                mm = pe.transpose(work[0][:, 0, k * TS:(k + 1) * TS], xs_tok[:, k * P:(k + 1) * P], ident[0:TS, 0:TS])
            mm.then_inc(round_done, 1)
            pe.wait_ge(states_in, 16)
            for i in range(2):
                work_wait(pe, f"sb{i}")
                for k in range(4 * i, 4 * i + 4):
                    for b in range(2):
                        q = (k - 4 * i)
                        mm = pe.transpose(work[TILE[f"sb{i}"]][:, q // 2, q % 2 * 240 + b * 120:q % 2 * 240 + b * 120 + 120],
                                          sb_tok[:, b, k * P:(k + 1) * P], ident[0:120, 0:120])
                mm.then_inc(round_done, 1)
            pe.wait_ge(spatial_masked, 1)
            for i in range(2):
                work_wait(pe, f"ws{i}")
                for g in range(4):
                    mm = pe.transpose(work[TILE[f"ws{i}"]][:, 0, g * P:(g + 1) * P], ws_nat[:, 4 * i + g, :], ident[:])
                mm.then_inc(round_done, 1)
            pe.wait_ge(x_split, KB + 1)

            def project(slot, n, hi, lo):
                pe.wait_ge(w_split, n + 3)
                pe.wait_ge(evacuated, n + 1)
                for k in range(KB):
                    for w, x in ((w_hi, hi), (w_hi, lo), (w_lo, hi)):
                        for h in range(2):
                            mm = pe.matmul(pr[slot][:, h, 0:HALF], w[:, slot, k, :], x[:, k, h * HALF:(h + 1) * HALF],
                                           start=(k == 0 and w is w_hi and x is hi), stop=(k == KB - 1 and w is w_lo))
                mm.then_inc(proj_done, 1)

            def mean(name, z):
                work_wait(pe, name)
                for h in range(2):
                    for k in range(KB):
                        mm = pe.matmul(work[TILE[name]][:, h, 0:HALF], mean_w[:], z[:, k, h * HALF:(h + 1) * HALF],
                                       start=(k == 0), stop=(k == KB - 1))
                mm.then_inc(round_done, 1)

            with pe.Fori(0, KB) as j:
                for r in range(6):
                    project(r % 2, j * 6 + r, x_hi, x_lo)

            def pairs(n0, count, hi, lo, ready):
                with pe.Fori(0, count) as o:
                    project(0, o * 2 + n0, x_hi, x_lo)
                    pe.wait_ge(ready, KB)
                    project(1, o * 2 + (n0 + 1), hi, lo)

            def singles(n0, hi, lo):
                with pe.Fori(0, KB // 2) as i:
                    for s in range(2):
                        project(s, i * 2 + (n0 + s), hi, lo)

            pe.wait_ge(const_ready, 2)
            pe.wait_ge(evacuated, N_GA + 2)
            mean("meanV", v)
            pairs(N_GA, 4, p_hi, p_lo, a_split)
            pe.wait_ge(sq_ready, 1)
            mean("varV", sq)
            pe.wait_ge(conv_done, KB)
            mean("meanB", cb)
            pairs(N_GA + 8, 4, p_hi, p_lo, a_split)
            pe.wait_ge(sq_ready, 2)
            mean("varB", sq)
            pe.wait_ge(v_ready, KB)
            for c in range(4):
                work_wait(pe, f"vt{c}")
                for g in range(KB):
                    mm = pe.transpose(work[TILE[f"vt{c}"]][:, g // 4, g % 4 * P:(g % 4 + 1) * P], v[:, g, c * P:(c + 1) * P], ident[:])
                mm.then_inc(round_done, 1)
            for name, src in (("tailB", tail_b[:]), ("tailA", tail_a[:]), ("tailV", v[:, :, TP:T])):
                work_wait(pe, name)
                k = src.shape[2]
                for g in range(KB):
                    mm = pe.transpose(work[TILE[name]][0:k, g // 4, g % 4 * P:(g % 4 + 1) * P], src[:, g, :], ident[:])
                mm.then_inc(round_done, 1)
            pe.wait_ge(vt_ready, 4)
            for q in range(4):
                work_wait(pe, f"sp{q}")
                for i in range(2):
                    g = 2 * q + i
                    for c in range(4):
                        mm = pe.matmul(work[TILE[f"sp{q}"]][:, i, c * P:(c + 1) * P], vt[:, c, g * P:(g + 1) * P], ws_t[:, g, :],
                                       start=True, stop=True)
                mm.then_inc(round_done, 1)
            singles(N_U, x_hi, x_lo)
            pairs(N_GC, KB, q_hi, q_lo, c_split)
            pairs(N_GB, KB, p_hi, p_lo, b_split)
            pe.wait_ge(merged_split, KB)
            singles(N_WO, q_hi, q_lo)
            pe.wait_ge(h_pre, KB)
            mean("meanH", m)
            pe.wait_ge(sq_ready, 3)
            mean("varH", sq_h)
            pe.wait_ge(late_in, 32)
            pe.wait_ge(h_ready, KB)
            work_wait(pe, "logits")
            for b in range(NTB):
                n = P if b < 4 else TS
                for k in range(KB):
                    mm = pe.matmul(work[1][0:n, 0, b * E:(b + 1) * E], m[:, k, b * P:b * P + n], rw[:, k, :],
                                   start=(k == 0), stop=(k == KB - 1))
            mm.then_inc(round_done, 1)
            for b in range(NTB):
                n = P if b < 4 else TS
                work_wait(pe, f"ht{b}")
                for k in range(KB):
                    mm = pe.transpose(work[TILE[f"ht{b}"]][0:n, k // 4, k % 4 * P:(k % 4 + 1) * P], m[:, k, b * P:b * P + n], ident[:])
                mm.then_inc(round_done, 1)
            pe.wait_ge(mb_ready, 1)
            pe.wait_ge(const_ready, 3)
            work_wait(pe, "pos")
            for b in range(NTB):
                mm = pe.matmul(work[1][:, 0, b * E:(b + 1) * E], tri[:], mb[:, b, :], start=True, stop=(b == 0))
                for c in range(b):
                    mm = pe.matmul(work[1][:, 0, b * E:(b + 1) * E], ones_b[:], mb[:, c, :], start=False, stop=(c == b - 1))
            for b in range(NTB):
                mm = pe.matmul(work[1][:, 0, NTB * E:(NTB + 1) * E], ones_b[:], mb[:, b, :], start=(b == 0), stop=(b == NTB - 1))
            mm.then_inc(round_done, 1)

            def find_ids(ps, n0):
                with pe.Fori(0, E // 2) as i:
                    pe.wait_ge(ps.y_ready, n0 + 1)
                    for s in range(2):
                        pe.wait_ge(ps.onehot_ready, i * 2 + s + n0 + 1)
                        pe.wait_ge(ps.ids_ready, i * 2 + s + n0 + 1)
                        for b in range(NTB):
                            mm = pe.matmul(work[1][:, s, 0:2], onehot[:, s, b, :], id_cols[:, b, :], start=(b == 0), stop=(b == NTB - 1))
                        mm.then_inc(ps.ids_mm, 1)

            def turn(ps, s, t, use):
                pe.wait_ge(ps.gathered[s], use * 16 + 16)
                pe.wait_ge(ps.hs_t_ready, t + 1)
                for k in range(KB):
                    mm = pe.transpose(work[0][:, k // 4, k % 4 * P:(k % 4 + 1) * P], hs[:, s, k * P:(k + 1) * P], ident[:])
                mm.then_inc(ps.turned, 1)

            def expert(ps, s, t, use, ahead):
                pe.wait_ge(ps.hs_t_ready, t + 2)
                for h, (w, landed, done) in enumerate(((w_gate, ps.gate_in, ps.gate_done), (w_up, ps.up_in, ps.up_done))):
                    pe.wait_ge(landed[s], use * 16 + 16)
                    for f in range(FB):
                        for k in range(KB):
                            mm = pe.matmul(pr[s][:, h, f * P:(f + 1) * P], w[s][:, k, f * P:(f + 1) * P], hs_t[:, s, k, :],
                                           start=(k == 0), stop=(k == KB - 1))
                    mm.then_inc(done, 1)
                if ahead:
                    turn(ps, 1 - s, t + 1, use + s)
                pe.wait_ge(ps.down_in[s], use * 16 + 16)
                pe.wait_ge(ps.u_ready, t + 1)
                pe.wait_ge(ps.y_ready, t + 1)
                for f in range(FB):
                    for h in range(2):
                        mm = pe.matmul(work[1][:, h, :], u_t[:, s, f, :], w_down[s][:, f, h * 512:(h + 1) * 512],
                                       start=(f == 0), stop=(f == FB - 1))
                mm.then_inc(ps.down_done, 1)

            def expert_pass(ps, n0, i0):
                find_ids(ps, n0)
                turn(ps, 0, n0, i0)
                with pe.Fori(0, E // 2 - 1) as i:
                    for s in range(2):
                        expert(ps, s, i * 2 + s + n0, i + i0, True)
                for s in range(2):
                    expert(ps, s, n0 + (E - 2 + s), i0 + (E // 2 - 1), s == 0)

            pe.sem_inc(first.turned, 2)
            expert_pass(first, 0, 0)
            n_max = further_passes(pe)
            with pe.If(n_max > P):
                pe.sem_inc(further.turned, 2)
                pe.wait_ge(first.y_ready, E + 1)
                with pe.Fori(0, PASSES - 1) as q:
                    expert_pass(further, q * E, q * (E // 2))
                pe.nop()
            with pe.Else():
                pe.nop()

        @block.vector
        def _(dve):
            chain = Tally(dve, dve_chain)
            last = [chain]

            def do(ins, tally=chain):
                tally.inc(ins)
                last[0] = tally

            def settle():
                last[0].wait()

            gates = Tally(dve, gated, 3)
            dve.sem_inc(gated, 3)
            tallies = {s: Tally(dve, s) for s in (setup_done, x_split, tail_cols, a_split, b_split, c_split, merged_split, conv_done,
                                                  b_normed, centred, sq_ready, std_used, v_ready, spatial_read, h_pre, h_ready)}

            def to(s):
                return tallies[s]

            to_logits, to_mb, to_count, to_slots = (Tally(dve, s) for s in (logits_ready, mb_ready, count_ready, slots_ready))
            to_var, to_scale, to_fin = (Tally(dve, s) for s in (var_ready, scale_ready, fin_ready))

            def col(k, r):
                return par[:, bass.ds(k * NROWS + r, 1)]

            def blk(t, k, a=0, b=T):
                return t[:, bass.ds(k, 1), a:b].rearrange("p o t -> p (o t)")

            do(dve.memset(b_pad[:, 0:KC - 1], 0.0))
            do(dve.memset(a_pad[:, 0:KA - 1], 0.0))
            do(dve.memset(mb[:], 0.0))
            for j in range(KB):
                dve.wait_ge(x_rounded, j + 1)
                do(dve.tensor_tensor(x_lo[:, j, 0:TP], pr[j // 2 % 2][:, j % 2, :], x_hi[:, j, 0:TP].bitcast(F32), ALU.subtract), to(x_split))
            dve.wait_ge(x_rounded, KB + 1)
            do(dve.tensor_tensor(x_lo[:, :, TP:T], work[0][:, 0, 0:KB * TS].rearrange("p (k s) -> p k s", s=TS),
                                 x_hi[:, :, TP:T].bitcast(F32), ALU.subtract), to(x_split))
            dve.wait_ge(round_done, DONE["rows"])
            do(dve.tensor_copy(par[:], work[1][:, 0, 0:KB * NROWS]), to(setup_done))
            for i in range(2):
                dve.wait_ge(round_done, DONE[f"sb{i}"])
                for q in range(2):
                    do(dve.tensor_copy(sb_t[:, 4 * i + 2 * q:4 * i + 2 * q + 2].rearrange("p k s c -> p (k s c)"),
                                       work[TILE[f"sb{i}"]][:, q, 0:480]), chain if q == 0 else to(setup_done))
            for i in range(2):
                dve.wait_ge(round_done, DONE[f"ws{i}"])
                do(dve.tensor_copy(ws_t[:, 4 * i:4 * i + 4].rearrange("p g t -> p (g t)"), work[TILE[f"ws{i}"]][:, 0, :]), to(setup_done))
            settle()
            par_k = par[:].rearrange("p (k r) -> p k r", r=NROWS)
            state_a = par_k[:, :, R_STA:R_STA + 2 * TS].rearrange("p k (s c) -> p k s c", c=2)
            do(dve.tensor_tensor(sb_t[:], sb_t[:], rep(par_k[:, :, R_CONVB:R_CONVB + KC - 1], 2, TS), ALU.mult))
            do(dve.tensor_tensor(samp_a[:], state_a[:, :, :, 0], par_k[:, :, R_CONVA:R_CONVA + 1].to_broadcast([P, KB, TS]), ALU.mult))
            do(dve.tensor_tensor(samp_t[:], state_a[:, :, :, 1], par_k[:, :, R_CONVA + 1:R_CONVA + 2].to_broadcast([P, KB, TS]), ALU.mult))
            settle()
            do(dve.tensor_tensor(samp_a[:], samp_a[:], samp_t[:], ALU.add))
            do(dve.tensor_reduce(samp_b[:], sb_t[:], AX.X, ALU.add))
            settle()
            do(dve.tensor_tensor(samp_b[:], samp_b[:], par_k[:, :, R_BIAS:R_BIAS + 1].to_broadcast([P, KB, TS]), ALU.add))

            def branches(j):
                dve.wait_ge(evacuated, j * 6 + (1 + 3))
                settle()
                do(dve.tensor_tensor(b_pad[:, KC - 1:KC - 1 + T], ev[0][:], ev[1][:], ALU.mult), gates)
                dve.wait_ge(evacuated, j * 6 + (4 + 3))
                do(dve.tensor_tensor(a_pad[:, KA - 1:KA - 1 + T], ev[2][:], ev[3][:], ALU.mult), gates)
                gates.wait(1)
                do(dve.tensor_copy(blk(tail_b, j, 0, 38), b_pad[:, TP:TP + 38]))
                gates.wait()
                do(dve.tensor_copy(blk(tail_a, j, 0, 10), a_pad[:, TP:TP + 10]))
                do(dve.tensor_scalar(acc_a[:, 0:TP], a_pad[:, 0:TP], col(j, R_CONVA), None, ALU.mult))
                do(dve.scalar_tensor_tensor(acc_a[:, TP:T], a_pad[:, KA - 1 + TP:], col(j, R_CONVA + 2), blk(samp_a, j, 0, TS), ALU.mult, ALU.add))
                for k in (1, 2):
                    settle()
                    do(dve.scalar_tensor_tensor(acc_a[:, 0:TP], a_pad[:, k:k + TP], col(j, R_CONVA + k), acc_a[:, 0:TP], ALU.mult, ALU.add))
                dve.wait_ge(evacuated, j * 6 + (5 + 3))
                settle()
                do(dve.tensor_tensor(acc_a[:], acc_a[:], ev[4][:], ALU.mult), gates)
                settle()
                do(dve.tensor_copy(blk(p_hi, j), acc_a[:]))
                do(dve.tensor_scalar(blk(cb, j, 0, TP), b_pad[:, 0:TP], col(j, R_CONVB), col(j, R_BIAS), ALU.mult, ALU.add))
                chain.wait(1)
                do(dve.tensor_tensor(blk(p_lo, j), acc_a[:], blk(p_hi, j).bitcast(F32), ALU.subtract), to(a_split))
                do(dve.tensor_scalar(acc_b[:], b_pad[:, 1:1 + TP], col(j, R_CONVB + 1), None, ALU.mult))
                for k in range(2, KC):
                    acc = acc_b[:] if k % 2 else blk(cb, j, 0, TP)
                    chain.wait(1)
                    do(dve.scalar_tensor_tensor(acc, b_pad[:, k:k + TP], col(j, R_CONVB + k), acc, ALU.mult, ALU.add))
                settle()
                do(dve.tensor_tensor(blk(cb, j, 0, TP), blk(cb, j, 0, TP), acc_b[:], ALU.add))
                do(dve.scalar_tensor_tensor(blk(cb, j, TP, T), b_pad[:, KC - 1 + TP:], col(j, R_CONVB + KC - 1), blk(samp_b, j, 0, TS),
                                            ALU.mult, ALU.add), to(conv_done))

                settle()

            settle()
            looped = ((chain, 39), (gates, 3), (to(a_split), 1), (to(conv_done), 1))
            with dve.Fori(0, KB) as j:
                for t, n in looped:
                    t.enter(j, n)
                branches(j)
                for t, _ in looped:
                    t.leave(KB)

            def centre(name, z):
                dve.wait_ge(round_done, DONE[name])
                for h in range(2):
                    part = z[:, :, h * HALF:(h + 1) * HALF]
                    do(dve.tensor_tensor(part, part, rep(work[TILE[name]][:, h, 0:HALF], 1, KB), ALU.subtract),
                       to(centred) if h else chain)

            def squares(z, out):
                settle()
                do(dve.tensor_tensor(out[:], z[:], z[:], ALU.mult), to(sq_ready))

            def whiten(z, k):
                dve.wait_ge(std_ready, k)
                settle()
                do(dve.reciprocal(std[:], std[:]))
                settle()
                do(dve.tensor_tensor(z[:], z[:], rep(std[:], 1, KB), ALU.mult), to(std_used))
                settle()

            def affine(z, k, g, b, tally):
                do(dve.tensor_scalar(z[:, k, :], z[:, k, :], col(k, g), col(k, b), ALU.mult, ALU.add), tally)

            def merge(n0, o, b, how):
                dve.wait_ge(evacuated, o * 2 + (n0 + 1 + 3))
                gate, prod = ev[2 * b], ev[2 * b + 1]
                if how == "first":
                    do(dve.tensor_tensor(blk(m, o), gate[:], prod[:], ALU.mult), gates)
                    return
                do(dve.tensor_tensor(gate[:], gate[:], prod[:], ALU.mult))
                settle()
                do(dve.tensor_tensor(blk(m, o), blk(m, o), gate[:], ALU.add), gates)
                if how == "last":
                    settle()
                    split(blk(m, o), blk(q_hi, o), blk(q_lo, o), to(merged_split))

            def split(z, hi, lo, tally):
                do(dve.tensor_copy(hi, z))
                settle()
                do(dve.tensor_tensor(lo, z, hi.bitcast(F32), ALU.subtract), tally)

            merge(N_GA, 0, 0, "first")
            centre("meanV", v)
            merge(N_GA, 1, 1, "first")
            squares(v, sq)
            merge(N_GA, 2, 0, "first")
            merge(N_GA, 3, 1, "first")
            whiten(v, 1)
            for k in range(KB):
                affine(v, k, R_VG, R_VB, to(v_ready))
            merge(N_GA, 4, 0, "first")
            centre("meanB", cb)
            merge(N_GA, 5, 1, "first")
            squares(cb, sq)
            merge(N_GA, 6, 0, "first")
            merge(N_GA, 7, 1, "first")
            whiten(cb, 2)
            for q in range(4):
                dve.wait_ge(round_done, DONE[f"sp{q}"])
                do(dve.tensor_tensor(v[:, 2 * q:2 * q + 2, 0:TP].rearrange("p g (c t) -> p g c t", c=4),
                                     work[TILE[f"sp{q}"]][:].rearrange("p g (c t) -> p g c t", c=4),
                                     rep(bs[:, 2 * q:2 * q + 2, :], 2, 4), ALU.add), to(spatial_read))
            do(dve.tensor_tensor(v[:, :, TP:T], v[:, :, TP:T], rep(w00[:], 2, TS), ALU.mult))
            settle()
            do(dve.tensor_tensor(v[:, :, TP:T], v[:, :, TP:T], bs[:, :, 0:1].to_broadcast([P, KB, TS]), ALU.add))
            dve.wait_ge(tails_out, 80)
            for i in range(KB):
                dve.wait_ge(evacuated, N_U + i + 3)
                settle()
                do(dve.tensor_tensor(v[:, i, :], v[:, i, :], ev[2 * (i % 2)][:], ALU.mult), gates)
                affine(cb, i, R_NBG, R_NBB, to(b_normed))
                gates.wait()
                split(v[:, i, :], q_hi[:, i, :], q_lo[:, i, :], to(c_split))
            settle()
            looped = ((chain, 6), (gates, 2), (to(b_split), 2))
            with dve.Fori(0, KB // 2) as i:
                for t, n in looped:
                    t.enter(i, n)
                for b in range(2):
                    o = i * 2 + b
                    merge(N_GC, o, b, "add")
                    dve.wait_ge(b_sig, o + 1)
                    do(dve.tensor_tensor(blk(cb, o), blk(cb, o), blk(sig_b, o), ALU.mult))
                    settle()
                    split(blk(cb, o), blk(p_hi, o), blk(p_lo, o), to(b_split))
                    settle()
                for t, _ in looped:
                    t.leave(KB // 2)
            looped = ((chain, 4), (gates, 2), (to(merged_split), 2))
            with dve.Fori(0, KB // 2) as i:
                for t, n in looped:
                    t.enter(i, n)
                for b in range(2):
                    merge(N_GB, i * 2 + b, b, "last")
                    settle()
                for t, _ in looped:
                    t.leave(KB // 2)
            for i in range(KB):
                dve.wait_ge(evacuated, N_WO + i + 3)
                do(dve.scalar_tensor_tensor(m[:, i, :], x_hi[:, i, :].bitcast(F32), ALPHA, ev[2 * (i % 2)][:], ALU.mult, ALU.add), gates)
                settle()
                do(dve.scalar_tensor_tensor(m[:, i, :], x_lo[:, i, :].bitcast(F32), ALPHA, m[:, i, :], ALU.mult, ALU.add), to(h_pre))
            centre("meanH", m)
            squares(m, sq_h)
            whiten(m, 3)
            for k in range(KB):
                affine(m, k, R_L1G, R_L1B, to(h_ready))

            grp = lambda t: t[:].rearrange("p b (g i) -> p (b g) i", i=PER_GROUP)
            flat = lambda t: t[:].rearrange("p b g -> p (b g)")
            over4 = lambda t: rep(flat(t), 2, PER_GROUP)
            over_e = lambda t: rep(t[:], 2, E)

            def step(ins, tally=chain):
                do(ins, tally)
                settle()

            step(dve.memset(probs[:], 0.0))
            dve.wait_ge(late_in, 32)
            dve.wait_ge(round_done, DONE["logits"])
            do(dve.tensor_tensor(probs[:, 0:4, :], work[1][:, 0, 0:4 * E].rearrange("p (b e) -> p b e", e=E), rep(rb[:], 1, 4), ALU.add))
            step(dve.tensor_tensor(probs[0:TS, 4, :], work[1][0:TS, 0, 4 * E:5 * E], rb[0:TS, :], ALU.add))
            step(dve.tensor_reduce(s_max[:], probs[:], AX.X, ALU.max))
            step(dve.tensor_tensor(probs[:], probs[:], over_e(s_max), ALU.subtract), to_logits)
            dve.wait_ge(exp_ready, 1)
            step(dve.tensor_reduce(s_sum[:], probs[:], AX.X, ALU.add))
            step(dve.reciprocal(s_sum[:], s_sum[:]))
            step(dve.tensor_tensor(probs[:], probs[:], over_e(s_sum), ALU.mult))

            def first_of(values, top, is_first, best, n):
                step(dve.tensor_reduce(top, values, AX.X, ALU.max))
                step(dve.tensor_tensor(is_first, values, rep(top, 2, n), ALU.is_equal))
                step(dve.tensor_tensor(is_first, is_first, grp(c4)[:, 0:is_first.shape[1], :], ALU.mult))
                step(dve.tensor_reduce(best, is_first, AX.X, ALU.max))
                step(dve.tensor_tensor(is_first, is_first, rep(best, 2, n), ALU.is_equal))

            dve.wait_ge(const_ready, 3)
            first_of(grp(probs), flat(g_m1), grp(oh1), flat(g_t), PER_GROUP)
            step(dve.scalar_tensor_tensor(probs[:], oh1[:], -2.0, probs[:], ALU.mult, ALU.add))
            first_of(grp(probs), flat(g_m2), grp(oh2), flat(g_t), PER_GROUP)
            step(dve.tensor_tensor(g_t[:], g_m1[:], g_m2[:], ALU.add))
            first_of(g_t[:], s_max[:], g_best[:], s_t[:], GROUPS)
            for t in (oh1, oh2):
                do(dve.tensor_tensor(grp(t), grp(t), over4(g_best), ALU.mult))
            settle()
            do(dve.tensor_tensor(mb[:, 0:4, :], oh1[:, 0:4, :], oh2[:, 0:4, :], ALU.add))
            do(dve.tensor_tensor(mb[0:TS, 4, :], oh1[0:TS, 4, :], oh2[0:TS, 4, :], ALU.add), to_mb)
            do(dve.tensor_tensor(g_m1[:], g_m1[:], g_best[:], ALU.mult))
            step(dve.tensor_tensor(g_m2[:], g_m2[:], g_best[:], ALU.mult))
            do(dve.tensor_reduce(s_w1[:], g_m1[:], AX.X, ALU.add))
            step(dve.tensor_reduce(s_w2[:], g_m2[:], AX.X, ALU.add))
            step(dve.tensor_tensor(s_sum[:], s_w1[:], s_w2[:], ALU.add))
            step(dve.reciprocal(s_sum[:], s_sum[:]))
            do(dve.tensor_tensor(s_w1[:], s_w1[:], s_sum[:], ALU.mult))
            step(dve.tensor_tensor(s_w2[:], s_w2[:], s_sum[:], ALU.mult))
            pos = t1
            dve.wait_ge(round_done, DONE["pos"])
            do(dve.tensor_copy(pos[:], work[1][:, 0, 0:NTB * E].rearrange("p (b e) -> p b e", e=E)))
            step(dve.tensor_reduce(s_ps[:, 0:1], work[1][:, 0, NTB * E:(NTB + 1) * E], AX.X, ALU.max))
            do(dve.tensor_copy(count_i[:], s_ps[:, 0:1]), to_count)
            step(dve.tensor_tensor(posm[:], pos[:], mb[:], ALU.mult))
            step(dve.scalar_tensor_tensor(posm[:], mb[:], -1.0, posm[:], ALU.add, ALU.add))

            def find_ids(ps, n0, hot, cast):
                for e in range(0, E, 2):
                    for s in range(2):
                        do(dve.tensor_tensor(onehot[:, s], rep(iota, 1, NTB), rep(posm[:, :, e + s], 2, P), ALU.is_equal), hot)
                    for s in range(2):
                        dve.wait_ge(ps.ids_mm, n0 + (e + s + 1))
                        with nc.allow_low_precision(reason="whole numbers"):
                            do(dve.tensor_reduce(ids[:, e + s:e + s + 1], work[1][:, s, 0:2], AX.X, ALU.add), cast)

            def experts(ps, n0, tally):
                def one(s, t):
                    dve.wait_ge(ps.silu_ready, t + 1)
                    dve.wait_ge(ps.up_done, t + 1)
                    do(dve.tensor_tensor(u_t[:, s].rearrange("p f t -> p (f t)"), silu[:, s].rearrange("p f t -> p (f t)"),
                                         pr[s][:, 1, :], ALU.mult), tally)
                with dve.Fori(0, E // 2) as i:
                    for s in range(2):
                        one(s, i * 2 + s + n0)

            hot, cast, us = Tally(dve, first.onehot_ready), Tally(dve, first.ids_ready, 2), Tally(dve, first.u_ready)
            dve.sem_inc(first.ids_ready, 2)
            dve.wait_ge(const_ready, 4)
            find_ids(first, 0, hot, cast)
            last[0] = cast
            for oh, out in ((oh1, slot_a), (oh2, slot_b)):
                do(dve.tensor_tensor(t2[:], oh[:], e_off[:], ALU.mult))
                do(dve.tensor_tensor(probs[:], oh[:], pos[:], ALU.mult))
                settle()
                do(dve.tensor_reduce(s_slot[:], t2[:], AX.X, ALU.add))
                step(dve.tensor_reduce(s_ps[:], probs[:], AX.X, ALU.add))
                step(dve.tensor_tensor(s_slot[:], s_slot[:], s_ps[:], ALU.add))
                for k in range(1, PASSES):
                    step(dve.tensor_scalar(s_t[:], s_ps[:], float(k * P), float(E * P - P), ALU.is_ge, ALU.mult))
                    step(dve.tensor_tensor(s_slot[:], s_slot[:], s_t[:], ALU.add))
                step(dve.tensor_copy(out[:], s_slot[:]), to_slots)
            experts(first, 0, us)
            n_max = further_passes(dve)
            with dve.If(n_max > P):
                dve.sem_inc(further.ids_ready, 2)
                dve.wait_ge(first.y_ready, E + 1)
                hot, cast, us = Tally(dve, further.onehot_ready), Tally(dve, further.ids_ready, 2), Tally(dve, further.u_ready)
                more = Tally(dve, more_posm)
                with dve.Fori(0, PASSES - 1) as q:
                    for t, n in ((hot, E), (cast, E), (more, 1)):
                        t.enter(q, n)
                    do(dve.tensor_scalar(posm[:], posm[:], -float(P), None, ALU.add), more)
                    settle()
                    find_ids(further, q * E, hot, cast)
                    for t in (hot, cast, more):
                        t.leave(PASSES - 1)
                    us.enter(q, 0)
                    experts(further, q * E, us)
                dve.nop()
            with dve.Else():
                dve.nop()

            dve.wait_ge(late_in, 64)

            def combine(b):
                n, s = P if b < 4 else TS, b % 2
                dve.wait_ge(y_in[s], 32 * (b // 2) + 32)
                a = y_a[0:n, s, :]
                step(dve.tensor_scalar(a, a, s_w1[0:n, b:b + 1], None, ALU.mult))
                step(dve.scalar_tensor_tensor(a, y_b[0:n, s, :], s_w2[0:n, b:b + 1], a, ALU.mult, ALU.add))
                step(dve.scalar_tensor_tensor(a, h_tok[0:n, b, :], ALPHA, a, ALU.mult, ALU.add))
                for h in range(2):
                    do(dve.bn_stats(stats[0:n, s, h, :], y_a[0:n, s, h * 512:(h + 1) * 512]))
                settle()
                step(dve.bn_aggr(agg[0:n, s, 0:2], stats[0:n, s].rearrange("p h c -> p (h c)")), to_var)
                dve.wait_ge(std2_ready, b + 1)
                step(dve.reciprocal(agg[0:n, s, 2:3], agg[0:n, s, 2:3]))
                do(dve.scalar_tensor_tensor(agg[0:n, s, 3:4], agg[0:n, s, 0:1], -1.0, agg[0:n, s, 2:3], ALU.mult, ALU.mult), to_scale)

            def shift(b):
                n, s = P if b < 4 else TS, b % 2
                dve.wait_ge(fin_g, b + 1)
                do(dve.tensor_tensor(fin[0:n, s, :], fin[0:n, s, :], ln2_rows[0:n, 1, :], ALU.add), to_fin)

            last[0] = chain
            combine(0)
            for b in range(1, NTB):
                combine(b)
                shift(b - 1)
            shift(NTB - 1)


_INS = ['x_prompt', 'x_sample', 'state_conv_a', 'state_conv_b', 'w_in', 'conv_a_w', 'w_a_out', 'conv_b_w', 'conv_b_bias',
        'norm_b_g', 'norm_b_b', 'w_b_out', 'v_norm_g', 'v_norm_b', 'w_spatial', 'b_spatial', 'w_c_out', 'w_o', 'ln1_g', 'ln1_b',
        'router_w', 'router_b', 'expert_w_gate', 'expert_w_up', 'expert_w_down', 'ln2_g', 'ln2_b']
_OUTS = [(1, 512, 1024), (8, 1, 1024), (1, 1, 2, 1024), (1, 1, 30, 1024), (1, 8, 2, 1024), (1, 8, 30, 1024), (1, 8, 1, 1024)]


def kernel(**inputs):
    import numpy as _np
    import concourse.bacc as _bacc
    from concourse import mybir as _mybir
    from concourse.bass_utils import run_bass_kernel_spmd as _run

    nc = _bacc.Bacc("TRN2", target_bir_lowering=False, num_devices=1)
    arrays, args = {}, []
    for name in _INS:
        a = _np.ascontiguousarray(inputs[name])
        arrays[f"in_{name}_dram"] = a
        args.append(nc.dram_tensor(f"in_{name}_dram", a.shape, _mybir.dt.from_np(a.dtype), kind="ExternalInput").ap())
    for i, shape in enumerate(_OUTS):
        args.append(nc.dram_tensor(f"out_{i}_dram", shape, _mybir.dt.float32, kind="ExternalOutput").ap())
    build(nc, *args)
    r = _run(nc, [arrays], core_ids=[0])
    return tuple(r.results[0][f"out_{i}_dram"] for i in range(len(_OUTS)))
```

```python
from contextlib import ExitStack

import concourse.bass as bass
from concourse import mybir

F32 = mybir.dt.float32
F32R = mybir.dt.float32r
BF16 = mybir.dt.bfloat16
I32 = mybir.dt.int32
ALU = mybir.AluOpType
ACT = mybir.ActivationFunctionType
AX = mybir.AxisListType

P = 128
D = 1024
KB = D // P
TP, TS = 512, 8
T = TP + TS
HALF = T // 2
NTB = 5
KA, KC = 3, 31
E, EF = 16, 512
FB = EF // P
GROUPS, PER_GROUP = 4, 4
C = 96
PASSES = -(-T // C)
ALPHA = 2.0 ** 0.25
EPS = 1e-5

A_BG, A_CG, A_H, B_VAL, B_GATE, C_U, C_V, G_A, G_B, G_C = (D * i for i in range(10))

R_CONVB, R_CONVA, R_BIAS, R_NBG, R_NBB, R_VG, R_VB, R_L1G, R_L1B, R_STA = 0, 31, 34, 35, 36, 37, 38, 39, 40, 41
NROWS = R_STA + 2 * TS

N_S1 = 0
N_GA = N_S1 + 6 * KB
N_U = N_GA + 2 * KB
N_GC = N_U + KB
N_GB = N_GC + 2 * KB
N_WO = N_GB + 2 * KB
N_END = N_WO + KB

ROUNDS = [("rows", 1), ("xs", 0), ("sb0", 1), ("sb1", 0), ("ws0", 1), ("ws1", 0),
          ("meanV", 0), ("varV", 0), ("meanB", 1), ("varB", 0),
          ("vt0", 1), ("vt1", 0), ("vt2", 1), ("vt3", 0), ("tailB", 1), ("tailA", 0), ("tailV", 1),
          ("sp0", 0), ("sp1", 1), ("sp2", 0), ("sp3", 1),
          ("meanH", 0), ("varH", 1), ("logits", 0), ("ht0", 1), ("ht1", 0), ("ht2", 1), ("ht3", 0), ("ht4", 1),
          ("pos", 0)]
DONE = {name: i + 1 for i, (name, _) in enumerate(ROUNDS)}
TILE = dict(ROUNDS)
BEFORE = {name: next((n for n, t in reversed(ROUNDS[:i]) if t == tile), None) for i, (name, tile) in enumerate(ROUNDS)}


class Tally:

    def __init__(self, eng, sem, start=0):
        self.eng, self.sem, self.base, self.n, self.var = eng, sem, start, 0, None

    def inc(self, ins):
        ins.then_inc(self.sem, 1)
        self.n += 1

    def value(self, lag=0):
        now = self.base + self.n - lag
        return now if self.var is None else self.var + now

    def wait(self, lag=0):
        self.eng.wait_ge(self.sem, self.value(lag))

    def enter(self, i, per):
        self.outer, self.per, self.var, self.n0 = self.n, per, i * per, self.n

    def leave(self, count):
        assert self.n - self.n0 == self.per, (self.n - self.n0, self.per)
        self.var, self.n = None, self.n0 + self.per * count


def rep(ap, axis, n):
    v = ap.unsqueeze(axis)
    shape = list(v.shape)
    shape[axis] = n
    return v.to_broadcast(shape)


def build(nc, x_prompt, x_sample, state_conv_a, state_conv_b, w_in, conv_a_w, w_a_out, conv_b_w, conv_b_bias,
          norm_b_g, norm_b_b, w_b_out, v_norm_g, v_norm_b, w_spatial, b_spatial, w_c_out, w_o, ln1_g, ln1_b,
          router_w, router_b, expert_w_gate, expert_w_up, expert_w_down, ln2_g, ln2_b,
          y_prompt, y_sample, new_a_prompt, new_b_prompt, new_a_sample, new_b_sample, new_v_sample):
    h_rows = nc.dram_tensor("h_rows", (T, D), F32, kind="Internal").ap()
    y_rows = nc.dram_tensor("y_rows", (PASSES * E * C, D), F32, kind="Internal").ap()

    in_v = w_in[0].rearrange("(k p) n -> p k n", p=P)
    a_out_v = w_a_out[0].rearrange("(k p) n -> p k n", p=P)
    b_out_v = w_b_out[0].rearrange("(k p) n -> p k n", p=P)
    c_out_v = w_c_out[0].rearrange("(k p) n -> p k n", p=P)
    o_v = w_o[0].rearrange("(k p) n -> p k n", p=P)
    gate_v = expert_w_gate[0].rearrange("e (k p) f -> p (e k) f", p=P)
    up_v = expert_w_up[0].rearrange("e (k p) f -> p (e k) f", p=P)
    down_v = expert_w_down[0].rearrange("e (k p) n -> p (e k) n", p=P)

    with ExitStack() as ctx:
        U = KB * T * 4
        base = (nc.sbuf_base + 31) // 32 * 32
        at = {}
        cursor = [base]

        def region(name, size):
            at[name] = cursor[0]
            cursor[0] += (size + 31) // 32 * 32

        for name in ("P_HI", "P_LO", "CB", "Q_HI", "Q_LO", "X_HI", "X_LO", "V", "M"):
            region(name, U)
        region("RING", 6 * D * 4)

        def place(name, where, shape, dt=F32, plus=0):
            return nc.alloc_sbuf_tensor_at(name, shape, dt, offset=at[where] + plus)

        def sb(name, shape, dt=F32):
            size = 1
            for n in shape[1:]:
                size *= n
            region(name, size * (2 if dt == BF16 else 4))
            return place(name, name, shape, dt)

        def sem(name):
            return ctx.enter_context(nc.semaphore(name))

        p_hi, p_lo = place("p_hi", "P_HI", [P, KB, T], F32R), place("p_lo", "P_LO", [P, KB, T], F32R)
        q_hi, q_lo = place("q_hi", "Q_HI", [P, KB, T], F32R), place("q_lo", "Q_LO", [P, KB, T], F32R)
        x_hi, x_lo = place("x_hi", "X_HI", [P, KB, T], F32R), place("x_lo", "X_LO", [P, KB, T], F32R)
        cb = place("cb", "CB", [P, KB, T])
        v = place("v", "V", [P, KB, T])
        m = place("m", "M", [P, KB, T])
        sig_b = place("sig_b", "V", [P, KB, T])
        vt = place("vt", "Q_HI", [P, 4, D])
        sq = place("sq", "Q_LO", [P, KB, T])
        sq_h = place("sq_h", "RING", [P, KB, T])
        tails = place("tails", "Q_LO", [38, 3, D])
        raw = place("raw", "RING", [P, 2, KB, P])
        w_hi = place("w_hi", "RING", [P, 2, KB, P], F32R, plus=2 * D * 4)
        w_lo = place("w_lo", "RING", [P, 2, KB, P], F32R, plus=4 * D * 4)
        x_tok = place("x_tok", "V", [P, 4, D])
        rows = place("rows", "M", [NROWS, D])
        xs_tok = place("xs_tok", "M", [TS, D], plus=D * 4)
        sb_tok = place("sb_tok", "M", [120, 2, D], plus=2 * D * 4)
        ws_nat = place("ws_nat", "CB", [P, KB, P])
        sb_t = place("sb_t", "Q_LO", [P, KB, TS, KC - 1])
        WB = KB * EF * 4
        slot_at = ("P_HI", "Q_HI", "X_LO")
        w_gate = [place(f"w_gate{i}", r, [P, KB, EF]) for i, r in enumerate(slot_at)]
        w_up = [place(f"w_up{i}", r, [P, KB, EF], plus=WB) for i, r in enumerate(slot_at)]
        w_down = [place(f"w_down{i}", r, [P, FB, D], plus=2 * WB) for i, r in enumerate(slot_at)]
        h_tok = place("h_tok", "RING", [P, NTB, D])
        hs = place("hs", "RING", [C, D])
        y_out = place("y_out", "RING", [C, D], plus=D * 4)
        onehot = place("onehot", "RING", [P, NTB, C], BF16, plus=NTB * D * 4)
        y_a = place("y_a", "Q_HI", [P, 2, D])
        y_b = place("y_b", "Q_HI", [P, 2, D], plus=2 * D * 4)
        fin = place("fin", "Q_HI", [P, 2, D], plus=4 * D * 4)
        h_back = place("h_back", "X_LO", [P, NTB, D])
        ln2_rows = place("ln2_rows", "X_LO", [P, 2, D], plus=NTB * D * 4)

        ev = [sb(f"ev{i}", [P, T]) for i in range(5)]
        b_pad = sb("b_pad", [P, KC - 1 + T])
        a_pad = sb("a_pad", [P, KA - 1 + T])
        acc_b = sb("acc_b", [P, T])
        acc_a = sb("acc_a", [P, T])
        par = sb("par", [P, KB * NROWS])
        bs = sb("bs", [P, KB, P])
        w00 = sb("w00", [P, KB])
        ws_t = sb("ws_t", [P, KB, P])
        ident = sb("ident", [P, P])
        mean_w = sb("mean_w", [P, P])
        tail_b = sb("tail_b", [P, KB, 38])
        tail_a = sb("tail_a", [P, KB, 10])
        samp_b = sb("samp_b", [P, KB, TS])
        samp_a = sb("samp_a", [P, KB, TS])
        samp_t = sb("samp_t", [P, KB, TS])
        std = sb("std", [P, T])
        sums_b = acc_b
        sums = acc_a
        eps_t = sb("eps_t", [P, 1])
        rw = sb("rw", [P, KB, E])
        rb = sb("rb", [P, E])
        tri = sb("tri", [P, P], BF16)
        ones_b = sb("ones_b", [P, P], BF16)
        id_cols = sb("id_cols", [P, NTB, 2], BF16)
        probs, oh1, oh2, t1, t2, posm = (place(f"router{i}", "b_pad", [P, NTB, E], plus=i * NTB * E * 4) for i in range(6))
        e_off, c4 = sb("e_off", [P, NTB, E]), sb("c4", [P, NTB, E])
        mb = sb("mb", [P, NTB, E], BF16)
        g_m1, g_m2, g_t, g_best = (sb(f"g{i}", [P, NTB, GROUPS]) for i in range(4))
        s_max, s_sum, s_w1, s_w2, s_ps, s_t, s_slot = (sb(f"s{i}", [P, NTB]) for i in range(7))
        slot_a, slot_b = sb("slot_a", [P, NTB], I32), sb("slot_b", [P, NTB], I32)
        ids = sb("ids", [C, E], I32)
        count_i = sb("count_i", [P, 1], I32)
        hs_t = place("hs_t", "ev0", [P, KB, C])
        silu = place("silu", "ev2", [P, FB * C])
        u_t = place("u_t", "ev3", [P, FB, C])
        iota = ev[4][:, 0:C]
        lg = ev[3]
        stats = sb("stats", [P, 2, 2, 6])
        agg = sb("agg", [P, 2, 4])
        assert cursor[0] <= nc.sbuf_usable_end - 64, (cursor[0], nc.sbuf_usable_end)

        pr = [ctx.enter_context(nc.psum_tensor(f"pr{i}", [P, 2, 512], F32)) for i in range(2)]
        work = [ctx.enter_context(nc.psum_tensor(f"work{i}", [P, 2, 512], F32)) for i in range(2)]

        x_in, rows_in, states_in, spatial_in, late_in = (sem(n) for n in ("x_in", "rows_in", "states_in", "spatial_in", "late_in"))
        const_ready, spatial_masked, pool_chain = sem("const_ready"), sem("spatial_masked"), sem("pool_chain")
        x_turned, x_rounded, x_split = sem("x_turned"), sem("x_rounded"), sem("x_split")
        raw_in = [sem("raw_in0"), sem("raw_in1")]
        w_rounded = sem("w_rounded")
        w_split = sem("w_split")
        proj_done = sem("proj_done")
        evacuated = sem("evacuated")
        gated = sem("gated")
        round_done = sem("round_done")
        dve_chain = sem("dve_chain")
        setup_done = sem("setup_done")
        summed = sem("summed")
        h_centred, h_white, sq_h_ready = sem("h_centred"), sem("h_white"), sem("sq_h_ready")
        centred = sem("centred")
        std_ready = sem("std_ready")
        std_used = sem("std_used")
        v_ready = sem("v_ready")
        tails_ready = sem("tails_ready")
        tails_out = sem("tails_out")
        vt_ready = sem("vt_ready")
        tail_cols = sem("tail_cols")
        a_split, b_split, c_split, merged_split = sem("a_split"), sem("b_split"), sem("c_split"), sem("merged_split")
        conv_done = sem("conv_done")
        b_normed, b_sig = sem("b_normed"), sem("b_sig")
        spatial_read = sem("spatial_read")
        pos_read = sem("pos_read")
        h_ready = sem("h_ready")
        h_tok_ready = sem("h_tok_ready")
        h_stored = sem("h_stored")
        logits_ready, exp_ready = sem("logits_ready"), sem("exp_ready")
        mb_ready = sem("mb_ready")
        count_ready = sem("count_ready")
        states_out = sem("states_out")
        slots_ready = sem("slots_ready")
        back_in = sem("back_in")
        lg_turned, lg_ready = sem("lg_turned"), sem("lg_ready")
        loads_begun, gathers_begun = sem("loads_begun"), sem("gathers_begun")
        more_posm = sem("more_posm")
        y_in = [sem("y_in0"), sem("y_in1")]
        y_read = sem("y_read")
        var_ready, std2_ready, scale_ready, normed, fin_ready, fin_g = (sem(n) for n in ("var_ready", "std2_ready", "scale_ready", "normed", "fin_ready", "fin_g"))
        fin_out = [sem("fin_out0"), sem("fin_out1")]

        class Pass:

            def __init__(self, tag):
                self.onehot_ready, self.ids_mm, self.ids_ready = sem(tag + "onehot"), sem(tag + "ids_mm"), sem(tag + "ids_ready")
                self.gathered = sem(tag + "gathered")
                self.turned, self.hs_t_ready = sem(tag + "turned"), sem(tag + "hs_t")
                self.gate_in = [sem(tag + f"gate_in{i}") for i in range(3)]
                self.up_in = [sem(tag + f"up_in{i}") for i in range(3)]
                self.down_in = [sem(tag + f"down_in{i}") for i in range(3)]
                self.gate_done, self.up_done, self.down_done = sem(tag + "gate_done"), sem(tag + "up_done"), sem(tag + "down_done")
                self.silu_ready, self.u_ready, self.y_ready = sem(tag + "silu"), sem(tag + "u"), sem(tag + "y_ready")
                self.stored = sem(tag + "stored")

        first, further = Pass("first_"), Pass("more_")

        block = ctx.enter_context(nc.Block())

        READ = {"rows": (setup_done, 1), "xs": (x_split, KB + 1), "sb0": (setup_done, 2), "sb1": (setup_done, 3),
                "ws0": (setup_done, 4), "ws1": (setup_done, 5), "meanV": (centred, 1), "varV": (std_ready, 1),
                "meanB": (centred, 2), "varB": (std_ready, 2), "meanH": (h_centred, KB), "varH": (std_ready, 3),
                "tailB": (tails_ready, 1), "tailA": (tails_ready, 2), "tailV": (tails_ready, 3), "logits": (logits_ready, 1)}
        READ.update({f"vt{c}": (vt_ready, c + 1) for c in range(4)})
        READ.update({f"sp{q}": (spatial_read, q + 1) for q in range(4)})
        READ.update({f"ht{b}": (h_tok_ready, b + 1) for b in range(NTB)})

        def work_wait(eng, name):
            if BEFORE[name]:
                eng.wait_ge(*READ[BEFORE[name]])

        def further_passes(eng):
            eng.wait_ge(count_ready, 1)
            return eng.value_load(count_i[0:1, 0:1], min_val=0, max_val=T)

        @block.sync
        def _(sp):
            sp.dma_start(x_tok[:], x_prompt[0].rearrange("(b p) n -> p b n", p=P)).then_inc(x_in, 16)
            sp.dma_start(xs_tok[:], x_sample[:, 0, :]).then_inc(x_in, 16)

            def load(slot, n, view, col):
                sp.wait_ge(w_split, n * 2 + 2)
                sp.sem_inc(loads_begun, 1)
                sp.dma_start(raw[:, slot], view[:, :, bass.ds(col, P)]).then_inc(raw_in[slot], 16)

            with sp.Fori(0, KB) as j:
                for r, role in enumerate((B_GATE, B_VAL, C_V, A_CG, A_H, A_BG)):
                    load(r % 2, j * 6 + (N_S1 + r), in_v, j * P + role)

            def pairs(n0, gate, out_v):
                with sp.Fori(0, KB) as o:
                    load(0, o * 2 + n0, in_v, o * P + gate)
                    load(1, o * 2 + (n0 + 1), out_v, o * P)

            def singles(n0, view, col0):
                with sp.Fori(0, KB // 2) as i:
                    for s in range(2):
                        load(s, i * 2 + (n0 + s), view, i * 2 * P + (col0 + s * P))

            pairs(N_GA, G_A, a_out_v)
            singles(N_U, in_v, C_U)
            sp.dma_start(new_a_sample[0, :, 0:KA - 2, :], state_conv_a[0, :, 1:KA - 1, :]).then_inc(states_out, 16)
            sp.dma_start(new_b_sample[0, :, 0:KC - 2, :], state_conv_b[0, :, 1:KC - 1, :]).then_inc(states_out, 16)
            pairs(N_GC, G_C, c_out_v)
            pairs(N_GB, G_B, b_out_v)
            singles(N_WO, o_v, 0)

            def expert_load(ps, s, e, which):
                dst, src, k, sems = {"gate": (w_gate, gate_v, KB, ps.gate_in), "up": (w_up, up_v, KB, ps.up_in),
                                     "down": (w_down, down_v, FB, ps.down_in)}[which]
                sp.dma_start(dst[s][:], src[:, bass.ds(e * k, k), :]).then_inc(sems[s], 16)

            MATRICES = ("gate", "up", "down")

            def store(ps, e, t, row0):
                sp.wait_ge(ps.y_ready, t + 2)
                sp.dma_start(y_rows[bass.ds(e * C + row0, C), :], y_out[:]).then_inc(ps.stored, 16)

            def reload(ps, s, e, t):
                for which, done in zip(MATRICES, (ps.gate_done, ps.up_done, ps.down_done)):
                    sp.wait_ge(done, t + 1)
                    expert_load(ps, s, e + 3, which)

            def expert_pass(ps, row0, n0):
                with sp.Fori(0, 4) as i:
                    for s in range(3):
                        e = i * 3 + s
                        reload(ps, s, e, e + n0)
                        store(ps, e, e + n0, row0)
                reload(ps, 0, 12, n0 + 12)
                for e in range(12, E - 1):
                    store(ps, e, n0 + e, row0)

            def h_out():
                for b in range(NTB):
                    n = P if b < 4 else TS
                    sp.wait_ge(h_tok_ready, b + 1)
                    sp.dma_start(h_rows[b * P:b * P + n, :], h_tok[0:n, b, :]).then_inc(h_stored, 16)

            sp.wait_ge(proj_done, 2 + N_WO)
            for which in MATRICES:
                expert_load(first, 0, 0, which)
            sp.wait_ge(proj_done, 2 + N_END)
            sp.wait_ge(gated, 28 + 3 * KB + KB - 1)
            for which in MATRICES:
                expert_load(first, 1, 1, which)
            h_out()
            for which in MATRICES:
                expert_load(first, 2, 2, which)
            sp.sem_inc(first.stored, 16)
            expert_pass(first, 0, 0)

            def load_back():
                sp.dma_start(h_back[:, 0:4, :], h_rows[0:TP, :].rearrange("(b p) n -> p b n", p=P)).then_inc(back_in, 16)
                sp.dma_start(h_back[0:TS, 4, :], h_rows[TP:T, :]).then_inc(back_in, 16)
                sp.dma_start(ln2_rows[:, 0, :], ln2_g[0].partition_broadcast(P)).then_inc(back_in, 16)
                sp.dma_start(ln2_rows[:, 1, :], ln2_b[0].partition_broadcast(P)).then_inc(back_in, 16)

            n_max = further_passes(sp)
            with sp.If(n_max > C):
                store(first, E - 1, E - 1, 0)
                sp.wait_ge(first.stored, 16 * (E + 1))
                sp.sem_inc(further.stored, 16)
                with sp.Fori(0, PASSES - 1) as q:
                    for s in range(3):
                        for which in MATRICES:
                            expert_load(further, s, s, which)
                    expert_pass(further, q * (E * C) + E * C, q * E)
                    store(further, E - 1, q * E + (E - 1), q * (E * C) + E * C)
                sp.wait_ge(further.stored, 16 * (E * (PASSES - 1) + 1))
                load_back()
            with sp.Else():
                load_back()
                store(first, E - 1, E - 1, 0)
                sp.wait_ge(first.stored, 16 * (E + 1))
                sp.nop()
            sp.sem_inc(y_read, 1)
            for b in range(NTB):
                n = P if b < 4 else TS
                sp.wait_ge(fin_ready, b + 1)
                dst = y_prompt[0, b * P:(b + 1) * P, :] if b < 4 else y_sample[:, 0, :]
                sp.dma_start(dst, fin[0:n, b % 2, :]).then_inc(fin_out[b % 2], 16)
            sp.wait_ge(fin_out[0], 48)
            sp.wait_ge(fin_out[1], 32)
            sp.wait_ge(tails_out, 80)
            sp.wait_ge(states_out, 32)

        @block.gpsimd
        def _(pool):
            chain = Tally(pool, pool_chain)
            pool.sem_inc(w_split, 4)
            chain.inc(pool.memset(ident[:], 0.0))
            chain.wait()
            pool.affine_select(out=ident[:], in_=ident[:], compare_op=ALU.not_equal, fill=1.0, base=0,
                               pattern=[[-1, P]], channel_multiplier=1).then_inc(const_ready, 1)
            pool.memset(mean_w[:], 1.0 / D)
            pool.memset(eps_t[:], EPS).then_inc(const_ready, 1)
            pool.wait_ge(spatial_in, 48)
            pool.affine_select(out=ws_nat[:], in_=ws_nat[:], compare_op=ALU.is_ge, fill=0.0, base=0,
                               pattern=[[0, KB], [-1, P]], channel_multiplier=1).then_inc(spatial_masked, 1)

            def lower(slot, n):
                for h in range(2):
                    k = slice(h * KB // 2, (h + 1) * KB // 2)
                    pool.wait_ge(w_rounded, n * 2 + (h + 1))
                    pool.tensor_tensor(w_lo[:, slot, k], raw[:, slot, k], w_hi[:, slot, k].bitcast(F32), ALU.subtract).then_inc(w_split, 1)

            with pool.Fori(0, N_GA // 6) as j:
                for r in range(6):
                    lower(r % 2, j * 6 + r)
            chain.inc(pool.memset(tri[:], 1.0))
            pool.memset(ones_b[:], 1.0)
            chain.wait()
            pool.affine_select(out=tri[:], in_=tri[:], compare_op=ALU.is_ge, fill=0.0, base=-1,
                               pattern=[[1, P]], channel_multiplier=-1)
            pool.iota(id_cols[:, :, 0], pattern=[[P, NTB]], base=0, channel_multiplier=0, allow_small_or_imprecise_dtypes=True)
            pool.iota(id_cols[:, :, 1], pattern=[[0, NTB]], base=0, channel_multiplier=1, allow_small_or_imprecise_dtypes=True)
            pool.iota(e_off[:], pattern=[[0, NTB], [C, E]], base=0, channel_multiplier=0, allow_small_or_imprecise_dtypes=True)
            pool.iota(c4[:].rearrange("p b (g i) -> p (b g) i", i=PER_GROUP), pattern=[[0, NTB * GROUPS], [-1, PER_GROUP]],
                      base=PER_GROUP, channel_multiplier=0, allow_small_or_imprecise_dtypes=True).then_inc(const_ready, 1)
            with pool.Fori(0, (N_END - N_GA) // 2) as j:
                for s in range(2):
                    lower(s, j * 2 + (N_GA + s))
            pool.wait_ge(gated, 28 + 4 * KB + KB - 1)
            pool.iota(iota, pattern=[[1, C]], base=0, channel_multiplier=0,
                      allow_small_or_imprecise_dtypes=True).then_inc(const_ready, 1)

            def gathers(ps, n0):
                for e in range(E):
                    t = e + n0
                    pool.wait_ge(ps.ids_ready, t + 2)
                    pool.wait_ge(ps.turned, t + 1)
                    pool.sem_inc(gathers_begun, 1)
                    pool.indirect_dma_start(out=hs[:], out_offset=None, in_=h_rows,
                                            in_offset=bass.IndirectOffsetOnAxis(ap=ids[:, e:e + 1], axis=0)).then_inc(ps.gathered, 16)

            pool.wait_ge(h_stored, 16 * NTB)
            gathers(first, 0)

            def finish(table):
                pool.wait_ge(y_read, 1)
                pool.wait_ge(slots_ready, 2)

                def fetch(b):
                    n = P if b < 4 else TS
                    for dst, slot in ((y_a, slot_a), (y_b, slot_b)):
                        pool.indirect_dma_start(out=dst[0:n, b % 2, :], out_offset=None, in_=table,
                                                in_offset=bass.IndirectOffsetOnAxis(ap=slot[0:n, b:b + 1], axis=0)).then_inc(y_in[b % 2], 16)

                fetch(0)
                fetch(1)
                for b in range(NTB):
                    n = P if b < 4 else TS
                    pool.wait_ge(normed, b + 1)
                    pool.tensor_tensor(fin[0:n, b % 2, :], fin[0:n, b % 2, :], ln2_rows[0:n, 0, :], ALU.mult).then_inc(fin_g, 1)
                    if b + 2 < NTB:
                        fetch(b + 2)

            n_max = further_passes(pool)
            with pool.If(n_max > C):
                pool.wait_ge(first.turned, 1 + E)
                with pool.Fori(0, PASSES - 1) as q:
                    gathers(further, q * E)
                finish(y_rows)
            with pool.Else():
                finish(y_rows[0:E * C, :])

        @block.scalar
        def _(act):
            act.sem_inc(evacuated, 2)
            for view, r, k in ((conv_b_w[0], R_CONVB, KC), (conv_a_w[0], R_CONVA, KA), (conv_b_bias, R_BIAS, 1), (norm_b_g, R_NBG, 1),
                               (norm_b_b, R_NBB, 1), (v_norm_g, R_VG, 1), (v_norm_b, R_VB, 1), (ln1_g, R_L1G, 1), (ln1_b, R_L1B, 1),
                               (state_conv_a[0].rearrange("s k n -> (s k) n"), R_STA, 2 * TS)):
                act.dma_start(rows[r:r + k, :], view).then_inc(rows_in, 16)
            act.dma_start(sb_tok[:], state_conv_b[0].rearrange("(b s) k n -> (s k) b n", b=2)).then_inc(states_in, 16)
            act.dma_start(ws_nat[:], w_spatial[0].rearrange("g t s -> t g s")).then_inc(spatial_in, 16)
            act.dma_start(bs[:], b_spatial[0].partition_broadcast(P)).then_inc(spatial_in, 16)
            with nc.allow_non_contiguous_dma(reason="one weight per group"):
                act.dma_start(w00[:].unsqueeze(2), w_spatial[0, :, 0, 0:1].partition_broadcast(P)).then_inc(spatial_in, 16)
            act.dma_start(rw[:], router_w.rearrange("(k p) e -> p k e", p=P)).then_inc(late_in, 16)
            act.dma_start(rb[:], router_b.partition_broadcast(P)).then_inc(late_in, 16)

            def round_w(slot, use, n):
                act.wait_ge(raw_in[slot], use * 16 + 16)
                act.wait_ge(proj_done, n + 1)
                for h in range(2):
                    k = slice(h * KB // 2, (h + 1) * KB // 2)
                    act.activation(w_hi[:, slot, k], raw[:, slot, k], ACT.Copy).then_inc(w_rounded, 1)

            def evacuate(n, src, out, func=ACT.Copy):
                act.wait_ge(proj_done, n + 3)
                act.activation(out, src[:, :, 0:HALF], func).then_inc(evacuated, 1)

            def halves(ap):
                return ap.rearrange("p (h t) -> p h t", h=2)

            for j in range(KB):
                act.wait_ge(x_turned, j + 1)
                act.activation(x_hi[:, j, 0:TP], pr[j // 2 % 2][:, j % 2, :], ACT.Copy).then_inc(x_rounded, 1)
            act.wait_ge(round_done, DONE["xs"])
            act.activation(x_hi[:, :, TP:T], work[TILE["xs"]][:, 0, 0:KB * TS].rearrange("p (k s) -> p k s", s=TS),
                           ACT.Copy).then_inc(x_rounded, 1)
            round_w(0, 0, 0)

            def next_w(s, use, n):
                round_w(1 - s, use if s == 0 else use + 1, n + 1)

            with act.Fori(0, KB) as j:
                for r, (out, func, g) in enumerate(((halves(ev[0][:]), ACT.Sigmoid, 1), (halves(ev[1][:]), ACT.Copy, 1),
                                                    (None, ACT.Copy, 0), (halves(ev[2][:]), ACT.Copy, 2),
                                                    (halves(ev[3][:]), ACT.Copy, 2), (halves(ev[4][:]), ACT.Copy, 3))):
                    n = j * 6 + r
                    next_w(r % 2, j * 3 + r // 2, n)
                    if out is None:
                        out = v[:, bass.ds(j, 1), :].rearrange("p o (h t) -> p (o h) t", h=2)
                    else:
                        act.wait_ge(gated, j * 3 + g)
                    evacuate(n, pr[r % 2], out, func)

            def gate_pairs(n0, m0, count, with_b=False):
                with act.Fori(0, count // 2) as i:
                    for b in range(2):
                        mm = i * 2 + (m0 + b)
                        for s in range(2):
                            n = i * 4 + (n0 + 2 * b + s)
                            next_w(s, i * 2 + (n0 // 2 + b), n)
                            if s == 0:
                                act.wait_ge(gated, mm + 26)
                            evacuate(n, pr[s], halves(ev[2 * b + s][:]), ACT.Copy if s else ACT.Sigmoid)
                        if with_b:
                            act.wait_ge(b_normed, i * 2 + (b + 1))
                            act.activation(sig_b[:, bass.ds(i * 2 + b, 1), :], cb[:, bass.ds(i * 2 + b, 1), :], ACT.Sigmoid).then_inc(b_sig, 1)

            def singles(n0, m0, count, last=False):
                with act.Fori(0, count // 2 - (1 if last else 0)) as i:
                    for s in range(2):
                        n = i * 2 + (n0 + s)
                        next_w(s, i + n0 // 2, n)
                        act.wait_ge(gated, i * 2 + (m0 + s + 26))
                        evacuate(n, pr[s], halves(ev[2 * s][:]))
                if last:
                    for s in range(2):
                        n = n0 + count - 2 + s
                        if s == 0:
                            next_w(s, n // 2, n)
                        act.wait_ge(gated, m0 + count - 2 + s + 26)
                        evacuate(n, pr[s], halves(ev[2 * s][:]))

            def root(name, k):
                act.wait_ge(round_done, DONE[name])
                if k:
                    act.wait_ge(std_used, k)
                act.activation(halves(std[:]), work[TILE[name]][:, :, 0:HALF], ACT.Sqrt, bias=eps_t[:]).then_inc(std_ready, 1)

            gate_pairs(N_GA, 0, 4)
            gate_pairs(N_GA + 8, 4, 2)
            root("varV", 0)
            gate_pairs(N_GA + 12, 6, 2)
            root("varB", 1)
            for c in range(4):
                act.wait_ge(round_done, DONE[f"vt{c}"])
                act.activation(vt[:, c, :].rearrange("p (h t) -> p h t", h=2), work[TILE[f"vt{c}"]][:], ACT.Copy).then_inc(vt_ready, 1)
            for i, (name, k) in enumerate((("tailB", 38), ("tailA", 10), ("tailV", 8))):
                act.wait_ge(round_done, DONE[name])
                act.activation(tails[0:k, i, :].rearrange("p (h t) -> p h t", h=2), work[TILE[name]][0:k], ACT.Copy).then_inc(tails_ready, 1)
            act.wait_ge(tails_ready, 3)
            act.dma_start(new_b_prompt[0, 0], tails[0:30, 0, :]).then_inc(tails_out, 16)
            act.dma_start(new_b_sample[0, :, KC - 2, :], tails[30:38, 0, :]).then_inc(tails_out, 16)
            act.dma_start(new_a_prompt[0, 0], tails[0:2, 1, :]).then_inc(tails_out, 16)
            act.dma_start(new_a_sample[0, :, KA - 2, :], tails[2:10, 1, :]).then_inc(tails_out, 16)
            act.dma_start(new_v_sample[0, :, 0, :], tails[0:8, 2, :]).then_inc(tails_out, 16)
            singles(N_U, 8, 8)
            gate_pairs(N_GC, 16, 8, with_b=True)
            gate_pairs(N_GB, 24, 8)
            singles(N_WO, 32, 8, last=True)
            for k in range(KB):
                act.wait_ge(h_centred, k + 1)
                act.activation(sq_h[:, k, :], m[:, k, :], ACT.Square).then_inc(sq_h_ready, 1)
            root("varH", 2)
            for k in range(KB):
                act.wait_ge(h_white, k + 1)
                act.activation(m[:, k, :], m[:, k, :], ACT.Identity, scale=par[:, k * NROWS + R_L1G:k * NROWS + R_L1G + 1],
                               bias=par[:, k * NROWS + R_L1B:k * NROWS + R_L1B + 1]).then_inc(h_ready, 1)
            act.wait_ge(lg_turned, 1)
            act.activation(lg[0:E, :].rearrange("p (h t) -> p h t", h=2), work[TILE["logits"]][0:E, :, 0:HALF], ACT.Copy).then_inc(lg_ready, 1)
            act.wait_ge(logits_ready, 1)
            act.activation(probs[:], probs[:], ACT.Exp).then_inc(exp_ready, 1)
            for b in range(NTB):
                n = P if b < 4 else TS
                act.wait_ge(round_done, DONE[f"ht{b}"])
                act.activation(h_tok[0:n, b, :].rearrange("p (h t) -> p h t", h=2), work[TILE[f"ht{b}"]][0:n], ACT.Copy).then_inc(h_tok_ready, 1)
            def turn_in(ps, t):
                act.wait_ge(ps.turned, t + 2)
                act.activation(hs_t[:].rearrange("p (h k) t -> p h (k t)", h=2), work[0][:, :, 0:KB // 2 * C], ACT.Copy).then_inc(ps.hs_t_ready, 1)

            def expert(ps, t, ahead):
                act.wait_ge(ps.gate_done, t + 1)
                act.activation(silu[:], pr[0][:, 0, 0:FB * C], ACT.Silu).then_inc(ps.silu_ready, 1)
                if ahead:
                    turn_in(ps, t + 1)
                act.wait_ge(ps.down_done, t + 1)
                act.wait_ge(ps.stored, t * 16 + 16)
                act.activation(y_out[:].rearrange("p (h n) -> p h n", h=2), work[1][0:C], ACT.Copy).then_inc(ps.y_ready, 1)

            def expert_pass(ps, n0):
                turn_in(ps, n0)
                with act.Fori(0, 5) as i:
                    for s in range(3):
                        expert(ps, i * 3 + s + n0, True)
                expert(ps, n0 + E - 1, False)

            act.sem_inc(first.hs_t_ready, 1)
            act.sem_inc(first.y_ready, 1)
            act.wait_ge(mb_ready, 1)
            expert_pass(first, 0)
            n_max = further_passes(act)
            with act.If(n_max > C):
                act.sem_inc(further.hs_t_ready, 1)
                act.sem_inc(further.y_ready, 1)
                with act.Fori(0, PASSES - 1) as q:
                    expert_pass(further, q * E)
                act.nop()
            with act.Else():
                act.nop()
            for b in range(NTB):
                n = P if b < 4 else TS
                s = b % 2
                act.wait_ge(var_ready, b + 1)
                act.activation(agg[0:n, s, 2:3], agg[0:n, s, 1:2], ACT.Sqrt, bias=eps_t[0:n]).then_inc(std2_ready, 1)
                act.wait_ge(scale_ready, b + 1)
                if b >= 2:
                    act.wait_ge(fin_out[s], 16 * (b // 2))
                act.activation(fin[0:n, s, :], y_a[0:n, s, :], ACT.Identity, scale=agg[0:n, s, 2:3],
                               bias=agg[0:n, s, 3:4]).then_inc(normed, 1)

        @block.tensor
        def _(pe):
            pe.sem_inc(proj_done, 2)
            pe.wait_ge(const_ready, 1)
            pe.wait_ge(x_in, 32)
            for j in range(KB):
                if j >= 4:
                    pe.wait_ge(x_split, j - 3)
                for b in range(4):
                    mm = pe.transpose(pr[j // 2 % 2][:, j % 2, b * P:(b + 1) * P], x_tok[:, b, j * P:(j + 1) * P], ident[:])
                mm.then_inc(x_turned, 1)
            pe.wait_ge(rows_in, 160)
            for k in range(KB):
                mm = pe.transpose(work[1][:, 0, k * NROWS:(k + 1) * NROWS], rows[:, k * P:(k + 1) * P], ident[0:NROWS, 0:NROWS])
            mm.then_inc(round_done, 1)
            for k in range(KB):
                mm = pe.transpose(work[0][:, 0, k * TS:(k + 1) * TS], xs_tok[:, k * P:(k + 1) * P], ident[0:TS, 0:TS])
            mm.then_inc(round_done, 1)
            pe.wait_ge(states_in, 16)
            for i in range(2):
                work_wait(pe, f"sb{i}")
                for k in range(4 * i, 4 * i + 4):
                    for b in range(2):
                        q = (k - 4 * i)
                        mm = pe.transpose(work[TILE[f"sb{i}"]][:, q // 2, q % 2 * 240 + b * 120:q % 2 * 240 + b * 120 + 120],
                                          sb_tok[:, b, k * P:(k + 1) * P], ident[0:120, 0:120])
                mm.then_inc(round_done, 1)
            pe.wait_ge(spatial_masked, 1)
            for i in range(2):
                work_wait(pe, f"ws{i}")
                for g in range(4):
                    mm = pe.transpose(work[TILE[f"ws{i}"]][:, 0, g * P:(g + 1) * P], ws_nat[:, 4 * i + g, :], ident[:])
                mm.then_inc(round_done, 1)
            pe.wait_ge(x_split, KB + 1)

            def project(slot, n, hi, lo):
                pe.wait_ge(evacuated, n + 1)
                for k in range(KB):
                    if k % (KB // 2) == 0:
                        pe.wait_ge(w_split, n * 2 + (5 + k // (KB // 2)))
                    for w, x in ((w_hi, hi), (w_hi, lo), (w_lo, hi)):
                        for h in range(2):
                            mm = pe.matmul(pr[slot][:, h, 0:HALF], w[:, slot, k, :], x[:, k, h * HALF:(h + 1) * HALF],
                                           start=(k == 0 and w is w_hi and x is hi), stop=(k == KB - 1 and w is w_lo))
                mm.then_inc(proj_done, 1)

            def mean(name, z):
                work_wait(pe, name)
                for h in range(2):
                    mm = pe.matmul(work[TILE[name]][:, h, 0:HALF], mean_w[:], z[:, h * HALF:(h + 1) * HALF], start=True, stop=True)
                mm.then_inc(round_done, 1)

            with pe.Fori(0, KB) as j:
                for r in range(6):
                    project(r % 2, j * 6 + r, x_hi, x_lo)

            def pairs(n0, count, hi, lo, ready):
                with pe.Fori(0, count) as o:
                    project(0, o * 2 + n0, x_hi, x_lo)
                    pe.wait_ge(ready, KB)
                    project(1, o * 2 + (n0 + 1), hi, lo)

            def singles(n0, hi, lo):
                with pe.Fori(0, KB // 2) as i:
                    for s in range(2):
                        project(s, i * 2 + (n0 + s), hi, lo)

            pairs(N_GA, 3, p_hi, p_lo, a_split)
            pe.wait_ge(const_ready, 2)
            pe.wait_ge(summed, 1)
            mean("meanV", sums)
            pairs(N_GA + 6, 2, p_hi, p_lo, a_split)
            pe.wait_ge(summed, 2)
            mean("varV", sums)
            pe.wait_ge(summed, 3)
            mean("meanB", sums_b)
            pairs(N_GA + 10, 3, p_hi, p_lo, a_split)
            pe.wait_ge(summed, 4)
            mean("varB", sums)
            pe.wait_ge(v_ready, KB)
            for c in range(4):
                work_wait(pe, f"vt{c}")
                for g in range(KB):
                    mm = pe.transpose(work[TILE[f"vt{c}"]][:, g // 4, g % 4 * P:(g % 4 + 1) * P], v[:, g, c * P:(c + 1) * P], ident[:])
                mm.then_inc(round_done, 1)
            for name, src in (("tailB", tail_b[:]), ("tailA", tail_a[:]), ("tailV", v[:, :, TP:T])):
                work_wait(pe, name)
                k = src.shape[2]
                for g in range(KB):
                    mm = pe.transpose(work[TILE[name]][0:k, g // 4, g % 4 * P:(g % 4 + 1) * P], src[:, g, :], ident[:])
                mm.then_inc(round_done, 1)
            pe.wait_ge(vt_ready, 4)
            for q in range(4):
                work_wait(pe, f"sp{q}")
                for i in range(2):
                    g = 2 * q + i
                    for c in range(4):
                        mm = pe.matmul(work[TILE[f"sp{q}"]][:, i, c * P:(c + 1) * P], vt[:, c, g * P:(g + 1) * P], ws_t[:, g, :],
                                       start=True, stop=True)
                mm.then_inc(round_done, 1)
            singles(N_U, x_hi, x_lo)
            pairs(N_GC, KB, q_hi, q_lo, c_split)
            pairs(N_GB, KB, p_hi, p_lo, b_split)
            pe.wait_ge(merged_split, KB)
            singles(N_WO, q_hi, q_lo)
            pe.wait_ge(summed, 5)
            mean("meanH", sums)
            work_wait(pe, "varH")
            for k in range(KB):
                pe.wait_ge(sq_h_ready, k + 1)
                for h in range(2):
                    mm = pe.matmul(work[TILE["varH"]][:, h, 0:HALF], mean_w[:], sq_h[:, k, h * HALF:(h + 1) * HALF],
                                   start=(k == 0), stop=(k == KB - 1))
            mm.then_inc(round_done, 1)
            pe.wait_ge(late_in, 32)
            work_wait(pe, "logits")
            for k in range(KB):
                pe.wait_ge(h_ready, k + 1)
                for h in range(2):
                    mm = pe.matmul(work[TILE["logits"]][0:E, h, 0:HALF], rw[:, k, :], m[:, k, h * HALF:(h + 1) * HALF],
                                   start=(k == 0), stop=(k == KB - 1))
            mm.then_inc(lg_turned, 1)
            pe.wait_ge(lg_ready, 1)
            for b in range(NTB):
                n = P if b < 4 else TS
                mm = pe.transpose(work[TILE["logits"]][0:n, 0, b * E:(b + 1) * E], lg[0:E, b * P:b * P + n], ident[0:E, 0:E])
            mm.then_inc(round_done, 1)
            for b in range(NTB):
                n = P if b < 4 else TS
                work_wait(pe, f"ht{b}")
                for k in range(KB):
                    mm = pe.transpose(work[TILE[f"ht{b}"]][0:n, k // 4, k % 4 * P:(k % 4 + 1) * P], m[:, k, b * P:b * P + n], ident[:])
                mm.then_inc(round_done, 1)
            pe.wait_ge(mb_ready, 1)
            pe.wait_ge(const_ready, 3)
            work_wait(pe, "pos")
            for b in range(NTB):
                mm = pe.matmul(work[0][:, 0, b * E:(b + 1) * E], tri[:], mb[:, b, :], start=True, stop=(b == 0))
                for c in range(b):
                    mm = pe.matmul(work[0][:, 0, b * E:(b + 1) * E], ones_b[:], mb[:, c, :], start=False, stop=(c == b - 1))
            for b in range(NTB):
                mm = pe.matmul(work[0][:, 0, NTB * E:(NTB + 1) * E], ones_b[:], mb[:, b, :], start=(b == 0), stop=(b == NTB - 1))
            mm.then_inc(round_done, 1)

            def find_ids(ps, t):
                pe.wait_ge(ps.onehot_ready, t + 1)
                pe.wait_ge(ps.ids_ready, t + 1)
                for b in range(NTB):
                    mm = pe.matmul(pr[1][0:C, 0, 0:2], onehot[:, b, :], id_cols[:, b, :], start=(b == 0), stop=(b == NTB - 1))
                mm.then_inc(ps.ids_mm, 1)

            def turn(ps, t):
                pe.wait_ge(ps.gathered, t * 16 + 16)
                for k in range(KB):
                    mm = pe.transpose(work[0][:, k // 4, k % 4 * C:(k % 4 + 1) * C], hs[:, k * P:(k + 1) * P], ident[0:C, 0:C])
                mm.then_inc(ps.turned, 1)

            def expert(ps, s, t, use, ahead):
                if ahead:
                    find_ids(ps, t + 1)
                pe.wait_ge(ps.hs_t_ready, t + 2)
                for h, (w, landed, done) in enumerate(((w_gate, ps.gate_in, ps.gate_done), (w_up, ps.up_in, ps.up_done))):
                    pe.wait_ge(landed[s], use * 16 + 16)
                    for f in range(FB):
                        for k in range(KB):
                            mm = pe.matmul(pr[0][:, h, f * C:(f + 1) * C], w[s][:, k, f * P:(f + 1) * P], hs_t[:, k, :],
                                           start=(k == 0), stop=(k == KB - 1))
                    mm.then_inc(done, 1)
                if ahead:
                    turn(ps, t + 1)
                pe.wait_ge(ps.down_in[s], use * 16 + 16)
                pe.wait_ge(ps.u_ready, t + 1)
                pe.wait_ge(ps.y_ready, t + 1)
                for f in range(FB):
                    for h in range(2):
                        mm = pe.matmul(work[1][0:C, h, :], u_t[:, f, :], w_down[s][:, f, h * 512:(h + 1) * 512],
                                       start=(f == 0), stop=(f == FB - 1))
                mm.then_inc(ps.down_done, 1)

            def expert_pass(ps, n0, uses):
                find_ids(ps, n0)
                turn(ps, n0)
                for s in range(3):
                    expert(ps, s, n0 + s, uses[s], True)
                with pe.Fori(1, 5) as i:
                    for s in range(3):
                        expert(ps, s, i * 3 + s + n0, i + uses[s], True)
                expert(ps, 0, n0 + E - 1, uses[0] + 5, False)

            pe.sem_inc(first.turned, 1)
            pe.wait_ge(h_tok_ready, NTB)
            expert_pass(first, 0, (0, 0, 0))
            n_max = further_passes(pe)
            with pe.If(n_max > C):
                pe.sem_inc(further.turned, 1)
                pe.wait_ge(first.y_ready, E + 1)
                with pe.Fori(0, PASSES - 1) as q:
                    expert_pass(further, q * E, (q * 6, q * 5, q * 5))
                    pe.wait_ge(further.y_ready, q * E + (E + 1))
                    pe.nop()
                pe.nop()
            with pe.Else():
                pe.nop()

        @block.vector
        def _(dve):
            chain = Tally(dve, dve_chain)
            last = [chain]

            def do(ins, tally=chain):
                tally.inc(ins)
                last[0] = tally

            def settle():
                last[0].wait()

            gates = Tally(dve, gated, 3)
            dve.sem_inc(gated, 3)
            tallies = {s: Tally(dve, s) for s in (setup_done, x_split, tail_cols, a_split, b_split, c_split, merged_split, conv_done,
                                                  b_normed, centred, summed, h_centred, h_white, std_used, v_ready, spatial_read)}

            def to(s):
                return tallies[s]

            to_logits, to_mb, to_count, to_slots = (Tally(dve, s) for s in (logits_ready, mb_ready, count_ready, slots_ready))
            to_var, to_scale, to_fin = (Tally(dve, s) for s in (var_ready, scale_ready, fin_ready))

            def col(k, r):
                return par[:, bass.ds(k * NROWS + r, 1)]

            def blk(t, k, a=0, b=T):
                return t[:, bass.ds(k, 1), a:b].rearrange("p o t -> p (o t)")

            do(dve.memset(b_pad[:, 0:KC - 1], 0.0))
            do(dve.memset(a_pad[:, 0:KA - 1], 0.0))
            do(dve.memset(mb[:], 0.0))
            for j in range(KB):
                dve.wait_ge(x_rounded, j + 1)
                do(dve.tensor_tensor(x_lo[:, j, 0:TP], pr[j // 2 % 2][:, j % 2, :], x_hi[:, j, 0:TP].bitcast(F32), ALU.subtract), to(x_split))
            dve.wait_ge(x_rounded, KB + 1)
            do(dve.tensor_tensor(x_lo[:, :, TP:T], work[0][:, 0, 0:KB * TS].rearrange("p (k s) -> p k s", s=TS),
                                 x_hi[:, :, TP:T].bitcast(F32), ALU.subtract), to(x_split))
            dve.wait_ge(round_done, DONE["rows"])
            do(dve.tensor_copy(par[:], work[1][:, 0, 0:KB * NROWS]), to(setup_done))
            for i in range(2):
                dve.wait_ge(round_done, DONE[f"sb{i}"])
                for q in range(2):
                    do(dve.tensor_copy(sb_t[:, 4 * i + 2 * q:4 * i + 2 * q + 2].rearrange("p k s c -> p (k s c)"),
                                       work[TILE[f"sb{i}"]][:, q, 0:480]), chain if q == 0 else to(setup_done))
            for i in range(2):
                dve.wait_ge(round_done, DONE[f"ws{i}"])
                do(dve.tensor_copy(ws_t[:, 4 * i:4 * i + 4].rearrange("p g t -> p (g t)"), work[TILE[f"ws{i}"]][:, 0, :]), to(setup_done))
            settle()
            par_k = par[:].rearrange("p (k r) -> p k r", r=NROWS)
            state_a = par_k[:, :, R_STA:R_STA + 2 * TS].rearrange("p k (s c) -> p k s c", c=2)
            do(dve.tensor_tensor(sb_t[:], sb_t[:], rep(par_k[:, :, R_CONVB:R_CONVB + KC - 1], 2, TS), ALU.mult))
            do(dve.tensor_tensor(samp_a[:], state_a[:, :, :, 0], par_k[:, :, R_CONVA:R_CONVA + 1].to_broadcast([P, KB, TS]), ALU.mult))
            do(dve.tensor_tensor(samp_t[:], state_a[:, :, :, 1], par_k[:, :, R_CONVA + 1:R_CONVA + 2].to_broadcast([P, KB, TS]), ALU.mult))
            settle()
            do(dve.tensor_tensor(samp_a[:], samp_a[:], samp_t[:], ALU.add))
            do(dve.tensor_reduce(samp_b[:], sb_t[:], AX.X, ALU.add))
            settle()
            do(dve.tensor_tensor(samp_b[:], samp_b[:], par_k[:, :, R_BIAS:R_BIAS + 1].to_broadcast([P, KB, TS]), ALU.add))

            def branches(j):
                dve.wait_ge(evacuated, j * 6 + (1 + 3))
                settle()
                do(dve.tensor_tensor(b_pad[:, KC - 1:KC - 1 + T], ev[0][:], ev[1][:], ALU.mult), gates)
                dve.wait_ge(evacuated, j * 6 + (4 + 3))
                do(dve.tensor_tensor(a_pad[:, KA - 1:KA - 1 + T], ev[2][:], ev[3][:], ALU.mult), gates)
                gates.wait(1)
                do(dve.tensor_copy(blk(tail_b, j, 0, 38), b_pad[:, TP:TP + 38]))
                gates.wait()
                do(dve.tensor_copy(blk(tail_a, j, 0, 10), a_pad[:, TP:TP + 10]))
                do(dve.tensor_scalar(acc_a[:, 0:TP], a_pad[:, 0:TP], col(j, R_CONVA), None, ALU.mult))
                do(dve.scalar_tensor_tensor(acc_a[:, TP:T], a_pad[:, KA - 1 + TP:], col(j, R_CONVA + 2), blk(samp_a, j, 0, TS), ALU.mult, ALU.add))
                for k in (1, 2):
                    settle()
                    do(dve.scalar_tensor_tensor(acc_a[:, 0:TP], a_pad[:, k:k + TP], col(j, R_CONVA + k), acc_a[:, 0:TP], ALU.mult, ALU.add))
                dve.wait_ge(evacuated, j * 6 + (5 + 3))
                settle()
                do(dve.tensor_tensor(acc_a[:], acc_a[:], ev[4][:], ALU.mult), gates)
                settle()
                do(dve.tensor_copy(blk(p_hi, j), acc_a[:]))
                do(dve.tensor_scalar(blk(cb, j, 0, TP), b_pad[:, 0:TP], col(j, R_CONVB), col(j, R_BIAS), ALU.mult, ALU.add))
                chain.wait(1)
                do(dve.tensor_tensor(blk(p_lo, j), acc_a[:], blk(p_hi, j).bitcast(F32), ALU.subtract), to(a_split))
                do(dve.tensor_scalar(acc_b[:, 0:TP], b_pad[:, 1:1 + TP], col(j, R_CONVB + 1), None, ALU.mult))
                for k in range(2, KC):
                    acc = acc_b[:, 0:TP] if k % 2 else blk(cb, j, 0, TP)
                    chain.wait(1)
                    do(dve.scalar_tensor_tensor(acc, b_pad[:, k:k + TP], col(j, R_CONVB + k), acc, ALU.mult, ALU.add))
                settle()
                do(dve.tensor_tensor(blk(cb, j, 0, TP), blk(cb, j, 0, TP), acc_b[:, 0:TP], ALU.add))
                do(dve.scalar_tensor_tensor(blk(cb, j, TP, T), b_pad[:, KC - 1 + TP:], col(j, R_CONVB + KC - 1), blk(samp_b, j, 0, TS),
                                            ALU.mult, ALU.add), to(conv_done))

                settle()

            settle()
            looped = ((chain, 39), (gates, 3), (to(a_split), 1), (to(conv_done), 1))
            with dve.Fori(0, KB) as j:
                for t, n in looped:
                    t.enter(j, n)
                branches(j)
                for t, _ in looped:
                    t.leave(KB)

            def centre(name, z):
                dve.wait_ge(round_done, DONE[name])
                for h in range(2):
                    part = z[:, :, h * HALF:(h + 1) * HALF]
                    do(dve.tensor_tensor(part, part, rep(work[TILE[name]][:, h, 0:HALF], 1, KB), ALU.subtract),
                       to(centred) if h else chain)

            def squares(z, out):
                settle()
                do(dve.tensor_tensor(out[:], z[:], z[:], ALU.mult))

            def sum_blocks(z, out):
                settle()
                do(dve.tensor_reduce(out[:], z[:].rearrange("p k t -> p t k"), AX.X, ALU.add), to(summed))

            def whiten(z, k):
                dve.wait_ge(std_ready, k)
                settle()
                do(dve.reciprocal(std[:], std[:]))
                settle()
                do(dve.tensor_tensor(z[:], z[:], rep(std[:], 1, KB), ALU.mult), to(std_used))
                settle()

            def affine(z, k, g, b, tally):
                do(dve.tensor_scalar(z[:, k, :], z[:, k, :], col(k, g), col(k, b), ALU.mult, ALU.add), tally)

            def merge(n0, o, b, how):
                dve.wait_ge(evacuated, o * 2 + (n0 + 1 + 3))
                gate, prod = ev[2 * b], ev[2 * b + 1]
                if how == "first":
                    do(dve.tensor_tensor(blk(m, o), gate[:], prod[:], ALU.mult), gates)
                    return
                do(dve.tensor_tensor(gate[:], gate[:], prod[:], ALU.mult))
                settle()
                do(dve.tensor_tensor(blk(m, o), blk(m, o), gate[:], ALU.add), gates)
                if how == "last":
                    settle()
                    split(blk(m, o), blk(q_hi, o), blk(q_lo, o), to(merged_split))
                    settle()
                    do(dve.tensor_scalar(blk(m, o), blk(x_hi, o).bitcast(F32), ALPHA, None, ALU.mult))
                    settle()
                    do(dve.scalar_tensor_tensor(blk(m, o), blk(x_lo, o).bitcast(F32), ALPHA, blk(m, o), ALU.mult, ALU.add))

            def split(z, hi, lo, tally):
                do(dve.tensor_copy(hi, z))
                settle()
                do(dve.tensor_tensor(lo, z, hi.bitcast(F32), ALU.subtract), tally)

            merge(N_GA, 0, 0, "first")
            sum_blocks(v, sums)
            merge(N_GA, 1, 1, "first")
            merge(N_GA, 2, 0, "first")
            centre("meanV", v)
            squares(v, sq)
            merge(N_GA, 3, 1, "first")
            sum_blocks(sq, sums)
            sum_blocks(cb, sums_b)
            merge(N_GA, 4, 0, "first")
            centre("meanB", cb)
            squares(cb, sq)
            merge(N_GA, 5, 1, "first")
            dve.wait_ge(std_ready, 1)
            sum_blocks(sq, sums)
            whiten(v, 1)
            for k in range(KB):
                affine(v, k, R_VG, R_VB, to(v_ready))
            merge(N_GA, 6, 0, "first")
            merge(N_GA, 7, 1, "first")
            whiten(cb, 2)
            for q in range(4):
                dve.wait_ge(round_done, DONE[f"sp{q}"])
                do(dve.tensor_tensor(v[:, 2 * q:2 * q + 2, 0:TP].rearrange("p g (c t) -> p g c t", c=4),
                                     work[TILE[f"sp{q}"]][:].rearrange("p g (c t) -> p g c t", c=4),
                                     rep(bs[:, 2 * q:2 * q + 2, :], 2, 4), ALU.add), to(spatial_read))
            do(dve.tensor_tensor(v[:, :, TP:T], v[:, :, TP:T], rep(w00[:], 2, TS), ALU.mult))
            settle()
            do(dve.tensor_tensor(v[:, :, TP:T], v[:, :, TP:T], bs[:, :, 0:1].to_broadcast([P, KB, TS]), ALU.add))
            dve.wait_ge(tails_out, 80)
            for i in range(KB):
                dve.wait_ge(evacuated, N_U + i + 3)
                settle()
                do(dve.tensor_tensor(v[:, i, :], v[:, i, :], ev[2 * (i % 2)][:], ALU.mult), gates)
                affine(cb, i, R_NBG, R_NBB, to(b_normed))
                gates.wait()
                split(v[:, i, :], q_hi[:, i, :], q_lo[:, i, :], to(c_split))
            settle()
            looped = ((chain, 6), (gates, 2), (to(b_split), 2))
            with dve.Fori(0, KB // 2) as i:
                for t, n in looped:
                    t.enter(i, n)
                for b in range(2):
                    o = i * 2 + b
                    merge(N_GC, o, b, "add")
                    dve.wait_ge(b_sig, o + 1)
                    do(dve.tensor_tensor(blk(cb, o), blk(cb, o), blk(sig_b, o), ALU.mult))
                    settle()
                    split(blk(cb, o), blk(p_hi, o), blk(p_lo, o), to(b_split))
                    settle()
                for t, _ in looped:
                    t.leave(KB // 2)
            looped = ((chain, 8), (gates, 2), (to(merged_split), 2))
            with dve.Fori(0, KB // 2) as i:
                for t, n in looped:
                    t.enter(i, n)
                for b in range(2):
                    merge(N_GB, i * 2 + b, b, "last")
                    settle()
                for t, _ in looped:
                    t.leave(KB // 2)
            for i in range(KB):
                dve.wait_ge(evacuated, N_WO + i + 3)
                do(dve.tensor_tensor(m[:, i, :], m[:, i, :], ev[2 * (i % 2)][:], ALU.add), gates)
                if i:
                    settle()
                    do(dve.tensor_tensor(sums[:], m[:, 0, :] if i == 1 else sums[:], m[:, i, :], ALU.add), chain if i < KB - 1 else to(summed))
            dve.wait_ge(round_done, DONE["meanH"])
            for k in range(KB):
                mk = m[:, k, :].rearrange("p (h t) -> p h t", h=2)
                do(dve.tensor_tensor(mk, mk, work[TILE["meanH"]][:, :, 0:HALF], ALU.subtract), to(h_centred))
            dve.wait_ge(std_ready, 3)
            do(dve.reciprocal(std[:], std[:]))
            settle()
            for k in range(KB):
                do(dve.tensor_tensor(m[:, k, :], m[:, k, :], std[:], ALU.mult), to(h_white))

            grp = lambda t: t[:].rearrange("p b (g i) -> p (b g) i", i=PER_GROUP)
            flat = lambda t: t[:].rearrange("p b g -> p (b g)")
            over4 = lambda t: rep(flat(t), 2, PER_GROUP)
            over_e = lambda t: rep(t[:], 2, E)

            def step(ins, tally=chain):
                do(ins, tally)
                settle()

            step(dve.memset(probs[:], 0.0))
            dve.wait_ge(late_in, 32)
            dve.wait_ge(round_done, DONE["logits"])
            do(dve.tensor_tensor(probs[:, 0:4, :], work[0][:, 0, 0:4 * E].rearrange("p (b e) -> p b e", e=E), rep(rb[:], 1, 4), ALU.add))
            step(dve.tensor_tensor(probs[0:TS, 4, :], work[0][0:TS, 0, 4 * E:5 * E], rb[0:TS, :], ALU.add))
            step(dve.tensor_reduce(s_max[:], probs[:], AX.X, ALU.max))
            step(dve.tensor_tensor(probs[:], probs[:], over_e(s_max), ALU.subtract), to_logits)
            dve.wait_ge(exp_ready, 1)
            step(dve.tensor_reduce(s_sum[:], probs[:], AX.X, ALU.add))
            step(dve.reciprocal(s_sum[:], s_sum[:]))
            step(dve.tensor_tensor(probs[:], probs[:], over_e(s_sum), ALU.mult))

            def first_of(values, top, is_first, best, n):
                step(dve.tensor_reduce(top, values, AX.X, ALU.max))
                step(dve.tensor_tensor(is_first, values, rep(top, 2, n), ALU.is_equal))
                step(dve.tensor_tensor(is_first, is_first, grp(c4)[:, 0:is_first.shape[1], :], ALU.mult))
                step(dve.tensor_reduce(best, is_first, AX.X, ALU.max))
                step(dve.tensor_tensor(is_first, is_first, rep(best, 2, n), ALU.is_equal))

            dve.wait_ge(const_ready, 3)
            first_of(grp(probs), flat(g_m1), grp(oh1), flat(g_t), PER_GROUP)
            step(dve.scalar_tensor_tensor(probs[:], oh1[:], -2.0, probs[:], ALU.mult, ALU.add))
            first_of(grp(probs), flat(g_m2), grp(oh2), flat(g_t), PER_GROUP)
            step(dve.tensor_tensor(g_t[:], g_m1[:], g_m2[:], ALU.add))
            first_of(g_t[:], s_max[:], g_best[:], s_t[:], GROUPS)
            for t in (oh1, oh2):
                do(dve.tensor_tensor(grp(t), grp(t), over4(g_best), ALU.mult))
            settle()
            do(dve.tensor_tensor(mb[:, 0:4, :], oh1[:, 0:4, :], oh2[:, 0:4, :], ALU.add))
            do(dve.tensor_tensor(mb[0:TS, 4, :], oh1[0:TS, 4, :], oh2[0:TS, 4, :], ALU.add), to_mb)
            do(dve.tensor_tensor(g_m1[:], g_m1[:], g_best[:], ALU.mult))
            step(dve.tensor_tensor(g_m2[:], g_m2[:], g_best[:], ALU.mult))
            do(dve.tensor_reduce(s_w1[:], g_m1[:], AX.X, ALU.add))
            step(dve.tensor_reduce(s_w2[:], g_m2[:], AX.X, ALU.add))
            step(dve.tensor_tensor(s_sum[:], s_w1[:], s_w2[:], ALU.add))
            step(dve.reciprocal(s_sum[:], s_sum[:]))
            do(dve.tensor_tensor(s_w1[:], s_w1[:], s_sum[:], ALU.mult))
            step(dve.tensor_tensor(s_w2[:], s_w2[:], s_sum[:], ALU.mult))
            pos = t1
            dve.wait_ge(round_done, DONE["pos"])
            do(dve.tensor_copy(pos[:], work[0][:, 0, 0:NTB * E].rearrange("p (b e) -> p b e", e=E)))
            step(dve.tensor_reduce(s_ps[:, 0:1], work[0][:, 0, NTB * E:(NTB + 1) * E], AX.X, ALU.max))
            do(dve.tensor_copy(count_i[:], s_ps[:, 0:1]), to_count)
            step(dve.tensor_tensor(posm[:], pos[:], mb[:], ALU.mult))
            step(dve.scalar_tensor_tensor(posm[:], mb[:], -1.0, posm[:], ALU.add, ALU.add))

            def mark(ps, e):
                dve.tensor_tensor(onehot[:], rep(iota, 1, NTB), posm[:, :, bass.ds(e, 1)].to_broadcast([P, NTB, C]),
                                  ALU.is_equal).then_inc(ps.onehot_ready, 1)

            def take_ids(ps, e, t):
                dve.wait_ge(ps.ids_mm, t + 1)
                with nc.allow_low_precision(reason="whole numbers"):
                    dve.tensor_reduce(ids[:, bass.ds(e, 1)], pr[1][0:C, 0, 0:2], AX.X, ALU.add).then_inc(ps.ids_ready, 1)

            def gated_product(ps, t):
                dve.wait_ge(ps.silu_ready, t + 1)
                dve.wait_ge(ps.up_done, t + 1)
                dve.tensor_tensor(u_t[:].rearrange("p f t -> p (f t)"), silu[:], pr[0][:, 1, 0:FB * C], ALU.mult).then_inc(ps.u_ready, 1)

            def expert(ps, e, t):
                mark(ps, e + 1)
                take_ids(ps, e + 1, t + 1)
                gated_product(ps, t)

            dve.sem_inc(first.ids_ready, 1)
            dve.wait_ge(const_ready, 4)
            mark(first, 0)
            take_ids(first, 0, 0)
            expert(first, 0, 0)
            for oh, out in ((oh1, slot_a), (oh2, slot_b)):
                do(dve.tensor_tensor(t2[:], oh[:], e_off[:], ALU.mult))
                do(dve.tensor_tensor(probs[:], oh[:], pos[:], ALU.mult))
                settle()
                do(dve.tensor_reduce(s_slot[:], t2[:], AX.X, ALU.add))
                step(dve.tensor_reduce(s_ps[:], probs[:], AX.X, ALU.add))
                step(dve.tensor_tensor(s_slot[:], s_slot[:], s_ps[:], ALU.add))
                for k in range(1, PASSES):
                    step(dve.tensor_scalar(s_t[:], s_ps[:], float(k * C), float(E * C - C), ALU.is_ge, ALU.mult))
                    step(dve.tensor_tensor(s_slot[:], s_slot[:], s_t[:], ALU.add))
                step(dve.tensor_copy(out[:], s_slot[:]), to_slots)
            with dve.Fori(1, E - 1) as e:
                expert(first, e, e)
            gated_product(first, E - 1)
            n_max = further_passes(dve)
            with dve.If(n_max > C):
                dve.sem_inc(further.ids_ready, 1)
                dve.wait_ge(first.y_ready, E + 1)
                with dve.Fori(0, PASSES - 1) as q:
                    dve.tensor_scalar(posm[:], posm[:], -float(C), None, ALU.add).then_inc(more_posm, 1)
                    dve.wait_ge(more_posm, q + 1)
                    mark(further, 0)
                    take_ids(further, 0, q * E)
                    with dve.Fori(0, E - 1) as e:
                        expert(further, e, q * E + e)
                    gated_product(further, q * E + (E - 1))
                dve.nop()
            with dve.Else():
                dve.nop()

            dve.wait_ge(back_in, 64)
            for b in range(NTB):
                n = P if b < 4 else TS
                do(dve.tensor_scalar(h_back[0:n, b, :], h_back[0:n, b, :], ALPHA, None, ALU.mult))
            settle()

            def combine(b):
                n, s = P if b < 4 else TS, b % 2
                dve.wait_ge(y_in[s], 32 * (b // 2) + 32)
                a = y_a[0:n, s, :]
                step(dve.scalar_tensor_tensor(a, a, s_w1[0:n, b:b + 1], h_back[0:n, b, :], ALU.mult, ALU.add))
                step(dve.scalar_tensor_tensor(a, y_b[0:n, s, :], s_w2[0:n, b:b + 1], a, ALU.mult, ALU.add))
                for h in range(2):
                    do(dve.bn_stats(stats[0:n, s, h, :], y_a[0:n, s, h * 512:(h + 1) * 512]))
                settle()
                step(dve.bn_aggr(agg[0:n, s, 0:2], stats[0:n, s].rearrange("p h c -> p (h c)")), to_var)
                dve.wait_ge(std2_ready, b + 1)
                step(dve.reciprocal(agg[0:n, s, 2:3], agg[0:n, s, 2:3]))
                do(dve.scalar_tensor_tensor(agg[0:n, s, 3:4], agg[0:n, s, 0:1], -1.0, agg[0:n, s, 2:3], ALU.mult, ALU.mult), to_scale)

            def shift(b):
                n, s = P if b < 4 else TS, b % 2
                dve.wait_ge(fin_g, b + 1)
                do(dve.tensor_tensor(fin[0:n, s, :], fin[0:n, s, :], ln2_rows[0:n, 1, :], ALU.add), to_fin)

            last[0] = chain
            combine(0)
            for b in range(1, NTB):
                combine(b)
                shift(b - 1)
            shift(NTB - 1)


_INS = ['x_prompt', 'x_sample', 'state_conv_a', 'state_conv_b', 'w_in', 'conv_a_w', 'w_a_out', 'conv_b_w', 'conv_b_bias',
        'norm_b_g', 'norm_b_b', 'w_b_out', 'v_norm_g', 'v_norm_b', 'w_spatial', 'b_spatial', 'w_c_out', 'w_o', 'ln1_g', 'ln1_b',
        'router_w', 'router_b', 'expert_w_gate', 'expert_w_up', 'expert_w_down', 'ln2_g', 'ln2_b']
_OUTS = [(1, 512, 1024), (8, 1, 1024), (1, 1, 2, 1024), (1, 1, 30, 1024), (1, 8, 2, 1024), (1, 8, 30, 1024), (1, 8, 1, 1024)]


def kernel(**inputs):
    import numpy as _np
    import concourse.bacc as _bacc
    from concourse import mybir as _mybir
    from concourse.bass_utils import run_bass_kernel_spmd as _run

    nc = _bacc.Bacc("TRN2", target_bir_lowering=False, num_devices=1)
    arrays, args = {}, []
    for name in _INS:
        a = _np.ascontiguousarray(inputs[name])
        arrays[f"in_{name}_dram"] = a
        args.append(nc.dram_tensor(f"in_{name}_dram", a.shape, _mybir.dt.from_np(a.dtype), kind="ExternalInput").ap())
    for i, shape in enumerate(_OUTS):
        args.append(nc.dram_tensor(f"out_{i}_dram", shape, _mybir.dt.float32, kind="ExternalOutput").ap())
    build(nc, *args)
    r = _run(nc, [arrays], core_ids=[0])
    return tuple(r.results[0][f"out_{i}_dram"] for i in range(len(_OUTS)))
```

```python
from contextlib import ExitStack

import concourse.bass as bass
from concourse import mybir

F32 = mybir.dt.float32
F32R = mybir.dt.float32r
BF16 = mybir.dt.bfloat16
I32 = mybir.dt.int32
ALU = mybir.AluOpType
ACT = mybir.ActivationFunctionType
AX = mybir.AxisListType

P = 128
D = 1024
KB = D // P
TP, TS = 512, 8
T = TP + TS
HALF = T // 2
NTB = 5
KA, KC = 3, 31
E, EF = 16, 512
FB = EF // P
GROUPS, PER_GROUP = 4, 4
CH = 4
CW = D * FB // CH
BY_POOL = {"gate": (1, 3), "up": (1,), "down": (1,)}
C = 96
PASSES = -(-T // C)
ALPHA = 2.0 ** 0.25
EPS = 1e-5

A_BG, A_CG, A_H, B_VAL, B_GATE, C_U, C_V, G_A, G_B, G_C = (D * i for i in range(10))

R_CONVB, R_CONVA, R_BIAS, R_NBG, R_NBB, R_VG, R_VB, R_L1G, R_L1B, R_STA = 0, 31, 34, 35, 36, 37, 38, 39, 40, 41
NROWS = R_STA + 2 * TS

N_S1 = 0
N_GA = N_S1 + 6 * KB
N_U = N_GA + 2 * KB
N_GC = N_U + KB
N_GB = N_GC + 2 * KB
N_WO = N_GB + 2 * KB
N_END = N_WO + KB

ROUNDS = [("rows", 1), ("xs", 0), ("sb0", 1), ("sb1", 0), ("ws0", 1), ("ws1", 0),
          ("meanV", 0), ("varV", 0), ("meanB", 1), ("varB", 0),
          ("vt0", 1), ("vt1", 0), ("vt2", 1), ("vt3", 0), ("tailB", 1), ("tailA", 0), ("tailV", 1),
          ("sp0", 0), ("sp1", 1), ("sp2", 0), ("sp3", 1),
          ("meanH", 0), ("varH", 1), ("logits", 0), ("ht0", 1), ("ht1", 0), ("ht2", 1), ("ht3", 0), ("ht4", 1),
          ("pos", 0)]
DONE = {name: i + 1 for i, (name, _) in enumerate(ROUNDS)}
TILE = dict(ROUNDS)
BEFORE = {name: next((n for n, t in reversed(ROUNDS[:i]) if t == tile), None) for i, (name, tile) in enumerate(ROUNDS)}


class Tally:

    def __init__(self, eng, sem, start=0):
        self.eng, self.sem, self.base, self.n, self.var = eng, sem, start, 0, None

    def inc(self, ins):
        ins.then_inc(self.sem, 1)
        self.n += 1

    def value(self, lag=0):
        now = self.base + self.n - lag
        return now if self.var is None else self.var + now

    def wait(self, lag=0):
        self.eng.wait_ge(self.sem, self.value(lag))

    def enter(self, i, per):
        self.outer, self.per, self.var, self.n0 = self.n, per, i * per, self.n

    def leave(self, count):
        assert self.n - self.n0 == self.per, (self.n - self.n0, self.per)
        self.var, self.n = None, self.n0 + self.per * count


def rep(ap, axis, n):
    v = ap.unsqueeze(axis)
    shape = list(v.shape)
    shape[axis] = n
    return v.to_broadcast(shape)


def build(nc, x_prompt, x_sample, state_conv_a, state_conv_b, w_in, conv_a_w, w_a_out, conv_b_w, conv_b_bias,
          norm_b_g, norm_b_b, w_b_out, v_norm_g, v_norm_b, w_spatial, b_spatial, w_c_out, w_o, ln1_g, ln1_b,
          router_w, router_b, expert_w_gate, expert_w_up, expert_w_down, ln2_g, ln2_b,
          y_prompt, y_sample, new_a_prompt, new_b_prompt, new_a_sample, new_b_sample, new_v_sample):
    h_rows = nc.dram_tensor("h_rows", (T, D), F32, kind="Internal").ap()
    y_rows = nc.dram_tensor("y_rows", (PASSES * E * C, D), F32, kind="Internal").ap()

    in_v = w_in[0].rearrange("(k p) n -> p k n", p=P)
    a_out_v = w_a_out[0].rearrange("(k p) n -> p k n", p=P)
    b_out_v = w_b_out[0].rearrange("(k p) n -> p k n", p=P)
    c_out_v = w_c_out[0].rearrange("(k p) n -> p k n", p=P)
    o_v = w_o[0].rearrange("(k p) n -> p k n", p=P)
    gate_v = expert_w_gate[0].rearrange("e (k p) f -> p (e k) f", p=P)
    up_v = expert_w_up[0].rearrange("e (k p) f -> p (e k) f", p=P)
    down_v = expert_w_down[0].rearrange("e (k p) n -> p (e k) n", p=P)

    with ExitStack() as ctx:
        U = KB * T * 4
        base = (nc.sbuf_base + 31) // 32 * 32
        at = {}
        cursor = [base]

        def region(name, size):
            at[name] = cursor[0]
            cursor[0] += (size + 31) // 32 * 32

        for name in ("P_HI", "P_LO", "CB", "X_HI", "X_LO", "V", "Q_HI", "Q_LO", "M"):
            region(name, U)
        region("RING", 6 * D * 4)

        def place(name, where, shape, dt=F32, plus=0):
            return nc.alloc_sbuf_tensor_at(name, shape, dt, offset=at[where] + plus)

        def sb(name, shape, dt=F32):
            size = 1
            for n in shape[1:]:
                size *= n
            region(name, size * (2 if dt == BF16 else 4))
            return place(name, name, shape, dt)

        def sem(name):
            return ctx.enter_context(nc.semaphore(name))

        p_hi, p_lo = place("p_hi", "P_HI", [P, KB, T], F32R), place("p_lo", "P_LO", [P, KB, T], F32R)
        q_hi, q_lo = place("q_hi", "Q_HI", [P, KB, T], F32R), place("q_lo", "Q_LO", [P, KB, T], F32R)
        x_hi, x_lo = place("x_hi", "X_HI", [P, KB, T], F32R), place("x_lo", "X_LO", [P, KB, T], F32R)
        cb = place("cb", "CB", [P, KB, T])
        v = place("v", "V", [P, KB, T])
        m = place("m", "M", [P, KB, T])
        sig_b = place("sig_b", "V", [P, KB, T])
        vt = place("vt", "Q_HI", [P, 4, D])
        sq = place("sq", "Q_LO", [P, KB, T])
        sq_h = place("sq_h", "RING", [P, KB, T])
        tails = place("tails", "Q_LO", [38, 3, D])
        raw = place("raw", "RING", [P, 2, KB, P])
        w_hi = place("w_hi", "RING", [P, 2, KB, P], F32R, plus=2 * D * 4)
        w_lo = place("w_lo", "RING", [P, 2, KB, P], F32R, plus=4 * D * 4)
        x_tok = place("x_tok", "V", [P, 4, D])
        rows = place("rows", "M", [NROWS, D])
        xs_tok = place("xs_tok", "M", [TS, D], plus=D * 4)
        sb_tok = place("sb_tok", "M", [120, 2, D], plus=2 * D * 4)
        ws_nat = place("ws_nat", "CB", [P, KB, P])
        sb_t = place("sb_t", "Q_LO", [P, KB, TS, KC - 1])
        WB = KB * EF * 4
        slot_at = ("P_HI", "X_HI", "Q_HI")
        w_e = {"gate": [place(f"w_gate{i}", r, [P, D * FB]) for i, r in enumerate(slot_at)],
               "up": [place(f"w_up{i}", r, [P, D * FB], plus=WB) for i, r in enumerate(slot_at)],
               "down": [place(f"w_down{i}", r, [P, D * FB], plus=2 * WB) for i, r in enumerate(slot_at)]}
        w_e_lo = {kind: [place(f"w_{kind}_lo{i}", r, [P, D * FB], F32R, plus=j * WB) for i, r in enumerate(slot_at)]
                  for j, kind in enumerate(("gate", "up", "down"))}
        ring = place("ring", "RING", [P, CH, CW], F32R)
        hs = place("hs", "RING", [C, D], plus=4 * D * 4)
        y_out = place("y_out", "RING", [C, D], plus=5 * D * 4)
        y_a = place("y_a", "X_HI", [P, NTB, D])
        y_b = place("y_b", "X_HI", [P, NTB, D], plus=NTB * D * 4)
        fin = place("fin", "Q_HI", [P, NTB, D], plus=(NTB + 2) * D * 4)
        h_back = place("h_back", "Q_HI", [P, NTB, D])
        ln2_rows = place("ln2_rows", "Q_HI", [P, 2, D], plus=NTB * D * 4)

        ev = [sb(f"ev{i}", [P, T]) for i in range(5)]
        b_pad = sb("b_pad", [P, KC - 1 + T])
        a_pad = sb("a_pad", [P, KA - 1 + T])
        acc_b = sb("acc_b", [P, T])
        acc_a = sb("acc_a", [P, T])
        par = sb("par", [P, KB * NROWS])
        bs = sb("bs", [P, KB, P])
        w00 = sb("w00", [P, KB])
        ws_t = sb("ws_t", [P, KB, P])
        ident = sb("ident", [P, P])
        mean_w = sb("mean_w", [P, P])
        tail_b = sb("tail_b", [P, KB, 38])
        tail_a = sb("tail_a", [P, KB, 10])
        samp_b = sb("samp_b", [P, KB, TS])
        samp_a = sb("samp_a", [P, KB, TS])
        samp_t = sb("samp_t", [P, KB, TS])
        std = sb("std", [P, T])
        sums_b = acc_b
        sums = acc_a
        eps_t = sb("eps_t", [P, 2])
        rw = sb("rw", [P, KB, E])
        rb = sb("rb", [P, E])
        tri = sb("tri", [P, P], BF16)
        ones_b = sb("ones_b", [P, P], BF16)
        id_cols = sb("id_cols", [P, NTB, 2], BF16)
        probs, oh1, oh2, t1, t2, posm = (place(f"router{i}", "b_pad", [P, NTB, E], plus=i * NTB * E * 4) for i in range(6))
        e_off, c4 = sb("e_off", [P, NTB, E]), sb("c4", [P, NTB, E])
        mb = sb("mb", [P, NTB, E], BF16)
        g_m1, g_m2, g_t, g_best = (sb(f"g{i}", [P, NTB, GROUPS]) for i in range(4))
        s_max, s_sum, s_w1, s_w2, s_ps, s_t, s_slot = (sb(f"s{i}", [P, NTB]) for i in range(7))
        slot_a, slot_b = sb("slot_a", [P, NTB], I32), sb("slot_b", [P, NTB], I32)
        ids = sb("ids", [C, 2], I32)
        count_i = sb("count_i", [P, 1], I32)
        h_tok = [place("h_tok0", "RING", [P, D], plus=4 * D * 4), place("h_tok1", "RING", [P, D], plus=5 * D * 4),
                 place("h_tok2", "bs", [P, D]), place("h_tok3", "ws_t", [P, D]), place("h_tok4", "ev0", [TS, D])]
        hs_hi = place("hs_hi", "ev0", [P, 2, KB, C], F32R)
        hs_lo = place("hs_lo", "bs", [P, 2, KB, C], F32R)
        silu = place("silu", "ev3", [C, EF])
        u = place("u", "acc_b", [C, EF])
        u_hi = place("u_hi", "ev4", [P, FB, C], F32R, plus=C * 4)
        u_lo = place("u_lo", "acc_a", [P, FB, C], F32R)
        onehot = place("onehot", "std", [P, NTB, C], BF16)
        iota = ev[4][:, 0:C]
        lg = ev[3]
        stats = sb("stats", [P, 2, 2, 6])
        agg = sb("agg", [P, 2, 4])
        assert cursor[0] <= nc.sbuf_usable_end - 64, (cursor[0], nc.sbuf_usable_end)

        pr = [ctx.enter_context(nc.psum_tensor(f"pr{i}", [P, 2, 512], F32)) for i in range(2)]
        work = [ctx.enter_context(nc.psum_tensor(f"work{i}", [P, 2, 512], F32)) for i in range(2)]

        x_in, rows_in, states_in, spatial_in, late_in = (sem(n) for n in ("x_in", "rows_in", "states_in", "spatial_in", "late_in"))
        const_ready, spatial_masked, pool_chain = sem("const_ready"), sem("spatial_masked"), sem("pool_chain")
        x_turned, x_rounded, x_split = sem("x_turned"), sem("x_rounded"), sem("x_split")
        raw_in = [sem("raw_in0"), sem("raw_in1")]
        w_rounded = sem("w_rounded")
        w_split = sem("w_split")
        proj_done = sem("proj_done")
        evacuated = sem("evacuated")
        gated = sem("gated")
        round_done = sem("round_done")
        dve_chain = sem("dve_chain")
        setup_done = sem("setup_done")
        summed = sem("summed")
        h_centred, h_white, sq_h_ready = sem("h_centred"), sem("h_white"), sem("sq_h_ready")
        centred = sem("centred")
        std_ready = sem("std_ready")
        std_used = sem("std_used")
        v_ready = sem("v_ready")
        tails_ready = sem("tails_ready")
        tails_out = sem("tails_out")
        vt_ready = sem("vt_ready")
        a_split, b_split, c_split, merged_split = sem("a_split"), sem("b_split"), sem("c_split"), sem("merged_split")
        conv_done = sem("conv_done")
        b_normed, b_sig = sem("b_normed"), sem("b_sig")
        spatial_read = sem("spatial_read")
        h_ready = sem("h_ready")
        h_tok_ready = sem("h_tok_ready")
        h_stored = sem("h_stored")
        logits_ready, exp_ready = sem("logits_ready"), sem("exp_ready")
        mb_ready = sem("mb_ready")
        count_ready = sem("count_ready")
        states_out = sem("states_out")
        slots_ready = sem("slots_ready")
        back_in = sem("back_in")
        lg_turned, lg_ready = sem("lg_turned"), sem("lg_ready")
        loads_begun, gathers_begun = sem("loads_begun"), sem("gathers_begun")
        more_posm = sem("more_posm")
        y_in = [sem(f"y_in{b}") for b in range(NTB)]
        y_read = sem("y_read")
        var_ready, std2_ready, scale_ready, normed, fin_ready, fin_g = (sem(n) for n in ("var_ready", "std2_ready", "scale_ready", "normed", "fin_ready", "fin_g"))
        fin_out = [sem("fin_out0"), sem("fin_out1")]

        MATRICES = ("gate", "up", "down")

        class Pass:

            def __init__(self, tag):
                self.onehot_ready, self.ids_mm, self.ids_ready = sem(tag + "onehot"), sem(tag + "ids_mm"), sem(tag + "ids_ready")
                self.gathered = sem(tag + "gathered")
                self.turned, self.hs_hi_ready, self.hs_lo_ready = sem(tag + "turned"), sem(tag + "hs_hi"), sem(tag + "hs_lo")
                self.landed = {k: [sem(tag + f"{k}_in{i}") for i in range(3)] for k in MATRICES}
                self.hi = {k: sem(tag + f"{k}_hi") for k in MATRICES}
                self.lo_dve = {k: sem(tag + f"{k}_lo_dve") for k in MATRICES}
                self.lo_pool = {k: sem(tag + f"{k}_lo_pool") for k in MATRICES}
                self.done = {k: sem(tag + f"{k}_done") for k in MATRICES}
                self.silu_ready, self.u_ready, self.y_ready = sem(tag + "silu"), sem(tag + "u"), sem(tag + "y_ready")
                self.u_turned, self.u_hi_ready, self.u_lo_ready = sem(tag + "u_turned"), sem(tag + "u_hi"), sem(tag + "u_lo")
                self.stored = sem(tag + "stored")

        first, further = Pass("first_"), Pass("more_")

        block = ctx.enter_context(nc.Block())

        READ = {"rows": (setup_done, 1), "xs": (x_split, KB + 1), "sb0": (setup_done, 2), "sb1": (setup_done, 3),
                "ws0": (setup_done, 4), "ws1": (setup_done, 5), "meanV": (centred, 1), "varV": (std_ready, 1),
                "meanB": (centred, 2), "varB": (std_ready, 2), "meanH": (h_centred, KB), "varH": (std_ready, 3),
                "tailB": (tails_ready, 1), "tailA": (tails_ready, 2), "tailV": (tails_ready, 3), "logits": (logits_ready, 1)}
        READ.update({f"vt{c}": (vt_ready, c + 1) for c in range(4)})
        READ.update({f"sp{q}": (spatial_read, q + 1) for q in range(4)})
        READ.update({f"ht{b}": (h_tok_ready, b + 1) for b in range(NTB)})

        def work_wait(eng, name):
            if BEFORE[name]:
                eng.wait_ge(*READ[BEFORE[name]])

        def further_passes(eng):
            eng.wait_ge(count_ready, 1)
            return eng.value_load(count_i[0:1, 0:1], min_val=0, max_val=T)

        def each_tile(eng, step):
            step(0, 0, 0)
            with eng.Fori(0, 2) as i:
                for m in range(1, 7):
                    step(i * 6 + m, m, i * 2 + m // 3)
            for e in (13, 14, 15):
                step(e, e, e // 3)

        def chunk(kind, slot, i, of=w_e):
            return of[kind][slot][:, i * CW:(i + 1) * CW]

        @block.sync
        def _(sp):
            sp.dma_start(x_tok[:], x_prompt[0].rearrange("(b p) n -> p b n", p=P)).then_inc(x_in, 16)
            sp.dma_start(xs_tok[:], x_sample[:, 0, :]).then_inc(x_in, 16)

            def load(slot, n, view, col):
                sp.wait_ge(w_split, n * 2 + 2)
                sp.sem_inc(loads_begun, 1)
                sp.dma_start(raw[:, slot], view[:, :, bass.ds(col, P)]).then_inc(raw_in[slot], 16)

            with sp.Fori(0, KB) as j:
                for r, role in enumerate((B_GATE, B_VAL, C_V, A_CG, A_H, A_BG)):
                    load(r % 2, j * 6 + (N_S1 + r), in_v, j * P + role)

            def pairs(n0, gate, out_v):
                with sp.Fori(0, KB) as o:
                    load(0, o * 2 + n0, in_v, o * P + gate)
                    load(1, o * 2 + (n0 + 1), out_v, o * P)

            def singles(n0, view, col0):
                with sp.Fori(0, KB // 2) as i:
                    for s in range(2):
                        load(s, i * 2 + (n0 + s), view, i * 2 * P + (col0 + s * P))

            pairs(N_GA, G_A, a_out_v)
            singles(N_U, in_v, C_U)
            sp.dma_start(new_a_sample[0, :, 0:KA - 2, :], state_conv_a[0, :, 1:KA - 1, :]).then_inc(states_out, 16)
            sp.dma_start(new_b_sample[0, :, 0:KC - 2, :], state_conv_b[0, :, 1:KC - 1, :]).then_inc(states_out, 16)
            pairs(N_GC, G_C, c_out_v)
            pairs(N_GB, G_B, b_out_v)

            views = {"gate": (gate_v, KB), "up": (up_v, KB), "down": (down_v, FB)}

            def expert_load(ps, s, e, kind):
                view, k = views[kind]
                sp.dma_start(w_e[kind][s][:].rearrange("p (k n) -> p k n", k=k), view[:, bass.ds(e * k, k), :]).then_inc(ps.landed[kind][s], 16)

            def reload(ps, s, e, kind, t):
                sp.wait_ge(ps.done[kind], t * CH + CH)
                expert_load(ps, s, e + 3, kind)

            def store(ps, e, t, row0):
                sp.wait_ge(ps.y_ready, t + 2)
                sp.dma_start(y_rows[bass.ds(e * C + row0, C), :], y_out[:]).then_inc(ps.stored, 16)

            def expert_pass(ps, row0, n0):
                def step(e, m, third):
                    if m <= 12:
                        reload(ps, m % 3, e, "gate", e + n0)
                    if m:
                        if m <= 13:
                            reload(ps, (m - 1) % 3, e - 1, "down", e + n0 - 1)
                        store(ps, e - 1, e + n0 - 1, row0)
                    if m <= 12:
                        reload(ps, m % 3, e, "up", e + n0)

                each_tile(sp, step)

            def h_out():
                for b in range(NTB):
                    n = P if b < 4 else TS
                    sp.wait_ge(h_tok_ready, b + 1)
                    sp.dma_start(h_rows[b * P:b * P + n, :], h_tok[b][:]).then_inc(h_stored, 16)

            early = [(e, kind) for e in (0, 1) for kind in MATRICES][:4]
            for i in range(KB):
                load(i % 2, N_WO + i, o_v, i * P)
                if i % 2 and i // 2 < len(early):
                    e, kind = early[i // 2]
                    if i == 1:
                        sp.wait_ge(proj_done, 2 + N_WO)
                    if e == 1:
                        sp.wait_ge(gated, 28 + 3 * KB + KB - 1)
                    expert_load(first, e, e, kind)
            expert_load(first, 1, 1, "up")
            sp.wait_ge(proj_done, 2 + N_END)
            expert_load(first, 2, 2, "gate")
            expert_load(first, 2, 2, "up")
            expert_load(first, 1, 1, "down")
            h_out()
            expert_load(first, 2, 2, "down")
            sp.sem_inc(first.stored, 16)
            expert_pass(first, 0, 0)

            def load_back():
                sp.dma_start(h_back[:, 0:4, :], h_rows[0:TP, :].rearrange("(b p) n -> p b n", p=P)).then_inc(back_in, 16)
                sp.dma_start(h_back[0:TS, 4, :], h_rows[TP:T, :]).then_inc(back_in, 16)
                sp.dma_start(ln2_rows[:, 0, :], ln2_g[0].partition_broadcast(P)).then_inc(back_in, 16)
                sp.dma_start(ln2_rows[:, 1, :], ln2_b[0].partition_broadcast(P)).then_inc(back_in, 16)

            n_max = further_passes(sp)
            with sp.If(n_max > C):
                store(first, E - 1, E - 1, 0)
                sp.wait_ge(first.stored, 16 * (E + 1))
                sp.sem_inc(further.stored, 16)
                with sp.Fori(0, PASSES - 1) as q:
                    for s in range(3):
                        for which in MATRICES:
                            expert_load(further, s, s, which)
                    expert_pass(further, q * (E * C) + E * C, q * E)
                    store(further, E - 1, q * E + (E - 1), q * (E * C) + E * C)
                sp.wait_ge(further.stored, 16 * (E * (PASSES - 1) + 1))
                load_back()
            with sp.Else():
                load_back()
                store(first, E - 1, E - 1, 0)
                sp.wait_ge(first.stored, 16 * (E + 1))
                sp.nop()
            sp.sem_inc(y_read, 1)
            for b in range(NTB):
                n = P if b < 4 else TS
                sp.wait_ge(fin_ready, b + 1)
                dst = y_prompt[0, b * P:(b + 1) * P, :] if b < 4 else y_sample[:, 0, :]
                sp.dma_start(dst, fin[0:n, b, :]).then_inc(fin_out[b % 2], 16)
            sp.wait_ge(fin_out[0], 48)
            sp.wait_ge(fin_out[1], 32)
            sp.wait_ge(tails_out, 80)
            sp.wait_ge(states_out, 32)

        @block.gpsimd
        def _(pool):
            chain = Tally(pool, pool_chain)
            pool.sem_inc(w_split, 4)
            chain.inc(pool.memset(ident[:], 0.0))
            chain.wait()
            pool.affine_select(out=ident[:], in_=ident[:], compare_op=ALU.not_equal, fill=1.0, base=0,
                               pattern=[[-1, P]], channel_multiplier=1).then_inc(const_ready, 1)
            pool.memset(mean_w[:], 1.0 / D)
            pool.memset(eps_t[:, 1:2], EPS / ALPHA ** 2)
            pool.memset(eps_t[:, 0:1], EPS).then_inc(const_ready, 1)
            pool.wait_ge(spatial_in, 48)
            pool.affine_select(out=ws_nat[:], in_=ws_nat[:], compare_op=ALU.is_ge, fill=0.0, base=0,
                               pattern=[[0, KB], [-1, P]], channel_multiplier=1).then_inc(spatial_masked, 1)

            def lower(slot, n):
                for h in range(2):
                    k = slice(h * KB // 2, (h + 1) * KB // 2)
                    pool.wait_ge(w_rounded, n * 2 + (h + 1))
                    pool.tensor_tensor(w_lo[:, slot, k], raw[:, slot, k], w_hi[:, slot, k].bitcast(F32), ALU.subtract).then_inc(w_split, 1)

            with pool.Fori(0, N_GA // 6) as j:
                for r in range(6):
                    lower(r % 2, j * 6 + r)
            chain.inc(pool.memset(tri[:], 1.0))
            pool.memset(ones_b[:], 1.0)
            chain.wait()
            pool.affine_select(out=tri[:], in_=tri[:], compare_op=ALU.is_ge, fill=0.0, base=-1,
                               pattern=[[1, P]], channel_multiplier=-1)
            pool.iota(id_cols[:, :, 0], pattern=[[P, NTB]], base=0, channel_multiplier=0, allow_small_or_imprecise_dtypes=True)
            pool.iota(id_cols[:, :, 1], pattern=[[0, NTB]], base=0, channel_multiplier=1, allow_small_or_imprecise_dtypes=True)
            pool.iota(e_off[:], pattern=[[0, NTB], [C, E]], base=0, channel_multiplier=0, allow_small_or_imprecise_dtypes=True)
            pool.iota(c4[:].rearrange("p b (g i) -> p (b g) i", i=PER_GROUP), pattern=[[0, NTB * GROUPS], [-1, PER_GROUP]],
                      base=PER_GROUP, channel_multiplier=0, allow_small_or_imprecise_dtypes=True).then_inc(const_ready, 1)
            with pool.Fori(0, (N_END - N_GA) // 2) as j:
                for s in range(2):
                    lower(s, j * 2 + (N_GA + s))
            pool.wait_ge(gated, 28 + 4 * KB + KB - 1)
            pool.iota(iota, pattern=[[1, C]], base=0, channel_multiplier=0,
                      allow_small_or_imprecise_dtypes=True).then_inc(const_ready, 1)

            def gather(ps, m, t):
                pool.wait_ge(ps.ids_ready, t + 2)
                pool.wait_ge(ps.turned, t + 1)
                pool.sem_inc(gathers_begun, 1)
                pool.indirect_dma_start(out=hs[:], out_offset=None, in_=h_rows,
                                        in_offset=bass.IndirectOffsetOnAxis(ap=ids[:, m % 2:m % 2 + 1], axis=0)).then_inc(ps.gathered, 16)

            def low_parts(ps, kind, s, t):
                for i in BY_POOL[kind]:
                    pool.wait_ge(ps.hi[kind], t * CH + (i + 1))
                    pool.tensor_tensor(chunk(kind, s, i, w_e_lo), chunk(kind, s, i), ring[:, i].bitcast(F32), ALU.subtract).then_inc(ps.lo_pool[kind], 1)

            def expert_pass(ps, n0):
                gather(ps, 0, n0)
                def step(e, m, third):
                    t = e + n0
                    if m or ps is further:
                        low_parts(ps, "gate", m % 3, t)
                    if m == 0:
                        gather(ps, 1, t + 1)
                        low_parts(ps, "up", 0, t)
                    else:
                        low_parts(ps, "down", (m - 1) % 3, t - 1)
                    if m <= 13:
                        gather(ps, m, t + 2)
                    if m:
                        low_parts(ps, "up", m % 3, t)

                each_tile(pool, step)
                low_parts(ps, "down", 0, n0 + (E - 1))

            low_parts(first, "gate", 0, 0)
            pool.wait_ge(h_stored, 16 * NTB)
            expert_pass(first, 0)

            def finish(table):
                pool.wait_ge(y_read, 1)
                pool.wait_ge(slots_ready, 2)

                def fetch(b):
                    n = P if b < 4 else TS
                    for dst, slot in ((y_a, slot_a), (y_b, slot_b)):
                        pool.indirect_dma_start(out=dst[0:n, b, :], out_offset=None, in_=table,
                                                in_offset=bass.IndirectOffsetOnAxis(ap=slot[0:n, b:b + 1], axis=0)).then_inc(y_in[b], 16)

                for b in range(NTB):
                    fetch(b)
                for b in range(NTB):
                    n = P if b < 4 else TS
                    pool.wait_ge(normed, b + 1)
                    pool.tensor_tensor(fin[0:n, b, :], fin[0:n, b, :], ln2_rows[0:n, 0, :], ALU.mult).then_inc(fin_g, 1)

            n_max = further_passes(pool)
            with pool.If(n_max > C):
                with pool.Fori(0, PASSES - 1) as q:
                    expert_pass(further, q * E)
                finish(y_rows)
            with pool.Else():
                finish(y_rows[0:E * C, :])

        @block.scalar
        def _(act):
            act.sem_inc(evacuated, 2)
            for view, r, k in ((conv_b_w[0], R_CONVB, KC), (conv_a_w[0], R_CONVA, KA), (conv_b_bias, R_BIAS, 1), (norm_b_g, R_NBG, 1),
                               (norm_b_b, R_NBB, 1), (v_norm_g, R_VG, 1), (v_norm_b, R_VB, 1), (ln1_g, R_L1G, 1), (ln1_b, R_L1B, 1),
                               (state_conv_a[0].rearrange("s k n -> (s k) n"), R_STA, 2 * TS)):
                act.dma_start(rows[r:r + k, :], view).then_inc(rows_in, 16)
            act.dma_start(sb_tok[:], state_conv_b[0].rearrange("(b s) k n -> (s k) b n", b=2)).then_inc(states_in, 16)
            act.dma_start(ws_nat[:], w_spatial[0].rearrange("g t s -> t g s")).then_inc(spatial_in, 16)
            act.dma_start(bs[:], b_spatial[0].partition_broadcast(P)).then_inc(spatial_in, 16)
            with nc.allow_non_contiguous_dma(reason="one weight per group"):
                act.dma_start(w00[:].unsqueeze(2), w_spatial[0, :, 0, 0:1].partition_broadcast(P)).then_inc(spatial_in, 16)
            act.dma_start(rw[:], router_w.rearrange("(k p) e -> p k e", p=P)).then_inc(late_in, 16)
            act.dma_start(rb[:], router_b.partition_broadcast(P)).then_inc(late_in, 16)

            def round_w(slot, use, n):
                act.wait_ge(raw_in[slot], use * 16 + 16)
                act.wait_ge(proj_done, n + 1)
                for h in range(2):
                    k = slice(h * KB // 2, (h + 1) * KB // 2)
                    act.activation(w_hi[:, slot, k], raw[:, slot, k], ACT.Copy).then_inc(w_rounded, 1)

            def evacuate(n, src, out, func=ACT.Copy):
                act.wait_ge(proj_done, n + 3)
                act.activation(out, src[:, :, 0:HALF], func).then_inc(evacuated, 1)

            def halves(ap):
                return ap.rearrange("p (h t) -> p h t", h=2)

            for j in range(KB):
                act.wait_ge(x_turned, j + 1)
                act.activation(x_hi[:, j, 0:TP], pr[j // 2 % 2][:, j % 2, :], ACT.Copy).then_inc(x_rounded, 1)
            act.wait_ge(round_done, DONE["xs"])
            act.activation(x_hi[:, :, TP:T], work[TILE["xs"]][:, 0, 0:KB * TS].rearrange("p (k s) -> p k s", s=TS),
                           ACT.Copy).then_inc(x_rounded, 1)
            round_w(0, 0, 0)

            def next_w(s, use, n):
                round_w(1 - s, use if s == 0 else use + 1, n + 1)

            with act.Fori(0, KB) as j:
                for r, (out, func, g) in enumerate(((halves(ev[0][:]), ACT.Sigmoid, 1), (halves(ev[1][:]), ACT.Copy, 1),
                                                    (None, ACT.Copy, 0), (halves(ev[2][:]), ACT.Copy, 2),
                                                    (halves(ev[3][:]), ACT.Copy, 2), (halves(ev[4][:]), ACT.Copy, 3))):
                    n = j * 6 + r
                    next_w(r % 2, j * 3 + r // 2, n)
                    if out is None:
                        out = v[:, bass.ds(j, 1), :].rearrange("p o (h t) -> p (o h) t", h=2)
                    else:
                        act.wait_ge(gated, j * 3 + g)
                    evacuate(n, pr[r % 2], out, func)

            def gate_pairs(n0, m0, count, with_b=False):
                with act.Fori(0, count // 2) as i:
                    for b in range(2):
                        mm = i * 2 + (m0 + b)
                        for s in range(2):
                            n = i * 4 + (n0 + 2 * b + s)
                            next_w(s, i * 2 + (n0 // 2 + b), n)
                            if s == 0:
                                act.wait_ge(gated, mm + 26)
                            evacuate(n, pr[s], halves(ev[2 * b + s][:]), ACT.Copy if s else ACT.Sigmoid)
                        if with_b:
                            act.wait_ge(b_normed, i * 2 + (b + 1))
                            act.activation(sig_b[:, bass.ds(i * 2 + b, 1), :], cb[:, bass.ds(i * 2 + b, 1), :], ACT.Sigmoid).then_inc(b_sig, 1)

            def singles(n0, m0, count, last=False):
                with act.Fori(0, count // 2 - (1 if last else 0)) as i:
                    for s in range(2):
                        n = i * 2 + (n0 + s)
                        next_w(s, i + n0 // 2, n)
                        act.wait_ge(gated, i * 2 + (m0 + s + 26))
                        evacuate(n, pr[s], halves(ev[2 * s][:]))
                if last:
                    for s in range(2):
                        n = n0 + count - 2 + s
                        if s == 0:
                            next_w(s, n // 2, n)
                        act.wait_ge(gated, m0 + count - 2 + s + 26)
                        evacuate(n, pr[s], halves(ev[2 * s][:]))

            def root(name, k):
                act.wait_ge(round_done, DONE[name])
                if k:
                    act.wait_ge(std_used, k)
                act.activation(halves(std[:]), work[TILE[name]][:, :, 0:HALF], ACT.Sqrt, bias=eps_t[:, 0:1]).then_inc(std_ready, 1)

            gate_pairs(N_GA, 0, 4)
            gate_pairs(N_GA + 8, 4, 2)
            root("varV", 0)
            gate_pairs(N_GA + 12, 6, 2)
            root("varB", 1)
            for c in range(4):
                act.wait_ge(round_done, DONE[f"vt{c}"])
                act.activation(vt[:, c, :].rearrange("p (h t) -> p h t", h=2), work[TILE[f"vt{c}"]][:], ACT.Copy).then_inc(vt_ready, 1)
            for i, (name, k) in enumerate((("tailB", 38), ("tailA", 10), ("tailV", 8))):
                act.wait_ge(round_done, DONE[name])
                act.activation(tails[0:k, i, :].rearrange("p (h t) -> p h t", h=2), work[TILE[name]][0:k], ACT.Copy).then_inc(tails_ready, 1)
            act.wait_ge(tails_ready, 3)
            act.dma_start(new_b_prompt[0, 0], tails[0:30, 0, :]).then_inc(tails_out, 16)
            act.dma_start(new_b_sample[0, :, KC - 2, :], tails[30:38, 0, :]).then_inc(tails_out, 16)
            act.dma_start(new_a_prompt[0, 0], tails[0:2, 1, :]).then_inc(tails_out, 16)
            act.dma_start(new_a_sample[0, :, KA - 2, :], tails[2:10, 1, :]).then_inc(tails_out, 16)
            act.dma_start(new_v_sample[0, :, 0, :], tails[0:8, 2, :]).then_inc(tails_out, 16)
            singles(N_U, 8, 8)
            gate_pairs(N_GC, 16, 8, with_b=True)
            gate_pairs(N_GB, 24, 8)
            singles(N_WO, 32, 8, last=True)
            def rounded_parts(ps, kind, s, use, t, before=None, chunks=range(CH)):
                act.wait_ge(ps.landed[kind][s], use * 16 + 16)
                for i in chunks:
                    if before:
                        prev, tp = before
                        act.wait_ge(ps.done[prev], tp * CH + (i + 1))
                    act.activation(ring[:, i], chunk(kind, s, i), ACT.Copy).then_inc(ps.hi[kind], 1)

            for k in range(KB):
                act.wait_ge(h_centred, k + 1)
                act.activation(sq_h[:, k, :], m[:, k, :], ACT.Square).then_inc(sq_h_ready, 1)
            root("varH", 2)
            rounded_parts(first, "gate", 0, 0, 0)
            for k in range(KB):
                act.wait_ge(h_white, k + 1)
                act.activation(m[:, k, :], m[:, k, :], ACT.Identity, scale=par[:, k * NROWS + R_L1G:k * NROWS + R_L1G + 1],
                               bias=par[:, k * NROWS + R_L1B:k * NROWS + R_L1B + 1]).then_inc(h_ready, 1)
            act.wait_ge(lg_turned, 1)
            act.activation(lg[0:E, :].rearrange("p (h t) -> p h t", h=2), work[TILE["logits"]][0:E, :, 0:HALF], ACT.Copy).then_inc(lg_ready, 1)
            act.wait_ge(logits_ready, 1)
            act.activation(probs[:], probs[:], ACT.Exp).then_inc(exp_ready, 1)
            for b in range(NTB):
                n = P if b < 4 else TS
                act.wait_ge(round_done, DONE[f"ht{b}"])
                act.activation(h_tok[b][:].rearrange("p (h t) -> p h t", h=2), work[TILE[f"ht{b}"]][0:n], ACT.Copy).then_inc(h_tok_ready, 1)

            def tokens_in(ps, m, t):
                act.wait_ge(ps.turned, t + 2)
                act.activation(hs_hi[:, m % 2].rearrange("p (h k) t -> p h (k t)", h=2), work[0][:, :, 0:KB // 2 * C], ACT.Copy).then_inc(ps.hs_hi_ready, 1)

            def u_in(ps, t):
                act.wait_ge(ps.u_turned, t + 1)
                act.activation(u_hi[:].rearrange("p f t -> p (f t)"), pr[1][:, 0, 0:FB * C], ACT.Copy).then_inc(ps.u_hi_ready, 1)

            def rows_out(ps, t):
                act.wait_ge(ps.done["down"], t * CH + CH)
                act.wait_ge(ps.stored, t * 16 + 16)
                act.activation(y_out[:].rearrange("p (h n) -> p h n", h=2), work[1][0:C], ACT.Copy).then_inc(ps.y_ready, 1)

            def expert_pass(ps, n0, uses):
                def step(e, m, third):
                    t, s, last_s = e + n0, m % 3, (m - 1) % 3
                    third_before = third - 1 if m % 3 == 0 else third
                    if m or ps is further:
                        rounded_parts(ps, "gate", s, third + uses[s], t, before=("up", t - 1) if m else None)
                    if m == 0:
                        tokens_in(ps, 0, t)
                        rounded_parts(ps, "up", s, uses[s], t, before=("gate", t))
                    else:
                        use = third_before + uses[last_s]
                        rounded_parts(ps, "down", last_s, use, t - 1, before=("gate", t), chunks=range(CH - 1))
                        u_in(ps, t - 1)
                        rounded_parts(ps, "down", last_s, use, t - 1, before=("gate", t), chunks=(CH - 1,))
                    if m < 15:
                        tokens_in(ps, m + 1, t + 1)
                    act.wait_ge(ps.done["gate"], t * CH + CH)
                    act.wait_ge(ps.u_ready, t + 1)
                    act.activation(silu[:], pr[0][0:C, 0, :], ACT.Silu).then_inc(ps.silu_ready, 1)
                    if m:
                        rounded_parts(ps, "up", s, third + uses[s], t, before=("down", t - 1))
                        rows_out(ps, t - 1)

                each_tile(act, step)
                rounded_parts(ps, "down", 0, uses[0] + 5, n0 + (E - 1), before=("up", n0 + (E - 1)))
                u_in(ps, n0 + (E - 1))
                rows_out(ps, n0 + (E - 1))

            act.sem_inc(first.silu_ready, 1)
            act.sem_inc(first.y_ready, 1)
            expert_pass(first, 0, (0, 0, 0))
            n_max = further_passes(act)
            with act.If(n_max > C):
                act.sem_inc(further.silu_ready, 1)
                act.sem_inc(further.y_ready, 1)
                with act.Fori(0, PASSES - 1) as q:
                    expert_pass(further, q * E, (q * 6, q * 5, q * 5))
                act.nop()
            with act.Else():
                act.nop()
            for b in range(NTB):
                n = P if b < 4 else TS
                s = b % 2
                act.wait_ge(var_ready, b + 1)
                act.activation(agg[0:n, s, 2:3], agg[0:n, s, 1:2], ACT.Sqrt, bias=eps_t[0:n, 1:2]).then_inc(std2_ready, 1)
                act.wait_ge(scale_ready, b + 1)
                act.activation(fin[0:n, b, :], y_a[0:n, b, :], ACT.Identity, scale=agg[0:n, s, 2:3],
                               bias=agg[0:n, s, 3:4]).then_inc(normed, 1)

        @block.tensor
        def _(pe):
            pe.sem_inc(proj_done, 2)
            pe.wait_ge(const_ready, 1)
            pe.wait_ge(x_in, 32)
            for j in range(KB):
                if j >= 4:
                    pe.wait_ge(x_split, j - 3)
                for b in range(4):
                    mm = pe.transpose(pr[j // 2 % 2][:, j % 2, b * P:(b + 1) * P], x_tok[:, b, j * P:(j + 1) * P], ident[:])
                mm.then_inc(x_turned, 1)
            pe.wait_ge(rows_in, 160)
            for k in range(KB):
                mm = pe.transpose(work[1][:, 0, k * NROWS:(k + 1) * NROWS], rows[:, k * P:(k + 1) * P], ident[0:NROWS, 0:NROWS])
            mm.then_inc(round_done, 1)
            for k in range(KB):
                mm = pe.transpose(work[0][:, 0, k * TS:(k + 1) * TS], xs_tok[:, k * P:(k + 1) * P], ident[0:TS, 0:TS])
            mm.then_inc(round_done, 1)
            pe.wait_ge(states_in, 16)
            for i in range(2):
                work_wait(pe, f"sb{i}")
                for k in range(4 * i, 4 * i + 4):
                    for b in range(2):
                        q = (k - 4 * i)
                        mm = pe.transpose(work[TILE[f"sb{i}"]][:, q // 2, q % 2 * 240 + b * 120:q % 2 * 240 + b * 120 + 120],
                                          sb_tok[:, b, k * P:(k + 1) * P], ident[0:120, 0:120])
                mm.then_inc(round_done, 1)
            pe.wait_ge(spatial_masked, 1)
            for i in range(2):
                work_wait(pe, f"ws{i}")
                for g in range(4):
                    mm = pe.transpose(work[TILE[f"ws{i}"]][:, 0, g * P:(g + 1) * P], ws_nat[:, 4 * i + g, :], ident[:])
                mm.then_inc(round_done, 1)
            pe.wait_ge(x_split, KB + 1)

            def project(slot, n, hi, lo):
                pe.wait_ge(evacuated, n + 1)
                for k in range(KB):
                    if k % (KB // 2) == 0:
                        pe.wait_ge(w_split, n * 2 + (5 + k // (KB // 2)))
                    for w, x in ((w_hi, hi), (w_hi, lo), (w_lo, hi)):
                        for h in range(2):
                            mm = pe.matmul(pr[slot][:, h, 0:HALF], w[:, slot, k, :], x[:, k, h * HALF:(h + 1) * HALF],
                                           start=(k == 0 and w is w_hi and x is hi), stop=(k == KB - 1 and w is w_lo))
                mm.then_inc(proj_done, 1)

            def mean(name, z):
                work_wait(pe, name)
                for h in range(2):
                    mm = pe.matmul(work[TILE[name]][:, h, 0:HALF], mean_w[:], z[:, h * HALF:(h + 1) * HALF], start=True, stop=True)
                mm.then_inc(round_done, 1)

            with pe.Fori(0, KB) as j:
                for r in range(6):
                    project(r % 2, j * 6 + r, x_hi, x_lo)

            def pairs(n0, count, hi, lo, ready):
                with pe.Fori(0, count) as o:
                    project(0, o * 2 + n0, x_hi, x_lo)
                    pe.wait_ge(ready, KB)
                    project(1, o * 2 + (n0 + 1), hi, lo)

            def singles(n0, hi, lo):
                with pe.Fori(0, KB // 2) as i:
                    for s in range(2):
                        project(s, i * 2 + (n0 + s), hi, lo)

            pairs(N_GA, 3, p_hi, p_lo, a_split)
            pe.wait_ge(const_ready, 2)
            pe.wait_ge(summed, 1)
            mean("meanV", sums)
            pairs(N_GA + 6, 2, p_hi, p_lo, a_split)
            pe.wait_ge(summed, 2)
            mean("varV", sums)
            pe.wait_ge(summed, 3)
            mean("meanB", sums_b)
            pairs(N_GA + 10, 3, p_hi, p_lo, a_split)
            pe.wait_ge(summed, 4)
            mean("varB", sums)
            pe.wait_ge(v_ready, KB)
            for c in range(4):
                work_wait(pe, f"vt{c}")
                for g in range(KB):
                    mm = pe.transpose(work[TILE[f"vt{c}"]][:, g // 4, g % 4 * P:(g % 4 + 1) * P], v[:, g, c * P:(c + 1) * P], ident[:])
                mm.then_inc(round_done, 1)
            for name, src in (("tailB", tail_b[:]), ("tailA", tail_a[:]), ("tailV", v[:, :, TP:T])):
                work_wait(pe, name)
                k = src.shape[2]
                for g in range(KB):
                    mm = pe.transpose(work[TILE[name]][0:k, g // 4, g % 4 * P:(g % 4 + 1) * P], src[:, g, :], ident[:])
                mm.then_inc(round_done, 1)
            pe.wait_ge(vt_ready, 4)
            for q in range(4):
                work_wait(pe, f"sp{q}")
                for i in range(2):
                    g = 2 * q + i
                    for c in range(4):
                        mm = pe.matmul(work[TILE[f"sp{q}"]][:, i, c * P:(c + 1) * P], vt[:, c, g * P:(g + 1) * P], ws_t[:, g, :],
                                       start=True, stop=True)
                mm.then_inc(round_done, 1)
            singles(N_U, x_hi, x_lo)
            pairs(N_GC, KB, q_hi, q_lo, c_split)
            pairs(N_GB, KB, p_hi, p_lo, b_split)
            pe.wait_ge(merged_split, KB)
            singles(N_WO, q_hi, q_lo)
            pe.wait_ge(summed, 5)
            mean("meanH", sums)
            work_wait(pe, "varH")
            for k in range(KB):
                pe.wait_ge(sq_h_ready, k + 1)
                for h in range(2):
                    mm = pe.matmul(work[TILE["varH"]][:, h, 0:HALF], mean_w[:], sq_h[:, k, h * HALF:(h + 1) * HALF],
                                   start=(k == 0), stop=(k == KB - 1))
            mm.then_inc(round_done, 1)
            pe.wait_ge(late_in, 32)
            work_wait(pe, "logits")
            for k in range(KB):
                pe.wait_ge(h_ready, k + 1)
                for h in range(2):
                    mm = pe.matmul(work[TILE["logits"]][0:E, h, 0:HALF], rw[:, k, :], m[:, k, h * HALF:(h + 1) * HALF],
                                   start=(k == 0), stop=(k == KB - 1))
            mm.then_inc(lg_turned, 1)
            pe.wait_ge(lg_ready, 1)
            for b in range(NTB):
                n = P if b < 4 else TS
                mm = pe.transpose(work[TILE["logits"]][0:n, 0, b * E:(b + 1) * E], lg[0:E, b * P:b * P + n], ident[0:E, 0:E])
            mm.then_inc(round_done, 1)
            for b in range(NTB):
                n = P if b < 4 else TS
                work_wait(pe, f"ht{b}")
                for k in range(KB):
                    mm = pe.transpose(work[TILE[f"ht{b}"]][0:n, k // 4, k % 4 * P:(k % 4 + 1) * P], m[:, k, b * P:b * P + n], ident[:])
                mm.then_inc(round_done, 1)
            pe.wait_ge(mb_ready, 1)
            pe.wait_ge(const_ready, 3)
            work_wait(pe, "pos")
            for b in range(NTB):
                mm = pe.matmul(work[0][:, 0, b * E:(b + 1) * E], tri[:], mb[:, b, :], start=True, stop=(b == 0))
                for c in range(b):
                    mm = pe.matmul(work[0][:, 0, b * E:(b + 1) * E], ones_b[:], mb[:, c, :], start=False, stop=(c == b - 1))
            for b in range(NTB):
                mm = pe.matmul(work[0][:, 0, NTB * E:(NTB + 1) * E], ones_b[:], mb[:, b, :], start=(b == 0), stop=(b == NTB - 1))
            mm.then_inc(round_done, 1)

            def find_ids(ps, t):
                pe.wait_ge(ps.onehot_ready, t + 1)
                pe.wait_ge(ps.ids_ready, t + 1)
                for b in range(NTB):
                    mm = pe.matmul(pr[1][0:C, 1, 0:2], onehot[:, b, :], id_cols[:, b, :], start=(b == 0), stop=(b == NTB - 1))
                mm.then_inc(ps.ids_mm, 1)

            def turn(ps, t):
                pe.wait_ge(ps.gathered, t * 16 + 16)
                for k in range(KB):
                    mm = pe.transpose(work[0][:, k // 4, k % 4 * C:(k % 4 + 1) * C], hs[:, k * P:(k + 1) * P], ident[0:C, 0:C])
                mm.then_inc(ps.turned, 1)

            def product(ps, kind, s, t, hi, lo, out, halves):
                k_of = CW // (halves * 512)
                for i in range(CH):
                    by_pool = i in BY_POOL[kind]
                    mine = BY_POOL[kind] if by_pool else [j for j in range(CH) if j not in BY_POOL[kind]]
                    pe.wait_ge((ps.lo_pool if by_pool else ps.lo_dve)[kind], t * len(mine) + (list(mine).index(i) + 1))
                    w_lo_i, w_hi_i = chunk(kind, s, i, w_e_lo), ring[:, i]
                    for kk in range(k_of):
                        k = i * k_of + kk
                        for h in range(halves):
                            cols = slice(kk * 512 * halves + h * 512, kk * 512 * halves + (h + 1) * 512)
                            for x, w in ((hi, w_hi_i), (hi, w_lo_i), (lo, w_hi_i)):
                                mm = pe.matmul(out(h), x[:, k, :], w[:, cols], start=(k == 0 and x is hi and w is w_hi_i),
                                               stop=(k == k_of * CH - 1 and x is lo))
                    mm.then_inc(ps.done[kind], 1)

            def down(ps, s, t):
                pe.wait_ge(ps.u_lo_ready, t + 1)
                pe.wait_ge(ps.y_ready, t + 1)
                product(ps, "down", s, t, u_hi, u_lo, lambda h: work[1][0:C, h, :], 2)

            def turn_u(ps, t):
                pe.wait_ge(ps.u_ready, t + 2)
                for f in range(FB):
                    mm = pe.transpose(pr[1][:, 0, f * C:(f + 1) * C], u[:, f * P:(f + 1) * P], ident[0:C, 0:C])
                mm.then_inc(ps.u_turned, 1)

            def expert_pass(ps, n0):
                find_ids(ps, n0)
                find_ids(ps, n0 + 1)
                turn(ps, n0)

                def step(e, m, third):
                    t, s = e + n0, m % 3
                    x_hi_t, x_lo_t = hs_hi[:, m % 2], hs_lo[:, m % 2]
                    pe.wait_ge(ps.hs_lo_ready, t + 1)
                    pe.wait_ge(ps.silu_ready, t + 1)
                    product(ps, "gate", s, t, x_hi_t, x_lo_t, lambda h: pr[0][0:C, 0, :], 1)
                    if m <= 13:
                        find_ids(ps, t + 2)
                    if m:
                        turn_u(ps, t - 1)
                    if m < 15:
                        turn(ps, t + 1)
                    if m:
                        down(ps, (m - 1) % 3, t - 1)
                    product(ps, "up", s, t, x_hi_t, x_lo_t, lambda h: pr[0][0:C, 1, :], 1)

                each_tile(pe, step)
                turn_u(ps, n0 + (E - 1))
                down(ps, 0, n0 + (E - 1))

            pe.sem_inc(first.turned, 1)
            pe.wait_ge(h_tok_ready, NTB)
            expert_pass(first, 0)
            n_max = further_passes(pe)
            with pe.If(n_max > C):
                pe.sem_inc(further.turned, 1)
                pe.wait_ge(first.y_ready, E + 1)
                with pe.Fori(0, PASSES - 1) as q:
                    expert_pass(further, q * E)
                    pe.wait_ge(further.y_ready, q * E + (E + 1))
                    pe.nop()
                pe.nop()
            with pe.Else():
                pe.nop()

        @block.vector
        def _(dve):
            chain = Tally(dve, dve_chain)
            last = [chain]

            def do(ins, tally=chain):
                tally.inc(ins)
                last[0] = tally

            def settle():
                last[0].wait()

            gates = Tally(dve, gated, 3)
            dve.sem_inc(gated, 3)
            tallies = {s: Tally(dve, s) for s in (setup_done, x_split, a_split, b_split, c_split, merged_split, conv_done,
                                                  b_normed, centred, summed, h_centred, h_white, std_used, v_ready, spatial_read)}

            def to(s):
                return tallies[s]

            to_logits, to_mb, to_count, to_slots = (Tally(dve, s) for s in (logits_ready, mb_ready, count_ready, slots_ready))
            to_var, to_scale, to_fin = (Tally(dve, s) for s in (var_ready, scale_ready, fin_ready))

            def col(k, r):
                return par[:, bass.ds(k * NROWS + r, 1)]

            def blk(t, k, a=0, b=T):
                return t[:, bass.ds(k, 1), a:b].rearrange("p o t -> p (o t)")

            do(dve.memset(b_pad[:, 0:KC - 1], 0.0))
            do(dve.memset(a_pad[:, 0:KA - 1], 0.0))
            do(dve.memset(mb[:], 0.0))
            for j in range(KB):
                dve.wait_ge(x_rounded, j + 1)
                do(dve.tensor_tensor(x_lo[:, j, 0:TP], pr[j // 2 % 2][:, j % 2, :], x_hi[:, j, 0:TP].bitcast(F32), ALU.subtract), to(x_split))
            dve.wait_ge(x_rounded, KB + 1)
            do(dve.tensor_tensor(x_lo[:, :, TP:T], work[0][:, 0, 0:KB * TS].rearrange("p (k s) -> p k s", s=TS),
                                 x_hi[:, :, TP:T].bitcast(F32), ALU.subtract), to(x_split))
            dve.wait_ge(round_done, DONE["rows"])
            do(dve.tensor_copy(par[:], work[1][:, 0, 0:KB * NROWS]), to(setup_done))
            for i in range(2):
                dve.wait_ge(round_done, DONE[f"sb{i}"])
                for q in range(2):
                    do(dve.tensor_copy(sb_t[:, 4 * i + 2 * q:4 * i + 2 * q + 2].rearrange("p k s c -> p (k s c)"),
                                       work[TILE[f"sb{i}"]][:, q, 0:480]), chain if q == 0 else to(setup_done))
            for i in range(2):
                dve.wait_ge(round_done, DONE[f"ws{i}"])
                do(dve.tensor_copy(ws_t[:, 4 * i:4 * i + 4].rearrange("p g t -> p (g t)"), work[TILE[f"ws{i}"]][:, 0, :]), to(setup_done))
            settle()
            par_k = par[:].rearrange("p (k r) -> p k r", r=NROWS)
            state_a = par_k[:, :, R_STA:R_STA + 2 * TS].rearrange("p k (s c) -> p k s c", c=2)
            do(dve.tensor_tensor(sb_t[:], sb_t[:], rep(par_k[:, :, R_CONVB:R_CONVB + KC - 1], 2, TS), ALU.mult))
            do(dve.tensor_tensor(samp_a[:], state_a[:, :, :, 0], par_k[:, :, R_CONVA:R_CONVA + 1].to_broadcast([P, KB, TS]), ALU.mult))
            do(dve.tensor_tensor(samp_t[:], state_a[:, :, :, 1], par_k[:, :, R_CONVA + 1:R_CONVA + 2].to_broadcast([P, KB, TS]), ALU.mult))
            settle()
            do(dve.tensor_tensor(samp_a[:], samp_a[:], samp_t[:], ALU.add))
            do(dve.tensor_reduce(samp_b[:], sb_t[:], AX.X, ALU.add))
            settle()
            do(dve.tensor_tensor(samp_b[:], samp_b[:], par_k[:, :, R_BIAS:R_BIAS + 1].to_broadcast([P, KB, TS]), ALU.add))

            def branches(j):
                dve.wait_ge(evacuated, j * 6 + (1 + 3))
                settle()
                do(dve.tensor_tensor(b_pad[:, KC - 1:KC - 1 + T], ev[0][:], ev[1][:], ALU.mult), gates)
                dve.wait_ge(evacuated, j * 6 + (4 + 3))
                do(dve.tensor_tensor(a_pad[:, KA - 1:KA - 1 + T], ev[2][:], ev[3][:], ALU.mult), gates)
                gates.wait(1)
                do(dve.tensor_copy(blk(tail_b, j, 0, 38), b_pad[:, TP:TP + 38]))
                gates.wait()
                do(dve.tensor_copy(blk(tail_a, j, 0, 10), a_pad[:, TP:TP + 10]))
                do(dve.tensor_scalar(acc_a[:, 0:TP], a_pad[:, 0:TP], col(j, R_CONVA), None, ALU.mult))
                do(dve.scalar_tensor_tensor(acc_a[:, TP:T], a_pad[:, KA - 1 + TP:], col(j, R_CONVA + 2), blk(samp_a, j, 0, TS), ALU.mult, ALU.add))
                for k in (1, 2):
                    settle()
                    do(dve.scalar_tensor_tensor(acc_a[:, 0:TP], a_pad[:, k:k + TP], col(j, R_CONVA + k), acc_a[:, 0:TP], ALU.mult, ALU.add))
                dve.wait_ge(evacuated, j * 6 + (5 + 3))
                settle()
                do(dve.tensor_tensor(acc_a[:], acc_a[:], ev[4][:], ALU.mult), gates)
                settle()
                do(dve.tensor_copy(blk(p_hi, j), acc_a[:]))
                do(dve.tensor_scalar(blk(cb, j, 0, TP), b_pad[:, 0:TP], col(j, R_CONVB), col(j, R_BIAS), ALU.mult, ALU.add))
                chain.wait(1)
                do(dve.tensor_tensor(blk(p_lo, j), acc_a[:], blk(p_hi, j).bitcast(F32), ALU.subtract), to(a_split))
                do(dve.tensor_scalar(acc_b[:, 0:TP], b_pad[:, 1:1 + TP], col(j, R_CONVB + 1), None, ALU.mult))
                for k in range(2, KC):
                    acc = acc_b[:, 0:TP] if k % 2 else blk(cb, j, 0, TP)
                    chain.wait(1)
                    do(dve.scalar_tensor_tensor(acc, b_pad[:, k:k + TP], col(j, R_CONVB + k), acc, ALU.mult, ALU.add))
                settle()
                do(dve.tensor_tensor(blk(cb, j, 0, TP), blk(cb, j, 0, TP), acc_b[:, 0:TP], ALU.add))
                do(dve.scalar_tensor_tensor(blk(cb, j, TP, T), b_pad[:, KC - 1 + TP:], col(j, R_CONVB + KC - 1), blk(samp_b, j, 0, TS),
                                            ALU.mult, ALU.add), to(conv_done))

                settle()

            settle()
            looped = ((chain, 39), (gates, 3), (to(a_split), 1), (to(conv_done), 1))
            with dve.Fori(0, KB) as j:
                for t, n in looped:
                    t.enter(j, n)
                branches(j)
                for t, _ in looped:
                    t.leave(KB)

            def centre(name, z):
                dve.wait_ge(round_done, DONE[name])
                for h in range(2):
                    part = z[:, :, h * HALF:(h + 1) * HALF]
                    do(dve.tensor_tensor(part, part, rep(work[TILE[name]][:, h, 0:HALF], 1, KB), ALU.subtract),
                       to(centred) if h else chain)

            def squares(z, out):
                settle()
                do(dve.tensor_tensor(out[:], z[:], z[:], ALU.mult))

            def sum_blocks(z, out):
                settle()
                do(dve.tensor_reduce(out[:], z[:].rearrange("p k t -> p t k"), AX.X, ALU.add), to(summed))

            def whiten(z, k):
                dve.wait_ge(std_ready, k)
                settle()
                do(dve.reciprocal(std[:], std[:]))
                settle()
                do(dve.tensor_tensor(z[:], z[:], rep(std[:], 1, KB), ALU.mult), to(std_used))
                settle()

            def affine(z, k, g, b, tally):
                do(dve.tensor_scalar(z[:, k, :], z[:, k, :], col(k, g), col(k, b), ALU.mult, ALU.add), tally)

            def merge(n0, o, b, how):
                dve.wait_ge(evacuated, o * 2 + (n0 + 1 + 3))
                gate, prod = ev[2 * b], ev[2 * b + 1]
                if how == "first":
                    do(dve.tensor_tensor(blk(m, o), gate[:], prod[:], ALU.mult), gates)
                    return
                do(dve.tensor_tensor(gate[:], gate[:], prod[:], ALU.mult))
                settle()
                do(dve.tensor_tensor(blk(m, o), blk(m, o), gate[:], ALU.add), gates)
                if how == "last":
                    settle()
                    split(blk(m, o), blk(q_hi, o), blk(q_lo, o), to(merged_split))
                    settle()
                    do(dve.tensor_scalar(blk(m, o), blk(x_hi, o).bitcast(F32), ALPHA, None, ALU.mult))
                    settle()
                    do(dve.scalar_tensor_tensor(blk(m, o), blk(x_lo, o).bitcast(F32), ALPHA, blk(m, o), ALU.mult, ALU.add))

            def split(z, hi, lo, tally):
                do(dve.tensor_copy(hi, z))
                settle()
                do(dve.tensor_tensor(lo, z, hi.bitcast(F32), ALU.subtract), tally)

            merge(N_GA, 0, 0, "first")
            sum_blocks(v, sums)
            merge(N_GA, 1, 1, "first")
            merge(N_GA, 2, 0, "first")
            centre("meanV", v)
            squares(v, sq)
            merge(N_GA, 3, 1, "first")
            sum_blocks(sq, sums)
            sum_blocks(cb, sums_b)
            merge(N_GA, 4, 0, "first")
            centre("meanB", cb)
            squares(cb, sq)
            merge(N_GA, 5, 1, "first")
            dve.wait_ge(std_ready, 1)
            sum_blocks(sq, sums)
            whiten(v, 1)
            for k in range(KB):
                affine(v, k, R_VG, R_VB, to(v_ready))
            merge(N_GA, 6, 0, "first")
            merge(N_GA, 7, 1, "first")
            whiten(cb, 2)
            for q in range(4):
                dve.wait_ge(round_done, DONE[f"sp{q}"])
                do(dve.tensor_tensor(v[:, 2 * q:2 * q + 2, 0:TP].rearrange("p g (c t) -> p g c t", c=4),
                                     work[TILE[f"sp{q}"]][:].rearrange("p g (c t) -> p g c t", c=4),
                                     rep(bs[:, 2 * q:2 * q + 2, :], 2, 4), ALU.add), to(spatial_read))
            do(dve.tensor_tensor(v[:, :, TP:T], v[:, :, TP:T], rep(w00[:], 2, TS), ALU.mult))
            settle()
            do(dve.tensor_tensor(v[:, :, TP:T], v[:, :, TP:T], bs[:, :, 0:1].to_broadcast([P, KB, TS]), ALU.add))
            dve.wait_ge(tails_out, 80)
            for i in range(KB):
                dve.wait_ge(evacuated, N_U + i + 3)
                settle()
                do(dve.tensor_tensor(v[:, i, :], v[:, i, :], ev[2 * (i % 2)][:], ALU.mult), gates)
                affine(cb, i, R_NBG, R_NBB, to(b_normed))
                gates.wait()
                split(v[:, i, :], q_hi[:, i, :], q_lo[:, i, :], to(c_split))
            settle()
            looped = ((chain, 6), (gates, 2), (to(b_split), 2))
            with dve.Fori(0, KB // 2) as i:
                for t, n in looped:
                    t.enter(i, n)
                for b in range(2):
                    o = i * 2 + b
                    merge(N_GC, o, b, "add")
                    dve.wait_ge(b_sig, o + 1)
                    do(dve.tensor_tensor(blk(cb, o), blk(cb, o), blk(sig_b, o), ALU.mult))
                    settle()
                    split(blk(cb, o), blk(p_hi, o), blk(p_lo, o), to(b_split))
                    settle()
                for t, _ in looped:
                    t.leave(KB // 2)
            looped = ((chain, 8), (gates, 2), (to(merged_split), 2))
            with dve.Fori(0, KB // 2) as i:
                for t, n in looped:
                    t.enter(i, n)
                for b in range(2):
                    merge(N_GB, i * 2 + b, b, "last")
                    settle()
                for t, _ in looped:
                    t.leave(KB // 2)
            for i in range(KB):
                dve.wait_ge(evacuated, N_WO + i + 3)
                do(dve.tensor_tensor(m[:, i, :], m[:, i, :], ev[2 * (i % 2)][:], ALU.add), gates)
                if i:
                    settle()
                    do(dve.tensor_tensor(sums[:], m[:, 0, :] if i == 1 else sums[:], m[:, i, :], ALU.add), chain if i < KB - 1 else to(summed))
            dve.wait_ge(round_done, DONE["meanH"])
            for k in range(KB):
                mk = m[:, k, :].rearrange("p (h t) -> p h t", h=2)
                do(dve.tensor_tensor(mk, mk, work[TILE["meanH"]][:, :, 0:HALF], ALU.subtract), to(h_centred))
            dve.wait_ge(std_ready, 3)
            do(dve.reciprocal(std[:], std[:]))
            settle()
            for k in range(KB):
                do(dve.tensor_tensor(m[:, k, :], m[:, k, :], std[:], ALU.mult), to(h_white))

            grp = lambda t: t[:].rearrange("p b (g i) -> p (b g) i", i=PER_GROUP)
            flat = lambda t: t[:].rearrange("p b g -> p (b g)")
            over4 = lambda t: rep(flat(t), 2, PER_GROUP)
            over_e = lambda t: rep(t[:], 2, E)

            def step(ins, tally=chain):
                do(ins, tally)
                settle()

            step(dve.memset(probs[:], 0.0))
            dve.wait_ge(late_in, 32)
            dve.wait_ge(round_done, DONE["logits"])
            do(dve.tensor_tensor(probs[:, 0:4, :], work[0][:, 0, 0:4 * E].rearrange("p (b e) -> p b e", e=E), rep(rb[:], 1, 4), ALU.add))
            step(dve.tensor_tensor(probs[0:TS, 4, :], work[0][0:TS, 0, 4 * E:5 * E], rb[0:TS, :], ALU.add))
            step(dve.tensor_reduce(s_max[:], probs[:], AX.X, ALU.max))
            step(dve.tensor_tensor(probs[:], probs[:], over_e(s_max), ALU.subtract), to_logits)
            dve.wait_ge(exp_ready, 1)
            step(dve.tensor_reduce(s_sum[:], probs[:], AX.X, ALU.add))
            step(dve.reciprocal(s_sum[:], s_sum[:]))
            step(dve.tensor_tensor(probs[:], probs[:], over_e(s_sum), ALU.mult))

            def first_of(values, top, is_first, best, n):
                step(dve.tensor_reduce(top, values, AX.X, ALU.max))
                step(dve.tensor_tensor(is_first, values, rep(top, 2, n), ALU.is_equal))
                step(dve.tensor_tensor(is_first, is_first, grp(c4)[:, 0:is_first.shape[1], :], ALU.mult))
                step(dve.tensor_reduce(best, is_first, AX.X, ALU.max))
                step(dve.tensor_tensor(is_first, is_first, rep(best, 2, n), ALU.is_equal))

            dve.wait_ge(const_ready, 3)
            first_of(grp(probs), flat(g_m1), grp(oh1), flat(g_t), PER_GROUP)
            step(dve.scalar_tensor_tensor(probs[:], oh1[:], -2.0, probs[:], ALU.mult, ALU.add))
            first_of(grp(probs), flat(g_m2), grp(oh2), flat(g_t), PER_GROUP)
            step(dve.tensor_tensor(g_t[:], g_m1[:], g_m2[:], ALU.add))
            first_of(g_t[:], s_max[:], g_best[:], s_t[:], GROUPS)
            for t in (oh1, oh2):
                do(dve.tensor_tensor(grp(t), grp(t), over4(g_best), ALU.mult))
            settle()
            do(dve.tensor_tensor(mb[:, 0:4, :], oh1[:, 0:4, :], oh2[:, 0:4, :], ALU.add))
            do(dve.tensor_tensor(mb[0:TS, 4, :], oh1[0:TS, 4, :], oh2[0:TS, 4, :], ALU.add), to_mb)
            do(dve.tensor_tensor(g_m1[:], g_m1[:], g_best[:], ALU.mult))
            step(dve.tensor_tensor(g_m2[:], g_m2[:], g_best[:], ALU.mult))
            do(dve.tensor_reduce(s_w1[:], g_m1[:], AX.X, ALU.add))
            step(dve.tensor_reduce(s_w2[:], g_m2[:], AX.X, ALU.add))
            step(dve.tensor_tensor(s_sum[:], s_w1[:], s_w2[:], ALU.add))
            step(dve.reciprocal(s_sum[:], s_sum[:]))
            step(dve.tensor_scalar(s_sum[:], s_sum[:], 1.0 / ALPHA, None, ALU.mult))
            do(dve.tensor_tensor(s_w1[:], s_w1[:], s_sum[:], ALU.mult))
            step(dve.tensor_tensor(s_w2[:], s_w2[:], s_sum[:], ALU.mult))
            pos = t1
            dve.wait_ge(round_done, DONE["pos"])
            do(dve.tensor_copy(pos[:], work[0][:, 0, 0:NTB * E].rearrange("p (b e) -> p b e", e=E)))
            step(dve.tensor_reduce(s_ps[:, 0:1], work[0][:, 0, NTB * E:(NTB + 1) * E], AX.X, ALU.max))
            do(dve.tensor_copy(count_i[:], s_ps[:, 0:1]), to_count)
            step(dve.tensor_tensor(posm[:], pos[:], mb[:], ALU.mult))
            step(dve.scalar_tensor_tensor(posm[:], mb[:], -1.0, posm[:], ALU.add, ALU.add))

            def mark(ps, e):
                dve.tensor_tensor(onehot[:], rep(iota, 1, NTB), posm[:, :, bass.ds(e, 1)].to_broadcast([P, NTB, C]),
                                  ALU.is_equal).then_inc(ps.onehot_ready, 1)

            def take_ids(ps, m, t):
                dve.wait_ge(ps.ids_mm, t + 1)
                with nc.allow_low_precision(reason="whole numbers"):
                    dve.tensor_reduce(ids[:, m % 2:m % 2 + 1], pr[1][0:C, 1, 0:2], AX.X, ALU.add).then_inc(ps.ids_ready, 1)

            def low_parts(ps, kind, s, t, chunks=range(CH)):
                for i in chunks:
                    if i not in BY_POOL[kind]:
                        dve.wait_ge(ps.hi[kind], t * CH + (i + 1))
                        dve.tensor_tensor(chunk(kind, s, i, w_e_lo), chunk(kind, s, i), ring[:, i].bitcast(F32), ALU.subtract).then_inc(ps.lo_dve[kind], 1)

            def tokens_low(ps, m, t):
                dve.wait_ge(ps.hs_hi_ready, t + 1)
                part = lambda x: x[:, m % 2].rearrange("p (h k) t -> p h (k t)", h=2)
                dve.tensor_tensor(part(hs_lo), work[0][:, :, 0:KB // 2 * C], part(hs_hi).bitcast(F32), ALU.subtract).then_inc(ps.hs_lo_ready, 1)

            def gated_product(ps, t):
                dve.wait_ge(ps.silu_ready, t + 2)
                dve.wait_ge(ps.done["up"], t * CH + CH)
                dve.tensor_tensor(u[:], silu[:], pr[0][0:C, 1, :], ALU.mult).then_inc(ps.u_ready, 1)

            def u_low(ps, t):
                dve.wait_ge(ps.u_hi_ready, t + 1)
                dve.tensor_tensor(u_lo[:].rearrange("p f t -> p (f t)"), pr[1][:, 0, 0:FB * C],
                                  u_hi[:].rearrange("p f t -> p (f t)").bitcast(F32), ALU.subtract).then_inc(ps.u_lo_ready, 1)

            def expert_pass(ps, n0):
                mark(ps, 0)
                take_ids(ps, 0, n0)
                mark(ps, 1)
                take_ids(ps, 1, n0 + 1)

                def step(e, m, third):
                    t = e + n0
                    low_parts(ps, "gate", m % 3, t)
                    if m:
                        gated_product(ps, t - 1)
                    if m <= 13:
                        mark(ps, e + 2)
                    if m:
                        low_parts(ps, "down", (m - 1) % 3, t - 1, range(CH - 1))
                        u_low(ps, t - 1)
                        low_parts(ps, "down", (m - 1) % 3, t - 1, (CH - 1,))
                    else:
                        tokens_low(ps, 0, t)
                        low_parts(ps, "up", 0, t)
                    if m <= 13:
                        take_ids(ps, m, t + 2)
                    if m < 15:
                        tokens_low(ps, m + 1, t + 1)
                    if m:
                        low_parts(ps, "up", m % 3, t)

                each_tile(dve, step)
                gated_product(ps, n0 + (E - 1))
                low_parts(ps, "down", 0, n0 + (E - 1))
                u_low(ps, n0 + (E - 1))

            dve.sem_inc(first.ids_ready, 1)
            dve.sem_inc(first.u_ready, 1)
            dve.wait_ge(const_ready, 4)
            expert_pass(first, 0)
            for oh, out in ((oh1, slot_a), (oh2, slot_b)):
                do(dve.tensor_tensor(t2[:], oh[:], e_off[:], ALU.mult))
                do(dve.tensor_tensor(probs[:], oh[:], pos[:], ALU.mult))
                settle()
                do(dve.tensor_reduce(s_slot[:], t2[:], AX.X, ALU.add))
                step(dve.tensor_reduce(s_ps[:], probs[:], AX.X, ALU.add))
                step(dve.tensor_tensor(s_slot[:], s_slot[:], s_ps[:], ALU.add))
                for k in range(1, PASSES):
                    step(dve.tensor_scalar(s_t[:], s_ps[:], float(k * C), float(E * C - C), ALU.is_ge, ALU.mult))
                    step(dve.tensor_tensor(s_slot[:], s_slot[:], s_t[:], ALU.add))
                step(dve.tensor_copy(out[:], s_slot[:]), to_slots)
            n_max = further_passes(dve)
            with dve.If(n_max > C):
                dve.sem_inc(further.ids_ready, 1)
                dve.sem_inc(further.u_ready, 1)
                dve.wait_ge(first.y_ready, E + 1)
                with dve.Fori(0, PASSES - 1) as q:
                    dve.tensor_scalar(posm[:], posm[:], -float(C), None, ALU.add).then_inc(more_posm, 1)
                    dve.wait_ge(more_posm, q + 1)
                    expert_pass(further, q * E)
                dve.nop()
            with dve.Else():
                dve.nop()

            dve.wait_ge(back_in, 64)

            def combine(b):
                n, s = P if b < 4 else TS, b % 2
                dve.wait_ge(y_in[b], 32)
                if b >= 2:
                    dve.wait_ge(normed, b - 1)
                a = y_a[0:n, b, :]
                step(dve.scalar_tensor_tensor(a, a, s_w1[0:n, b:b + 1], h_back[0:n, b, :], ALU.mult, ALU.add))
                step(dve.scalar_tensor_tensor(a, y_b[0:n, b, :], s_w2[0:n, b:b + 1], a, ALU.mult, ALU.add))
                for h in range(2):
                    do(dve.bn_stats(stats[0:n, s, h, :], y_a[0:n, b, h * 512:(h + 1) * 512]))
                settle()
                step(dve.bn_aggr(agg[0:n, s, 0:2], stats[0:n, s].rearrange("p h c -> p (h c)")), to_var)
                dve.wait_ge(std2_ready, b + 1)
                step(dve.reciprocal(agg[0:n, s, 2:3], agg[0:n, s, 2:3]))
                do(dve.scalar_tensor_tensor(agg[0:n, s, 3:4], agg[0:n, s, 0:1], -1.0, agg[0:n, s, 2:3], ALU.mult, ALU.mult), to_scale)

            def shift(b):
                n, s = P if b < 4 else TS, b % 2
                dve.wait_ge(fin_g, b + 1)
                do(dve.tensor_tensor(fin[0:n, b, :], fin[0:n, b, :], ln2_rows[0:n, 1, :], ALU.add), to_fin)

            last[0] = chain
            combine(0)
            for b in range(1, NTB):
                combine(b)
                shift(b - 1)
            shift(NTB - 1)


_INS = ['x_prompt', 'x_sample', 'state_conv_a', 'state_conv_b', 'w_in', 'conv_a_w', 'w_a_out', 'conv_b_w', 'conv_b_bias',
        'norm_b_g', 'norm_b_b', 'w_b_out', 'v_norm_g', 'v_norm_b', 'w_spatial', 'b_spatial', 'w_c_out', 'w_o', 'ln1_g', 'ln1_b',
        'router_w', 'router_b', 'expert_w_gate', 'expert_w_up', 'expert_w_down', 'ln2_g', 'ln2_b']
_OUTS = [(1, 512, 1024), (8, 1, 1024), (1, 1, 2, 1024), (1, 1, 30, 1024), (1, 8, 2, 1024), (1, 8, 30, 1024), (1, 8, 1, 1024)]


def kernel(**inputs):
    import numpy as _np
    import concourse.bacc as _bacc
    from concourse import mybir as _mybir
    from concourse.bass_utils import run_bass_kernel_spmd as _run

    nc = _bacc.Bacc("TRN2", target_bir_lowering=False, num_devices=1)
    arrays, args = {}, []
    for name in _INS:
        a = _np.ascontiguousarray(inputs[name])
        arrays[f"in_{name}_dram"] = a
        args.append(nc.dram_tensor(f"in_{name}_dram", a.shape, _mybir.dt.from_np(a.dtype), kind="ExternalInput").ap())
    for i, shape in enumerate(_OUTS):
        args.append(nc.dram_tensor(f"out_{i}_dram", shape, _mybir.dt.float32, kind="ExternalOutput").ap())
    build(nc, *args)
    r = _run(nc, [arrays], core_ids=[0])
    return tuple(r.results[0][f"out_{i}_dram"] for i in range(len(_OUTS)))
```
